# Optimizing a Trainium2 kernel written in Bass

```python
import jax, jax.numpy as jnp
from jax import lax
import numpy as np
import jax
import jax.numpy as jnp

D_MODEL = 1024
BATCH = 1
SEQ = 512
DEPTH = 2

N_META = 16
D_MIX = 1024
FOURIER_HEADS = 4
FOURIER_HEAD_DIM = 64
D_FOURIER = FOURIER_HEADS * FOURIER_HEAD_DIM
POOL_WINDOWS = (2, 4, 8, 16)
N_POOL_GROUPS = 4
POOL_GROUP_DIM = 64
D_POOL = N_POOL_GROUPS * POOL_GROUP_DIM
MLA_HEADS = 4
QK_NOPE_DIM = 128
QK_ROPE_DIM = 64
V_HEAD_DIM = 128
D_ATTN = MLA_HEADS * V_HEAD_DIM
Q_LORA_RANK = 384
KV_LORA_RANK = 256
ROPE_THETA = 10000.0
QUERY_BLOCK = 128
NORM_EPS = 1e-6
IN_SIZES = (D_FOURIER, D_FOURIER, D_POOL, D_POOL, Q_LORA_RANK, KV_LORA_RANK, QK_ROPE_DIM, D_ATTN)
D_IN = 2 * D_FOURIER + 2 * D_POOL + Q_LORA_RANK + KV_LORA_RANK + QK_ROPE_DIM + D_ATTN


def rms_norm(x, w):
    xf = x.astype(jnp.float32)
    y = xf * lax.rsqrt(jnp.mean(xf * xf, axis=-1, keepdims=True) + NORM_EPS)
    return (y * w.astype(jnp.float32)).astype(x.dtype)

def rope_tables(length):
    inv = 1.0 / (ROPE_THETA ** (jnp.arange(0, QK_ROPE_DIM, 2, dtype=jnp.float32) / QK_ROPE_DIM))
    ang = jnp.arange(length, dtype=jnp.float32)[:, None] * inv[None, :]
    return jnp.cos(ang), jnp.sin(ang)

def apply_rope(t, cos, sin):
    tf = t.astype(jnp.float32)
    half = QK_ROPE_DIM // 2
    t1, t2 = tf[..., :half], tf[..., half:]
    out = jnp.concatenate([t1 * cos - t2 * sin, t2 * cos + t1 * sin], axis=-1)
    return out.astype(t.dtype)

def fourier_mix(f_in, fourier_w):
    B, L, _ = f_in.shape
    xf = f_in.reshape(B, L, FOURIER_HEADS, FOURIER_HEAD_DIM).astype(jnp.float32)
    y = jnp.fft.fft2(xf, axes=(1, 3), norm="ortho").real.astype(f_in.dtype)
    y = jnp.einsum('blhc,hcd->blhd', y, fourier_w)
    return y.reshape(B, L, D_FOURIER)

def pool_mix(p_in, pool_w, pool_scale):
    B, L, _ = p_in.shape
    xg = p_in.reshape(B, L, N_POOL_GROUPS, POOL_GROUP_DIM).astype(jnp.float32)
    cs = jnp.concatenate([jnp.zeros((B, 1, N_POOL_GROUPS, POOL_GROUP_DIM), jnp.float32),
                          jnp.cumsum(xg, axis=1)], axis=1)
    idx = jnp.arange(L)
    outs = []
    for g, w in enumerate(POOL_WINDOWS):
        lo = jnp.clip(idx - w // 2, 0, L)
        hi = jnp.clip(idx + w // 2, 0, L)
        s = cs[:, hi, g] - cs[:, lo, g]
        cnt = (hi - lo).astype(jnp.float32)[None, :, None]
        outs.append(s / cnt - xg[:, :, g])
    y = jnp.stack(outs, axis=2).astype(p_in.dtype)
    y = jnp.einsum('blgc,gcd->blgd', y, pool_w).reshape(B, L, D_POOL)
    return y * pool_scale

def mla_mix(c_q, c_kv, k_r, q_norm_w, w_uq, kv_norm_w, w_ukv, cos, sin):
    B, L, _ = c_q.shape
    dq = QK_NOPE_DIM + QK_ROPE_DIM
    q = (rms_norm(c_q, q_norm_w) @ w_uq).reshape(B, L, MLA_HEADS, dq)
    q = jnp.concatenate([q[..., :QK_NOPE_DIM],
                         apply_rope(q[..., QK_NOPE_DIM:], cos[None, :, None], sin[None, :, None])], axis=-1)
    kv = (rms_norm(c_kv, kv_norm_w) @ w_ukv).reshape(B, L, MLA_HEADS, QK_NOPE_DIM + V_HEAD_DIM)
    k_nope, v = kv[..., :QK_NOPE_DIM], kv[..., QK_NOPE_DIM:]
    k_rope = apply_rope(k_r, cos[None], sin[None])
    k = jnp.concatenate([k_nope, jnp.broadcast_to(k_rope[:, :, None, :], (B, L, MLA_HEADS, QK_ROPE_DIM))], axis=-1)
    scale = dq ** -0.5

    def attend(qb):
        s = jnp.einsum('bqhd,bkhd->bhqk', qb, k).astype(jnp.float32) * scale
        p = jax.nn.softmax(s, axis=-1).astype(v.dtype)
        return jnp.einsum('bhqk,bkhd->bqhd', p, v)

    o_meta = attend(q[:, :N_META])
    n_blk = (L - N_META) // QUERY_BLOCK
    qb = jnp.moveaxis(q[:, N_META:].reshape(B, n_blk, QUERY_BLOCK, MLA_HEADS, dq), 1, 0)
    o = lax.map(attend, qb)
    o = jnp.moveaxis(o, 0, 1).reshape(B, L - N_META, MLA_HEADS, V_HEAD_DIM)
    return jnp.concatenate([o_meta, o], axis=1).reshape(B, L, D_ATTN)

def first_inputs(seed: int = 0) -> dict:
    key = jax.random.key(seed)
    ks = jax.random.split(key, 13)
    f32 = jnp.float32
    nrm = lambda k, shape, fan: jax.random.normal(k, shape, f32) * (fan ** -0.5)
    return {
        "x": jax.random.normal(ks[0], (BATCH, SEQ, D_MODEL), f32),
        "meta_tokens": jax.random.normal(ks[1], (N_META, D_MODEL), f32),
        "norm_w": 1.0 + 0.02 * jax.random.normal(ks[2], (DEPTH, D_MODEL), f32),
        "w_in": nrm(ks[3], (DEPTH, D_MODEL, D_IN), D_MODEL),
        "fourier_w": nrm(ks[4], (DEPTH, FOURIER_HEADS, FOURIER_HEAD_DIM, FOURIER_HEAD_DIM), FOURIER_HEAD_DIM),
        "pool_w": nrm(ks[5], (DEPTH, N_POOL_GROUPS, POOL_GROUP_DIM, POOL_GROUP_DIM), POOL_GROUP_DIM),
        "pool_scale": 1.0 + 0.02 * jax.random.normal(ks[6], (DEPTH, D_POOL), f32),
        "q_norm_w": 1.0 + 0.02 * jax.random.normal(ks[7], (DEPTH, Q_LORA_RANK), f32),
        "w_uq": nrm(ks[8], (DEPTH, Q_LORA_RANK, MLA_HEADS * (QK_NOPE_DIM + QK_ROPE_DIM)), Q_LORA_RANK),
        "kv_norm_w": 1.0 + 0.02 * jax.random.normal(ks[9], (DEPTH, KV_LORA_RANK), f32),
        "w_ukv": nrm(ks[10], (DEPTH, KV_LORA_RANK, MLA_HEADS * (QK_NOPE_DIM + V_HEAD_DIM)), KV_LORA_RANK),
        "w_out": nrm(ks[11], (DEPTH, D_MIX, D_MODEL), D_MIX),
        "final_norm_w": 1.0 + 0.02 * jax.random.normal(ks[12], (D_MODEL,), f32),
    }

def first_block(x, meta_tokens, norm_w, w_in, fourier_w, pool_w, pool_scale, q_norm_w, w_uq,
              kv_norm_w, w_ukv, w_out, final_norm_w):
    B = x.shape[0]
    h = jnp.concatenate([jnp.broadcast_to(meta_tokens[None].astype(x.dtype), (B, N_META, D_MODEL)), x], axis=1)
    L = h.shape[1]
    cos, sin = rope_tables(L)
    split_idx = np.cumsum(IN_SIZES)[:-1].tolist()
    for l in range(DEPTH):
        u = rms_norm(h, norm_w[l]) @ w_in[l]
        f_in, f_gate, p_in, p_gate, c_q, c_kv, k_r, a_gate = jnp.split(u, split_idx, axis=-1)
        y_f = fourier_mix(f_in, fourier_w[l])
        y_p = pool_mix(p_in, pool_w[l], pool_scale[l])
        y_a = mla_mix(c_q, c_kv, k_r, q_norm_w[l], w_uq[l], kv_norm_w[l], w_ukv[l], cos, sin)
        mix = jnp.concatenate([y_f * jax.nn.silu(f_gate),
                               y_p * jax.nn.silu(p_gate),
                               y_a * jax.nn.silu(a_gate)], axis=-1)
        h = h + mix @ w_out[l]
    return rms_norm(h, final_norm_w)[:, N_META:]


DEPTH_2 = 1

CHUNK = 64
N_MEM = 256
D_MIX_2 = D_MODEL
D_RNN = D_MIX_2 // 2
D_ATT = D_MIX_2 - D_RNN
N_RNN_BLOCKS = 8
RNN_BLOCK = D_RNN // N_RNN_BLOCKS
CONV_WIDTH = 4
RG_LRU_C = 8.0
N_ATT_HEADS = 8
ATT_HEAD_DIM = D_ATT // N_ATT_HEADS
LEFT_CHUNKS = 8
BAND = (LEFT_CHUNKS + 1) * CHUNK
REL_CLIP = 128
N_XHEADS = 4
XHEAD_DIM = D_MODEL // N_XHEADS
N_GROUPS = 4
EXPERTS_PER_GROUP = 8
N_EXPERTS = N_GROUPS * EXPERTS_PER_GROUP
TOP_K = 2
D_EXPERT = D_MODEL // 2
MOE_BLOCK = 128
D_IN_PROJ = 2 * D_RNN + 3 * D_ATT
EPS = 1e-6
NEG_INF = -1e30


def rms_norm_2(x, w):
    xf = x.astype(jnp.float32)
    y = xf * lax.rsqrt(jnp.mean(xf * xf, axis=-1, keepdims=True) + EPS)
    return (y * w.astype(jnp.float32)).astype(x.dtype)

def _linear_recurrence_combine(left, right):
    a1, b1 = left
    a2, b2 = right
    return a1 * a2, a2 * b1 + b2

def recurrent_group(xr, xg, conv_w, conv_b, w_a, b_a, w_x, b_x, lam):
    b, s, _ = xr.shape
    xc = lax.conv_general_dilated(
        xr, conv_w[:, None, :].astype(xr.dtype), window_strides=(1,),
        padding=[(CONV_WIDTH - 1, 0)], dimension_numbers=('NWC', 'WIO', 'NWC'),
        feature_group_count=D_RNN) + conv_b
    xb = xc.reshape(b, s, N_RNN_BLOCKS, RNN_BLOCK)
    r = jax.nn.sigmoid((jnp.einsum('bsnc,ncd->bsnd', xb, w_a).reshape(b, s, D_RNN) + b_a).astype(jnp.float32))
    i = jax.nn.sigmoid((jnp.einsum('bsnc,ncd->bsnd', xb, w_x).reshape(b, s, D_RNN) + b_x).astype(jnp.float32))
    log_a = -RG_LRU_C * r * jax.nn.softplus(-lam.astype(jnp.float32))
    a = jnp.exp(log_a)
    u = jnp.sqrt(-jnp.expm1(2.0 * log_a)) * (i * xc.astype(jnp.float32))
    _, h = lax.associative_scan(_linear_recurrence_combine, (a, u), axis=1)
    return (jax.nn.gelu(xg.astype(jnp.float32)) * h).astype(xr.dtype)

def rel_bias_band(rel_bias):
    qi = np.arange(CHUNK)[:, None]
    kj = np.arange(BAND)[None, :]
    dist = LEFT_CHUNKS * CHUNK + qi - kj
    idx = np.clip(dist, -REL_CLIP, REL_CLIP) + REL_CLIP
    return rel_bias[:, idx]

def chunk_band_attention(q, k, v, rel_bias):
    b, s, _ = q.shape
    nc = s // CHUNK
    qc = q.reshape(b, nc, CHUNK, N_ATT_HEADS, ATT_HEAD_DIM)
    kc = k.reshape(b, nc, CHUNK, N_ATT_HEADS, ATT_HEAD_DIM)
    vc = v.reshape(b, nc, CHUNK, N_ATT_HEADS, ATT_HEAD_DIM)
    pad = ((0, 0), (LEFT_CHUNKS, 0), (0, 0), (0, 0), (0, 0))
    kp = jnp.pad(kc, pad)
    vp = jnp.pad(vc, pad)
    kb = jnp.concatenate([kp[:, j:j + nc] for j in range(LEFT_CHUNKS + 1)], axis=2)
    vb = jnp.concatenate([vp[:, j:j + nc] for j in range(LEFT_CHUNKS + 1)], axis=2)
    chunk_id = np.arange(nc)[:, None] - LEFT_CHUNKS + np.arange(LEFT_CHUNKS + 1)[None, :]
    valid = np.repeat(chunk_id >= 0, CHUNK, axis=1)
    scores = jnp.einsum('bnqhd,bnkhd->bhnqk', qc, kb, preferred_element_type=jnp.float32)
    scores = scores * (ATT_HEAD_DIM ** -0.5) + rel_bias_band(rel_bias).astype(jnp.float32)[None, :, None]
    scores = jnp.where(valid[None, None, :, None, :], scores, NEG_INF)
    probs = jax.nn.softmax(scores, axis=-1).astype(v.dtype)
    out = jnp.einsum('bhnqk,bnkhd->bnqhd', probs, vb)
    return out.reshape(b, s, D_ATT)

def memory_cross_attention(h, mem_n, wq, wk, wv, wo):
    b, s, _ = h.shape
    m = mem_n.shape[1]
    q = (h @ wq).reshape(b, s, N_XHEADS, XHEAD_DIM)
    k = (mem_n @ wk).reshape(b, m, N_XHEADS, XHEAD_DIM)
    v = (mem_n @ wv).reshape(b, m, N_XHEADS, XHEAD_DIM)
    scores = jnp.einsum('bshd,bmhd->bhsm', q, k, preferred_element_type=jnp.float32) * (XHEAD_DIM ** -0.5)
    probs = jax.nn.softmax(scores, axis=-1).astype(v.dtype)
    out = jnp.einsum('bhsm,bmhd->bshd', probs, v).reshape(b, s, D_MODEL)
    return out @ wo

def routed_experts(ht, expert_idx, combine_w, w_gate, w_up, w_down):
    t, d = ht.shape
    n_slots = t * TOP_K
    flat_e = expert_idx.reshape(-1)
    flat_tok = jnp.repeat(jnp.arange(t, dtype=jnp.int32), TOP_K)
    order = jnp.argsort(flat_e)
    e_sorted = flat_e[order]
    tok_sorted = flat_tok[order]
    w_sorted = combine_w.reshape(-1)[order]
    counts = jnp.bincount(flat_e, length=N_EXPERTS)
    padded = (counts + MOE_BLOCK - 1) // MOE_BLOCK * MOE_BLOCK
    pad_end = jnp.cumsum(padded)
    pad_start = pad_end - padded
    start = jnp.cumsum(counts) - counts
    dest = pad_start[e_sorted] + (jnp.arange(n_slots) - start[e_sorted])
    n_blocks = (n_slots + MOE_BLOCK - 1) // MOE_BLOCK + N_EXPERTS
    n_rows = n_blocks * MOE_BLOCK
    src_tok = jnp.full((n_rows,), t, dtype=jnp.int32).at[dest].set(tok_sorted)
    x_pad = jnp.concatenate([ht, jnp.zeros((1, d), ht.dtype)], axis=0)
    xs = x_pad[src_tok].reshape(n_blocks, MOE_BLOCK, d)
    block_expert = jnp.minimum(
        jnp.searchsorted(pad_end, jnp.arange(n_blocks) * MOE_BLOCK, side='right'), N_EXPERTS - 1)

    def expert_block(args):
        xb, e = args
        g = xb @ w_gate[e]
        u = xb @ w_up[e]
        return (jax.nn.silu(g) * u) @ w_down[e]

    ys = lax.map(expert_block, (xs, block_expert)).reshape(n_rows, d)
    contrib = (ys[dest].astype(jnp.float32) * w_sorted[:, None]).astype(ht.dtype)
    return jnp.zeros((t, d), ht.dtype).at[tok_sorted].add(contrib)

def hierarchical_moe(h, w_group, b_group, w_router, b_router, w_gate, w_up, w_down):
    b, s, d = h.shape
    t = b * s
    ht = h.reshape(t, d)
    g_logits = (ht @ w_group).astype(jnp.float32) + b_group.astype(jnp.float32)
    g_probs = jax.nn.softmax(g_logits, axis=-1)
    g_p, g_idx = lax.top_k(g_probs, 1)
    e_all = jnp.einsum('td,gde->tge', ht, w_router).astype(jnp.float32) + b_router.astype(jnp.float32)
    sel = jnp.broadcast_to(g_idx[:, :, None], (t, 1, EXPERTS_PER_GROUP))
    e_logits = jnp.take_along_axis(e_all, sel, axis=1)[:, 0]
    e_probs = jax.nn.softmax(e_logits, axis=-1)
    e_p, e_idx = lax.top_k(e_probs, TOP_K)
    e_p = e_p / jnp.sum(e_p, axis=-1, keepdims=True)
    combine_w = g_p * e_p
    expert_idx = g_idx * EXPERTS_PER_GROUP + e_idx
    y = routed_experts(ht, expert_idx, combine_w, w_gate, w_up, w_down)
    return y.reshape(b, s, d)

def second_inputs(seed: int = 0) -> dict:
    key = jax.random.key(seed)
    ks = jax.random.split(key, 32)
    f32 = jnp.float32

    def nrm(k, shape, scale):
        return jax.random.normal(k, shape, f32) * scale

    def gain(k, shape):
        return 1.0 + 0.02 * jax.random.normal(k, shape, f32)

    a0 = jax.random.uniform(ks[10], (DEPTH_2, D_RNN), f32, 0.9, 0.999)
    lam = jnp.log(a0) - jnp.log1p(-a0)
    return {
        'x': nrm(ks[0], (BATCH, SEQ, D_MODEL), 1.0),
        'mem': nrm(ks[1], (BATCH, N_MEM, D_MODEL), 1.0),
        'ln1_w': gain(ks[2], (DEPTH_2, D_MODEL)),
        'w_in': nrm(ks[3], (DEPTH_2, D_MODEL, D_IN_PROJ), D_MODEL ** -0.5),
        'conv_w': nrm(ks[4], (DEPTH_2, CONV_WIDTH, D_RNN), CONV_WIDTH ** -0.5),
        'conv_b': nrm(ks[5], (DEPTH_2, D_RNN), 0.02),
        'rnn_wa': nrm(ks[6], (DEPTH_2, N_RNN_BLOCKS, RNN_BLOCK, RNN_BLOCK), RNN_BLOCK ** -0.5),
        'rnn_ba': nrm(ks[7], (DEPTH_2, D_RNN), 0.02),
        'rnn_wx': nrm(ks[8], (DEPTH_2, N_RNN_BLOCKS, RNN_BLOCK, RNN_BLOCK), RNN_BLOCK ** -0.5),
        'rnn_bx': nrm(ks[9], (DEPTH_2, D_RNN), 0.02),
        'rnn_lambda': lam,
        'rel_bias': nrm(ks[11], (DEPTH_2, N_ATT_HEADS, 2 * REL_CLIP + 1), 0.2),
        'gn_rnn_w': gain(ks[12], (DEPTH_2, D_RNN)),
        'gn_att_w': gain(ks[13], (DEPTH_2, D_ATT)),
        'w_out': nrm(ks[14], (DEPTH_2, D_MIX_2, D_MODEL), D_MIX_2 ** -0.5),
        'ln2_w': gain(ks[15], (DEPTH_2, D_MODEL)),
        'mem_norm_w': gain(ks[16], (D_MODEL,)),
        'xq_w': nrm(ks[17], (DEPTH_2, D_MODEL, D_MODEL), D_MODEL ** -0.5),
        'xk_w': nrm(ks[18], (DEPTH_2, D_MODEL, D_MODEL), D_MODEL ** -0.5),
        'xv_w': nrm(ks[19], (DEPTH_2, D_MODEL, D_MODEL), D_MODEL ** -0.5),
        'xo_w': nrm(ks[20], (DEPTH_2, D_MODEL, D_MODEL), D_MODEL ** -0.5),
        'ln3_w': gain(ks[21], (DEPTH_2, D_MODEL)),
        'router_group_w': nrm(ks[22], (DEPTH_2, D_MODEL, N_GROUPS), D_MODEL ** -0.5),
        'router_group_b': nrm(ks[23], (DEPTH_2, N_GROUPS), 0.01),
        'router_expert_w': nrm(ks[24], (DEPTH_2, N_GROUPS, D_MODEL, EXPERTS_PER_GROUP), D_MODEL ** -0.5),
        'router_expert_b': nrm(ks[25], (DEPTH_2, N_GROUPS, EXPERTS_PER_GROUP), 0.01),
        'expert_gate_w': nrm(ks[26], (DEPTH_2, N_EXPERTS, D_MODEL, D_EXPERT), D_MODEL ** -0.5),
        'expert_up_w': nrm(ks[27], (DEPTH_2, N_EXPERTS, D_MODEL, D_EXPERT), D_MODEL ** -0.5),
        'expert_down_w': nrm(ks[28], (DEPTH_2, N_EXPERTS, D_EXPERT, D_MODEL), D_EXPERT ** -0.5),
        'final_norm_w': gain(ks[29], (D_MODEL,)),
    }

def second_block(x, mem, ln1_w, w_in, conv_w, conv_b, rnn_wa, rnn_ba, rnn_wx, rnn_bx, rnn_lambda,
              rel_bias, gn_rnn_w, gn_att_w, w_out, ln2_w, mem_norm_w, xq_w, xk_w, xv_w, xo_w,
              ln3_w, router_group_w, router_group_b, router_expert_w, router_expert_b,
              expert_gate_w, expert_up_w, expert_down_w, final_norm_w):
    mem_n = rms_norm_2(mem, mem_norm_w)
    for l in range(DEPTH_2):
        h = rms_norm_2(x, ln1_w[l])
        proj = h @ w_in[l]
        xr = proj[..., :D_RNN]
        xg = proj[..., D_RNN:2 * D_RNN]
        q = proj[..., 2 * D_RNN:2 * D_RNN + D_ATT]
        k = proj[..., 2 * D_RNN + D_ATT:2 * D_RNN + 2 * D_ATT]
        v = proj[..., 2 * D_RNN + 2 * D_ATT:]
        y_rnn = recurrent_group(xr, xg, conv_w[l], conv_b[l], rnn_wa[l], rnn_ba[l],
                                rnn_wx[l], rnn_bx[l], rnn_lambda[l])
        y_att = chunk_band_attention(q, k, v, rel_bias[l])
        mixed = jnp.concatenate([rms_norm_2(y_rnn, gn_rnn_w[l]), rms_norm_2(y_att, gn_att_w[l])], axis=-1)
        x = x + mixed @ w_out[l]
        h = rms_norm_2(x, ln2_w[l])
        x = x + memory_cross_attention(h, mem_n, xq_w[l], xk_w[l], xv_w[l], xo_w[l])
        h = rms_norm_2(x, ln3_w[l])
        x = x + hierarchical_moe(h, router_group_w[l], router_group_b[l], router_expert_w[l],
                                 router_expert_b[l], expert_gate_w[l], expert_up_w[l], expert_down_w[l])
    return rms_norm_2(x, final_norm_w)


def setup_inputs(seed=0):
    out = dict(first_inputs(seed))
    for name, value in second_inputs(seed + 1).items():
        if name != "x":
            out[name + "_2"] = value
    return out


def reference(
    x, meta_tokens, norm_w, w_in, fourier_w, pool_w, pool_scale, q_norm_w, w_uq, kv_norm_w,
    w_ukv, w_out, final_norm_w, mem_2, ln1_w_2, w_in_2, conv_w_2, conv_b_2, rnn_wa_2, rnn_ba_2,
    rnn_wx_2, rnn_bx_2, rnn_lambda_2, rel_bias_2, gn_rnn_w_2, gn_att_w_2, w_out_2, ln2_w_2,
    mem_norm_w_2, xq_w_2, xk_w_2, xv_w_2, xo_w_2, ln3_w_2, router_group_w_2, router_group_b_2,
    router_expert_w_2, router_expert_b_2, expert_gate_w_2, expert_up_w_2, expert_down_w_2,
    final_norm_w_2,
):
    x = first_block(
        x, meta_tokens, norm_w, w_in, fourier_w, pool_w, pool_scale, q_norm_w, w_uq, kv_norm_w,
        w_ukv, w_out, final_norm_w,
    )
    return second_block(
        x, mem_2, ln1_w_2, w_in_2, conv_w_2, conv_b_2, rnn_wa_2, rnn_ba_2, rnn_wx_2, rnn_bx_2,
        rnn_lambda_2, rel_bias_2, gn_rnn_w_2, gn_att_w_2, w_out_2, ln2_w_2, mem_norm_w_2,
        xq_w_2, xk_w_2, xv_w_2, xo_w_2, ln3_w_2, router_group_w_2, router_group_b_2,
        router_expert_w_2, router_expert_b_2, expert_gate_w_2, expert_up_w_2, expert_down_w_2,
        final_norm_w_2,
    )


_drawn_inputs = setup_inputs


def setup_inputs(seed=0):
    import zlib

    import numpy as np

    out = dict(_drawn_inputs(seed))
    spreads = {}
    factors = {'pool_scale': 3.003,
     'q_norm_w': 8.0,
     'kv_norm_w': 5.983,
     'rnn_ba_2': 4.992,
     'rnn_bx_2': 6.281,
     'gn_rnn_w_2': 2.768,
     'gn_att_w_2': 3.061,
     'ln2_w_2': 8.0,
     'mem_norm_w_2': 7.036,
     'router_group_b_2': 54.456,
     'router_expert_b_2': 39.752,
     'final_norm_w_2': 7.781,
     'ln3_w_2': 8.0}
    for name, (base, spread) in spreads.items():
        noise = np.random.default_rng([zlib.crc32(name.encode()), seed]).standard_normal(out[name].shape)
        drawn = base * np.exp(spread * noise) if base else spread * noise
        out[name] = jnp.asarray(drawn.astype(out[name].dtype))
    for name, factor in factors.items():
        out[name] = (out[name] * factor).astype(out[name].dtype)
    return out
```

```python
import math
from contextlib import ExitStack

import concourse.bass as bass
from concourse import mybir

F32 = mybir.dt.float32
ALU = mybir.AluOpType
ACT = mybir.ActivationFunctionType
AX = mybir.AxisListType

P = 128
D = 1024
KD = D // P
SEQ = 512
META = 16
L = SEQ + META
LH = L // 2
LAYERS = 2
LT = [(i * P, min(P, L - i * P)) for i in range(-(-L // P))]
NT = len(LT)
HEADS = 4
QR, KVR = 384, 256
KQ, KKV = QR // P, KVR // P
ROPE = 64
EPS = 1e-6
SCALE1 = (P + ROPE) ** -0.5

RING = 4
PANEL = 2048
PAIR = 1024
NPS = 4

def first_groups():
    g = [("u", 0), ("u", 1), ("rs", 0), ("u", 2), ("u", 3), ("u", 4), ("kr", 0), ("fi", 0), ("fi", 1),
         ("rs", 1), ("rs", 2), ("pi", 0), ("pi", 1)]
    g += [("ga", m) for m in range(8)]
    g += [("q", h) for h in range(HEADS)] + [("qr", 0), ("qr", 1)]
    g += [("kn", h) for h in range(HEADS)] + [("v", i) for i in range(3)]
    g += [("ab", 0)] + [("pq", i) for i in range(NT)] + [("yf", 0), ("yf", 1), ("yp", 0), ("yp", 1)]
    def s(h): return [("s", h, i) for i in range(NT)]
    def t(h): return [("t", h, j) for j in range(NT)]
    g += s(0) + s(1) + t(0) + s(2) + [("a", 0)] + t(1) + s(3) + [("a", 1)] + t(2) + [("a", 2)] + t(3) + [("a", 3)]
    g += [("o", m) for m in range(8)]
    return g

G1 = first_groups()
assert len(G1) % NPS == 0
ACT_OWNS1 = ("rs", "q", "kn", "v", "pq", "s", "t")
V1 = [g for g in G1 if g[0] not in ACT_OWNS1]
A1 = [g for g in G1 if g[0] in ACT_OWNS1]
GI1 = {g: n for n, g in enumerate(G1)}
VI1 = {g: n + 1 for n, g in enumerate(V1)}
AI1 = {g: n + 1 for n, g in enumerate(A1)}
NG1, NV1, NA1 = len(G1), len(V1), len(A1)

W1 = ([("win", i) for i in range(9)] + [("wuq", 0), ("wuq", 1), ("wukv", 0)]
      + [("dft", i) for i in range(4)] + [("wout", i) for i in range(4)])
NW1 = len(W1)
WI1 = {w: n for n, w in enumerate(W1)}
assert NW1 % RING == 0
W1_LAST = ([("u", 1), ("u", 3), ("kr", 0), ("fi", 1), ("pi", 1), ("ga", 1), ("ga", 3), ("ga", 5), ("ga", 7)]
           + [("q", 3), ("qr", 1), ("v", 2)] + [("yf", 1)] * 4 + [("o", 1), ("o", 3), ("o", 5), ("o", 7)])
WIN_COLS = [(0, 256), (256, 256), (512, 192)] + [(704 + 256 * i, 256) for i in range(6)]
LW_NORM, LW_POOL, LW_Q, LW_KV, LW_FW, LW_PW = 0, 8, 10, 13, 15, 271
LW = 527


class Tiles:
    pass


def first_block(nc, dram, T, sem):
    ctx = ExitStack()
    with ctx:
        def sb(name, shape):
            return ctx.enter_context(nc.sbuf_tensor(name, shape, F32))

        hT, ring, ones, ident, eps, lw, ps = T.hT, T.ring, T.ones, T.ident, T.eps, T.lw, T.ps
        xw = sb("xw", [P, KD, L])
        mix = xw
        gate = sb("gate", [P, 8, L])
        sq = gate
        rstd = sb("rstd", [P, 3, L])
        cq = sb("cq", [P, KQ + KKV, L])
        krE = sb("krE", [P, L])
        krO = sb("krO", [P, L])
        rt = sb("rt", [P, 4, L])
        qn = sb("qn", [P, HEADS, L])
        qr = sb("qr", [P, 2, L])
        kn = sb("kn", [P, HEADS, L])
        v = sb("v", [P, 6, HEADS * P])
        ab = sb("ab", [P, 2, 256])
        pq = sb("pq", [P, NT, 2, 256])
        PW = L + 32
        pin = sb("pin", [P, 2, PW])
        rope = sb("rope", [P, 2, L])
        cnt = sb("cnt", [P, 2, L])
        cdsd = sb("cdsd", [P, 2, P])
        pbuf = sb("pbuf", [P, 2 * NT * L])
        probs = pbuf[:, :].rearrange("p (b i n) -> p b i n", b=2, i=NT)
        s2 = pbuf[:, 0:2 * PW].rearrange("p (c n) -> p c n", c=2)
        s4 = pbuf[:, 2 * PW:4 * PW].rearrange("p (c n) -> p c n", c=2)
        s8 = pbuf[:, 4 * PW:5 * PW]
        pr = pbuf[:, 5 * PW:5 * PW + 2 * L].rearrange("p (c n) -> p c n", c=2)
        fin = pbuf[:, 5 * PW + 2 * L:5 * PW + 4 * L].rearrange("p (c n) -> p c n", c=2)
        pT = sb("pT", [P, NT, L])
        nmax = sb("nmax", [P, HEADS * NT])
        rsum = sb("rsum", [P, HEADS * NT])
        rinv = sb("rinv", [P, HEADS * NT])
        qws = sb("qws", [P, KQ])

        mm_done = sem("mm_done")
        vec_out = sem("vec_out")
        act_out = sem("act_out")
        w_ready = [sem(f"w_ready{i}") for i in range(RING)]
        lw_ready = T.lw_ready
        h_loaded = sem("h_loaded")
        const_ready = sem("const_ready")
        zeroed = sem("zeroed")
        sq_ready = sem("sq_ready")
        rstd_ready = sem("rstd_ready")
        xw_ready = sem("xw_ready")
        cn_ready = sem("cn_ready")
        k_step = sem("k_step")
        kr_ready = sem("kr_ready")
        qr_ready = sem("qr_ready")
        qws_ready = sem("qws_ready")
        pool_step = sem("pool_step")
        silu_done = sem("silu_done")
        max_ready = sem("max_ready")
        inv_ready = sem("inv_ready")
        probs_ready = sem("probs_ready")

        NSQ = KD + KQ + KKV
        NPOOL = 9
        NEXP = HEADS * NT

        def pst(g):
            return ps[GI1[g] % NPS]

        def phalf(g, p0=0, p1=P):
            return pst(g)[p0:p1, :, 0:LH]

        def pflat(g):
            return pst(g)[:, :, :].rearrange("p a n -> p (a n)")

        def two(ap):
            return ap.rearrange("p (a n) -> p a n", a=2)

        block = ctx.enter_context(nc.Block())

        @block.sync
        def _(sp):
            sp.dma_start(hT[:, :, :], dram["hT"].rearrange("(k p) n -> p k n", p=P)).then_inc(h_loaded, 16)
            with sp.Fori(0, LAYERS) as layer:
                for n, (name, i) in enumerate(W1):
                    slot = ring[:, n % RING, :]
                    if n < RING:
                        sp.wait_ge(mm_done, layer * NG1 + GI1[W1_LAST[n - RING]] + 1)
                    else:
                        sp.wait_ge(mm_done, (layer + 1) * NG1 + GI1[W1_LAST[n - RING]] + 1)
                    if name == "dft":
                        src = dram["dft"][i].rearrange("(k p) n -> p k n", p=P)
                        dst = slot[:, 0:NT * LH].rearrange("p (k n) -> p k n", k=NT)
                    else:
                        k = {"win": KD, "wuq": KQ, "wukv": KKV, "wout": KD}[name]
                        c0, c = {"win": WIN_COLS, "wuq": [(0, 512), (512, 256)], "wukv": [(0, 1024)],
                                 "wout": [(256 * m, 256) for m in range(4)]}[name][i]
                        src = dram[name][bass.ds(layer, 1), :, c0:c0 + c].rearrange("a (k p) n -> p (a k) n", p=P)
                        dst = slot[:, 0:k * c].rearrange("p (k n) -> p k n", k=k)
                    sp.dma_start(dst, src).then_inc(w_ready[n % RING], 16)

        @block.gpsimd
        def _(pool):
            pool.dma_start(lw[:, :], dram["lw"][0]).then_inc(lw_ready, 16)
            pool.dma_start(rope[:, :, :], dram["rope"]).then_inc(const_ready, 16)
            pool.dma_start(cnt[:, :, :], dram["cnt"]).then_inc(const_ready, 16)
            pool.dma_start(cdsd[:, :, :], dram["cdsd"]).then_inc(const_ready, 16)
            pool.memset(krE[:, :], 0.0).then_inc(zeroed, 1)
            pool.memset(krO[:, :], 0.0).then_inc(zeroed, 1)
            pool.memset(pin[:, :, 0:16], 0.0).then_inc(zeroed, 1)
            pool.memset(pin[:, :, 16 + L:PW], 0.0).then_inc(zeroed, 1)
            pool.wait_ge(zeroed, 4)
            pool.wait_ge(const_ready, 48)
            with pool.Fori(0, LAYERS) as layer:
                W = slice(16, 16 + L)

                def step(n):
                    pool.wait_ge(pool_step, layer * NPOOL + n)

                pool.wait_ge(vec_out, (layer + 1) * NV1 + VI1["pi", 1])
                pool.tensor_tensor(s2[:, :, 1:PW], pin[:, :, 1:PW], pin[:, :, 0:PW - 1], ALU.add).then_inc(pool_step, 1)
                step(1)
                pool.tensor_tensor(s4[:, :, 2:PW - 1], s2[:, :, 3:PW], s2[:, :, 1:PW - 2], ALU.add).then_inc(pool_step, 1)
                step(2)
                pool.tensor_tensor(s8[:, 4:PW - 3], s4[:, 1, 6:PW - 1], s4[:, 1, 2:PW - 5], ALU.add).then_inc(pool_step, 1)
                step(3)
                pool.tensor_tensor(pr[64:128, 1, :], s8[64:128, 20:20 + L], s8[64:128, 12:12 + L], ALU.add).then_inc(pool_step, 1)
                step(4)
                pool.tensor_tensor(pr[0:64, 0, :], s2[0:64, 0, W], cnt[0:64, 0, :], ALU.mult).then_inc(pool_step, 1)
                step(5)
                pool.tensor_tensor(pr[64:128, 0, :], s4[64:128, 0, W], cnt[64:128, 0, :], ALU.mult).then_inc(pool_step, 1)
                step(6)
                pool.tensor_tensor(pr[0:64, 1, :], s8[0:64, W], cnt[0:64, 1, :], ALU.mult).then_inc(pool_step, 1)
                step(7)
                pool.tensor_tensor(pr[64:128, 1, :], pr[64:128, 1, :], cnt[64:128, 1, :], ALU.mult).then_inc(pool_step, 1)
                step(8)
                pool.tensor_tensor(pr[:, :, :], pr[:, :, :], pin[:, :, W], ALU.subtract).then_inc(pool_step, 1)
                pool.wait_ge(vec_out, (layer + 1) * NV1 + VI1["yp", 1])
                pool.dma_start(lw[:, :], dram["lw"][bass.ds(layer + 1, 1), :, :].rearrange("a p n -> (a p) n")).then_inc(lw_ready, 16)

        @block.tensor
        def _(pe):
            pe.sem_inc(mm_done, NG1)
            pe.wait_ge(T.setup, T.N_SETUP)
            with pe.Fori(0, LAYERS) as layer:

                def begin(g):
                    prev = G1[(GI1[g] - NPS) % NG1]
                    s, idx, per = (act_out, AI1, NA1) if prev in AI1 else (vec_out, VI1, NV1)
                    pe.wait_ge(s, (layer + (0 if GI1[g] < NPS else 1)) * per + idx[prev])

                def panel(name, i):
                    n = WI1[name, i]
                    pe.wait_ge(w_ready[n % RING], (layer * (NW1 // RING) + n // RING + 1) * 16)
                    return ring[:, n % RING, :]

                def vec(g):
                    pe.wait_ge(vec_out, (layer + 1) * NV1 + VI1[g])

                def act(g):
                    pe.wait_ge(act_out, (layer + 1) * NA1 + AI1[g])

                def project(g, w, k, rhs, m=P):
                    begin(g)
                    for c in range(k):
                        for a in range(2):
                            mm = pe.matmul(pst(g)[0:m, a, 0:LH], w[:, c, :], rhs[:, c, a * LH:a * LH + LH],
                                           start=c == 0, stop=c == k - 1)
                    mm.then_inc(mm_done, 1)

                def sums(g, c0, k, ready):
                    begin(g)
                    for c in range(k):
                        pe.wait_ge(sq_ready, layer * NSQ + ready + c)
                        for a in range(2):
                            mm = pe.matmul(pst(g)[:, a, 0:LH], ones[:, :], sq[:, c0 + c, a * LH:a * LH + LH],
                                           start=c == 0, stop=c == k - 1)
                    mm.then_inc(mm_done, 1)

                chunks = [("u", 0), ("u", 1), ("u", 2), ("u", 3), ("u", 4), ("kr", 0), ("fi", 0), ("fi", 1),
                          ("pi", 0), ("pi", 1)] + [("ga", m) for m in range(8)]
                pe.wait_ge(xw_ready, layer * KD + KD)
                for n, g in enumerate(chunks):
                    width = WIN_COLS[n // 2][1]
                    w = panel("win", n // 2)[:, 0:KD * width].rearrange("p (k n) -> p k n", k=KD)
                    m = 64 if g[0] == "kr" else P
                    project(g, w[:, :, n % 2 * P:n % 2 * P + m], KD, xw, m)
                    if g == ("u", 1):
                        sums(("rs", 0), 0, KD, 1)
                    if g == ("fi", 1):
                        sums(("rs", 1), 0, KQ, 1 + KD)
                        sums(("rs", 2), KQ, KKV, 1 + KD + KQ)

                pe.wait_ge(cn_ready, layer * (KQ + KKV) + KQ + KKV)
                w = panel("wuq", 0)[:, 0:KQ * 512].rearrange("p (k n) -> p k n", k=KQ)
                for h in range(HEADS):
                    project(("q", h), w[:, :, h * P:h * P + P], KQ, cq)
                w = panel("wuq", 1)[:, 0:KQ * 256].rearrange("p (k n) -> p k n", k=KQ)
                for c in range(2):
                    project(("qr", c), w[:, :, c * P:c * P + P], KQ, cq)
                w = panel("wukv", 0).rearrange("p (k n) -> p k n", k=KKV)
                for h in range(HEADS):
                    project(("kn", h), w[:, :, h * P:h * P + P], KKV, cq[:, KQ:, :])
                for g in range(3):
                    begin(("v", g))
                    for b, (t0, m) in enumerate(LT[2 * g:2 * g + 2]):
                        for c in range(KKV):
                            mm = pe.matmul(pst(("v", g))[0:m, b, :], cq[:, KQ + c, t0:t0 + m], w[:, c, 512:1024],
                                           start=c == 0, stop=c == KKV - 1)
                    mm.then_inc(mm_done, 1)

                begin(("ab", 0))
                pe.wait_ge(lw_ready, layer * 16 + 16)
                pe.wait_ge(const_ready, 48)
                for c in range(2):
                    for f in range(2):
                        mm = pe.matmul(pst(("ab", 0))[:, c, f * P:f * P + P], cdsd[:, f, :],
                                       lw[:, LW_FW + c * P:LW_FW + c * P + P], start=True, stop=True)
                mm.then_inc(mm_done, 1)
                vec(("ab", 0))
                for i, (t0, m) in enumerate(LT):
                    begin(("pq", i))
                    for c in range(2):
                        mm = pe.matmul(pst(("pq", i))[0:m, c, 0:256], fin[:, c, t0:t0 + m], ab[:, c, :],
                                       start=True, stop=True)
                    mm.then_inc(mm_done, 1)
                act(("pq", NT - 1))
                begin(("yf", 0))
                begin(("yf", 1))
                for a in range(2):
                    for f in range(2):
                        tab = panel("dft", 2 * a + f)[:, 0:NT * LH].rearrange("p (k n) -> p k n", k=NT)
                        for c in range(2):
                            for i, (t0, m) in enumerate(LT):
                                mm = pe.matmul(pst(("yf", c))[:, a, 0:LH], pq[0:m, i, c, f * P:f * P + P],
                                               tab[0:m, i, :], start=f == 0 and i == 0, stop=f == 1 and i == NT - 1)
                            if a == 1 and f == 1:
                                mm.then_inc(mm_done, 1)

                pe.wait_ge(pool_step, layer * NPOOL + NPOOL)
                for c in range(2):
                    g = ("yp", c)
                    begin(g)
                    for a in range(2):
                        mm = pe.matmul(pst(g)[:, a, 0:LH], lw[:, LW_PW + c * P:LW_PW + c * P + P],
                                       pr[:, c, a * LH:a * LH + LH], start=True, stop=True)
                    mm.then_inc(mm_done, 1)

                def scores(h):
                    kr = krO if h % 2 else krE
                    for i, (t0, m) in enumerate(LT):
                        g = ("s", h, i)
                        begin(g)
                        for a in range(2):
                            keys = slice(a * LH, a * LH + LH)
                            pe.matmul(pst(g)[0:m, a, 0:LH], qn[:, h, t0:t0 + m], kn[:, h, keys], start=True, stop=False)
                            mm = pe.matmul(pst(g)[0:m, a, 0:LH], qr[:, h // 2, t0:t0 + m], kr[:, keys], start=False, stop=True)
                        mm.then_inc(mm_done, 1)

                def turn(h):
                    pe.wait_ge(probs_ready, layer * NEXP + h * NT + NT)
                    for j, (k0, kj) in enumerate(LT):
                        g = ("t", h, j)
                        begin(g)
                        for i, (t0, m) in enumerate(LT):
                            mm = pe.transpose(pflat(g)[0:kj, t0:t0 + m], probs[0:m, h % 2, i, k0:k0 + kj], ident[0:m, 0:m])
                        mm.then_inc(mm_done, 1)

                def attend(h):
                    g = ("a", h)
                    begin(g)
                    act(("t", h, NT - 1))
                    for j, (k0, kj) in enumerate(LT):
                        for a in range(2):
                            mm = pe.matmul(pst(g)[:, a, 0:LH], v[0:kj, j, h * P:h * P + P], pT[0:kj, j, a * LH:a * LH + LH],
                                           start=j == 0, stop=j == NT - 1)
                    mm.then_inc(mm_done, 1)

                act(("v", 2))
                pe.wait_ge(kr_ready, layer + 1)
                pe.wait_ge(qr_ready, layer + 1)
                scores(0)
                scores(1)
                turn(0)
                scores(2)
                attend(0)
                turn(1)
                scores(3)
                attend(1)
                turn(2)
                attend(2)
                turn(3)
                attend(3)

                vec(("a", HEADS - 1))
                for m in range(KD):
                    w = panel("wout", m // 2).rearrange("p (k n) -> p k n", k=KD)
                    project(("o", m), w[:, :, m % 2 * P:m % 2 * P + P], KD, mix)

        @block.vector
        def _(dve):
            dve.sem_inc(vec_out, NV1)
            dve.wait_ge(const_ready, 48)
            dve.wait_ge(h_loaded, 16)
            dve.wait_ge(zeroed, 4)
            with dve.Fori(0, LAYERS) as layer:

                def wait_mm(g):
                    dve.wait_ge(mm_done, (layer + 1) * NG1 + GI1[g] + 1)

                def wait_own(g):
                    dve.wait_ge(vec_out, (layer + 1) * NV1 + VI1[g])

                def normed(g, out, r):
                    wait_mm(g)
                    dve.tensor_tensor(two(out), phalf(g), two(rstd[:, r, :]), ALU.mult).then_inc(vec_out, 1)

                dve.wait_ge(vec_out, (layer + 1) * NV1)
                dve.wait_ge(lw_ready, layer * 16 + 16)
                for k in range(KD):
                    dve.tensor_scalar(xw[:, k, :], hT[:, k, :], lw[:, LW_NORM + k:LW_NORM + k + 1], None, ALU.mult).then_inc(xw_ready, 1)
                dve.tensor_scalar(qws[:, :], lw[:, LW_Q:LW_Q + KQ], SCALE1, None, ALU.mult).then_inc(qws_ready, 1)
                dve.wait_ge(rstd_ready, layer * 3 + 1)
                for k in range(5):
                    normed(("u", k), cq[:, k, :], 0)

                g = ("kr", 0)
                wait_mm(g)
                dve.tensor_tensor(two(rt[0:32, 0, :]), phalf(g, 0, 32), two(rstd[0:32, 0, :]), ALU.mult)
                dve.tensor_tensor(two(rt[0:32, 1, :]), phalf(g, 32, 64), two(rstd[32:64, 0, :]), ALU.mult).then_inc(vec_out, 1)
                wait_own(g)
                dve.tensor_tensor(rt[0:32, 2, :], rt[0:32, 0, :], rope[0:32, 0, :], ALU.mult)
                dve.tensor_tensor(rt[0:32, 3, :], rt[0:32, 1, :], rope[0:32, 1, :], ALU.mult).then_inc(k_step, 1)
                dve.wait_ge(k_step, layer * 3 + 1)
                dve.tensor_tensor(krE[0:32, :], rt[0:32, 2, :], rt[0:32, 3, :], ALU.subtract)
                dve.tensor_tensor(krO[64:96, :], rt[0:32, 2, :], rt[0:32, 3, :], ALU.subtract).then_inc(k_step, 1)
                dve.wait_ge(k_step, layer * 3 + 2)
                dve.tensor_tensor(rt[0:32, 2, :], rt[0:32, 1, :], rope[0:32, 0, :], ALU.mult)
                dve.tensor_tensor(rt[0:32, 3, :], rt[0:32, 0, :], rope[0:32, 1, :], ALU.mult).then_inc(k_step, 1)
                dve.wait_ge(k_step, layer * 3 + 3)
                dve.tensor_tensor(krE[32:64, :], rt[0:32, 2, :], rt[0:32, 3, :], ALU.add)
                dve.tensor_tensor(krO[96:128, :], rt[0:32, 2, :], rt[0:32, 3, :], ALU.add).then_inc(kr_ready, 1)

                for c in range(2):
                    normed(("fi", c), fin[:, c, :], 0)
                for c in range(2):
                    normed(("pi", c), pin[:, c, 16:16 + L], 0)

                dve.wait_ge(qws_ready, layer + 1)
                dve.wait_ge(rstd_ready, layer * 3 + 2)
                for k in range(KQ):
                    dve.scalar_tensor_tensor(cq[:, k, :], cq[:, k, :], qws[:, k:k + 1], rstd[:, 1, :], ALU.mult, ALU.mult).then_inc(cn_ready, 1)
                dve.wait_ge(rstd_ready, layer * 3 + 3)
                for k in range(KKV):
                    dve.scalar_tensor_tensor(cq[:, KQ + k, :], cq[:, KQ + k, :], lw[:, LW_KV + k:LW_KV + k + 1], rstd[:, 2, :],
                                             ALU.mult, ALU.mult).then_inc(cn_ready, 1)
                for m in range(8):
                    normed(("ga", m), gate[:, m, :], 0)

                for c, order in ((0, (0, 1)), (1, (1, 0))):
                    g = ("qr", c)
                    wait_mm(g)
                    dve.tensor_tensor(two(rt[:, 2 * c, :]), phalf(g), two(rope[:, order[0], :]), ALU.mult)
                    dve.tensor_tensor(two(rt[:, 2 * c + 1, :]), phalf(g), two(rope[:, order[1], :]), ALU.mult).then_inc(vec_out, 1)
                wait_own(("qr", 1))
                for h in range(HEADS):
                    src, to = slice(32 * h, 32 * h + 32), 64 * (h % 2)
                    dve.tensor_tensor(qr[to:to + 32, h // 2, :], rt[src, 0, :], rt[src, 2, :], ALU.subtract)
                    last = dve.tensor_tensor(qr[to + 32:to + 64, h // 2, :], rt[src, 1, :], rt[src, 3, :], ALU.add)
                last.then_inc(qr_ready, 1)

                wait_mm(("ab", 0))
                dve.tensor_copy(ab[:, :, :], pst(("ab", 0))[:, :, 0:256]).then_inc(vec_out, 1)
                for c in range(2):
                    g = ("yf", c)
                    wait_mm(g)
                    dve.wait_ge(silu_done, layer * 8 + c + 1)
                    dve.tensor_tensor(two(mix[:, c, :]), phalf(g), two(gate[:, c, :]), ALU.mult).then_inc(vec_out, 1)
                for c in range(2):
                    g = ("yp", c)
                    wait_mm(g)
                    dve.wait_ge(silu_done, layer * 8 + c + 3)
                    dve.scalar_tensor_tensor(two(mix[:, 2 + c, :]), phalf(g), lw[:, LW_POOL + c:LW_POOL + c + 1], two(gate[:, 2 + c, :]),
                                             ALU.mult, ALU.mult).then_inc(vec_out, 1)
                dve.wait_ge(silu_done, layer * 8 + 8)

                def maximum(h, i):
                    g, m, n = ("s", h, i), LT[i][1], h * NT + i
                    wait_mm(g)
                    dve.tensor_reduce(nmax[0:m, n:n + 1], phalf(g, 0, m), AX.XY, ALU.max, negate=True).then_inc(max_ready, 1)

                def normalise(h, i):
                    m, n = LT[i][1], h * NT + i
                    dve.wait_ge(act_out, (layer + 1) * NA1 + AI1["s", h, i])
                    dve.reciprocal(rinv[0:m, n:n + 1], rsum[0:m, n:n + 1]).then_inc(inv_ready, 1)
                    dve.wait_ge(inv_ready, layer * NEXP + n + 1)
                    dve.tensor_scalar(probs[0:m, h % 2, i, :], probs[0:m, h % 2, i, :], rinv[0:m, n:n + 1], None,
                                      ALU.mult).then_inc(probs_ready, 1)

                def softmax(h):
                    for i in range(NT):
                        maximum(h, i)
                        if i:
                            normalise(h, i - 1)
                    normalise(h, NT - 1)

                def gated(h):
                    wait_mm(("a", h))
                    dve.tensor_tensor(two(mix[:, 4 + h, :]), phalf(("a", h)), two(gate[:, 4 + h, :]), ALU.mult).then_inc(vec_out, 1)

                softmax(0)
                softmax(1)
                softmax(2)
                gated(0)
                softmax(3)
                for h in range(1, HEADS):
                    gated(h)
                for m in range(KD):
                    wait_mm(("o", m))
                    dve.tensor_tensor(two(hT[:, m, :]), phalf(("o", m)), two(hT[:, m, :]), ALU.add).then_inc(vec_out, 1)

        @block.scalar
        def _(act):
            act.sem_inc(act_out, NA1)
            act.wait_ge(h_loaded, 16)
            act.wait_ge(T.setup, T.N_SETUP)
            with act.Fori(0, LAYERS) as layer:

                def wait_mm(g):
                    act.wait_ge(mm_done, (layer + 1) * NG1 + GI1[g] + 1)

                def wait_vec(g):
                    act.wait_ge(vec_out, (layer + 1) * NV1 + VI1[g])

                def rms(r, size):
                    g = ("rs", r)
                    wait_mm(g)
                    act.activation(two(rstd[:, r, :]), phalf(g), ACT.Ln, bias=eps[:, :], scale=1.0 / size).then_inc(act_out, 1)
                    act.wait_ge(act_out, (layer + 1) * NA1 + AI1[g])
                    act.activation(rstd[:, r, :], rstd[:, r, :], ACT.Exp, scale=-0.5).then_inc(rstd_ready, 1)

                def copy(g, out, src):
                    wait_mm(g)
                    act.activation(out, src, ACT.Copy).then_inc(act_out, 1)

                act.wait_ge(vec_out, (layer + 1) * NV1)
                for k in range(KD):
                    act.activation(sq[:, k, :], hT[:, k, :], ACT.Square).then_inc(sq_ready, 1)
                rms(0, D)
                for k in range(KQ + KKV):
                    wait_vec(("u", k))
                    act.activation(sq[:, k, :], cq[:, k, :], ACT.Square).then_inc(sq_ready, 1)
                rms(1, QR)
                rms(2, KVR)
                for m in range(8):
                    wait_vec(("ga", m))
                    act.activation(gate[:, m, :], gate[:, m, :], ACT.Silu).then_inc(silu_done, 1)
                for h in range(HEADS):
                    copy(("q", h), two(qn[:, h, :]), phalf(("q", h)))
                for h in range(HEADS):
                    copy(("kn", h), two(kn[:, h, :]), phalf(("kn", h)))
                for i in range(2):
                    copy(("v", i), v[:, 2 * i:2 * i + 2, :], pst(("v", i))[:, :, :])
                copy(("v", 2), v[0:LT[-1][1], NT - 1, :], pst(("v", 2))[0:LT[-1][1], 0, :])
                for i, (t0, m) in enumerate(LT):
                    copy(("pq", i), pq[0:m, i, :, :], pst(("pq", i))[0:m, :, 0:256])

                def exponentials(h):
                    for i, (t0, m) in enumerate(LT):
                        n = h * NT + i
                        act.wait_ge(max_ready, layer * NEXP + n + 1)
                        act.activation(two(probs[0:m, h % 2, i, :]), phalf(("s", h, i), 0, m), ACT.Exp, bias=nmax[0:m, n:n + 1],
                                       accum_out=rsum[0:m, n:n + 1]).then_inc(act_out, 1)

                def turned(h):
                    for j, (k0, kj) in enumerate(LT):
                        copy(("t", h, j), pT[0:kj, j, :], pflat(("t", h, j))[0:kj, 0:L])

                exponentials(0)
                exponentials(1)
                turned(0)
                exponentials(2)
                turned(1)
                exponentials(3)
                turned(2)
                turned(3)


MEM = 256
DH = 512
KH = DH // P
AH = 8
XH = 4
TT = SEQ // P
NE, NGRP = 32, 4
NL = NGRP + NE
CONV = 4


def second_groups():
    g = [("nm",), ("kx", 0), ("kx", 1), ("n", 0), ("n", 1)]
    g += [(n, c) for n in ("xr", "xg", "qa", "ka", "va") for c in range(2)]
    g += [("gt", c) for c in range(KH)]
    def s(h): return [("sA", h), ("sB", h)]
    def t(h): return [("tA", h), ("tB", h)]
    g += s(0) + s(1)
    for h in range(AH):
        g += t(h) + (s(h + 2) if h + 2 < AH else []) + [("at", h)]
    g += [("n", 2)] + [("o", m) for m in range(4)] + [("vx", 0), ("vx", 1), ("n", 3)]
    g += [("qx", m) for m in range(4)] + [("sx", 0), ("sx", 1)]
    for h in range(XH):
        g += [("tx", h)] + ([("sx", h + 2)] if h + 2 < XH else []) + [("ax", h)]
    g += [("xo", m) for m in range(4)] + [("n", 4), ("lg",)]
    g += [("ht", i) for i in range(TT)] + [("xt", i) for i in range(TT)]
    return g


G2 = second_groups()
ACT_OWNS2 = ("nm", "n", "kx", "qa", "ka", "gt", "tA", "tB", "qx", "sx", "tx", "ht")
GI2 = {g: n for n, g in enumerate(G2)}
VI2 = {g: n + 1 for n, g in enumerate(g for g in G2 if g[0] not in ACT_OWNS2)}
AI2 = {g: n + 1 for n, g in enumerate(g for g in G2 if g[0] in ACT_OWNS2)}
W2 = ([("xk", i) for i in range(4)] + [("win2", i) for i in range(10)] + [("wout2", i) for i in range(4)]
      + [("xv", i) for i in range(4)] + [("xq", i) for i in range(4)] + [("xo", i) for i in range(4)])
WI2 = {w: n for n, w in enumerate(W2)}
W2_LAST = ([("kx", 0)] * 2 + [("kx", 1)] * 2
           + [(n, c) for n in ("xr", "xg", "qa", "ka") for c in range(2)] + [("va", 1)] * 2
           + [("o", m) for m in range(4)] + [("vx", 1)] * 4 + [("qx", m) for m in range(4)] + [("xo", m) for m in range(4)])
V2 = {}
for _name, _n in (("ln1", KD), ("cw", CONV * KH), ("cb", KH), ("ba", KH), ("bx", KH), ("lam", KH), ("gnr", KH), ("gna", KH),
                  ("ln2", KD), ("mem", KD), ("ln3", KD)):
    V2[_name] = sum(n for _, n in V2.values()), _n
NV2 = sum(n for _, n in V2.values())
LW_VEC = KD
LW_WR = LW_VEC + NV2
LW_RB = LW_WR + KD * NL
assert LW_RB + TT * NL <= LW
SOFF = {3: 0, 2: 512, 1: 896, 0: 1152}
SBW = 1280
NORMS = ["mem", "first", "ln1", "mixed", "ln2", "ln3"]
TINY = 1e-18


def second_block(nc, dram, T, sem):
    ctx = ExitStack()
    with ctx:
        def sb(name, shape):
            return ctx.enter_context(nc.sbuf_tensor(name, shape, F32))

        hT, ring, ones, ident, eps, lw, ps = T.hT, T.ring, T.ones, T.ident, T.eps, T.lw, T.ps
        x = hT[:, :, META:L]
        sq = sb("sq", [P, KD, SEQ])
        xn = sb("xn", [P, KD, SEQ])
        rstd = sb("rstd2", [P, 2, SEQ])
        memT = sb("memT", [P, KD, MEM])
        memn = sb("memn", [P, KD, MEM])
        kx = sb("kx", [P, KD, MEM])
        vx = sb("vx", [P, 2, D])
        wide = sb("wide", [P, KH * (SEQ + 3) + KH * SEQ])
        xr = wide[:, 0:KH * (SEQ + 3)].rearrange("p (c n) -> p c n", c=KH)
        xg = wide[:, KH * (SEQ + 3):].rearrange("p (c n) -> p c n", c=KH)
        qx = wide[:, 0:KD * SEQ].rearrange("p (c n) -> p c n", c=KD)
        qa = sb("qa", [P, KH, SEQ])
        ka = sb("ka", [P, KH, SEQ])
        va = sb("va", [P, TT, DH])
        bias = sb("bias", [P, AH, SEQ])
        ox = bias
        sbuf = sb("sbuf", [P, 2, SBW])
        pT = sb("pT2", [P, TT, SEQ])
        xc = sb("xc", [P, KH, SEQ])
        r = memT[:, :, :].rearrange("p (c b) n -> p c (b n)", c=KH)
        gi = vx[:, :, :].rearrange("p c (b n) -> p (c b) n", b=2)
        aa, th = sq[:, 0:KH, :], sq[:, KH:, :]
        yr = xn[:, 0:KH, :]
        vec = lw[:, LW_VEC:LW_VEC + NV2]
        wr = lw[:, LW_WR:LW_WR + KD * NL].rearrange("p (k n) -> p k n", k=KD)
        rb = lw[:, LW_RB:LW_RB + TT * NL]
        wab = sb("wab", [P, 2 * KH, P])
        nsp = sb("nsp", [P, 6, KH])
        mx = sb("mx", [P, 4 * AH])
        nmx = sb("nmx", [P, 4 * (AH + XH)])
        rsum = sb("rsum2", [P, 4 * (AH + XH)])
        rinv = sb("rinv2", [P, 4 * (AH + XH)])

        mm_done = sem("mm2_done")
        vec_out = sem("vec2_out")
        act_out = sem("act2_out")
        w_ready = [sem(f"w2_ready{i}") for i in range(RING)]
        loaded = sem("loaded2")
        mem_loaded = sem("mem_loaded")
        sq_ready = sem("sq2_ready")
        rstd_ready = sem("rstd2_ready")
        norm_ready = sem("norm_ready")
        pad_ready = sem("pad_ready")
        mask_ready = sem("mask_ready")
        conv_step = sem("conv_step")
        sp_step = sem("sp_step")
        sp_exp = sem("sp_exp")
        decay_ready = sem("decay_ready")
        m2_ready = sem("m2_ready")
        logs_ready = sem("logs_ready")
        root_ready = sem("root_ready")
        gelu_ready = sem("gelu_ready")
        rnn_step = sem("rnn_step")
        scanned = sem("scanned")
        max_ready = sem("max2_ready")
        nmax_ready = sem("nmax_ready")
        exp_done = sem("exp2_done")
        inv_ready = sem("inv2_ready")
        probs_ready = sem("probs2_ready")

        def col(name, c):
            o = V2[name][0] + c
            return vec[:, o:o + 1]

        def pst(g):
            return ps[GI2[g] % NPS]

        def pflat(g):
            return pst(g)[:, :, :].rearrange("p a n -> p (a n)")

        def norm_at(name):
            return KD * NORMS.index(name)

        block = ctx.enter_context(nc.Block())

        @block.sync
        def _(sp):
            sp.dma_start(memT[:, :, :], dram["memT"].rearrange("(k p) n -> p k n", p=P)).then_inc(mem_loaded, 16)
            for n, (name, i) in enumerate(W2):
                if n >= RING:
                    sp.wait_ge(mm_done, GI2[W2_LAST[n - RING]] + 1)
                sp.dma_start(ring[:, n % RING, :].rearrange("p (k n) -> p k n", k=KD),
                             dram[name][:, 256 * i:256 * i + 256].rearrange("(k p) n -> p k n", p=P)).then_inc(w_ready[n % RING], 16)

        @block.gpsimd
        def _(pool):
            pool.dma_start(wab[:, :, :], dram["wab"]).then_inc(loaded, 16)
            pool.dma_start(bias[:, :, :], dram["bias"].rearrange("h p n -> p h n")).then_inc(loaded, 16)
            pool.memset(xr[:, :, 0:3], 0.0).then_inc(pad_ready, 1)
            pool.wait_ge(loaded, 16 * 2)
            pool.memset(bias[0:64, :, SEQ - 64:SEQ], -1e30).then_inc(mask_ready, 1)
            pool.wait_ge(act_out, AI2["gt", KH - 1])
            pool.tensor_tensor(gi, gi, xc[:, :, :], ALU.mult).then_inc(rnn_step, 1)
            pool.wait_ge(logs_ready, 2)
            pool.tensor_tensor(yr, yr, th, ALU.subtract).then_inc(rnn_step, 1)
            pool.wait_ge(root_ready, 1)
            pool.wait_ge(rnn_step, 2)
            pool.tensor_tensor(gi, gi, yr, ALU.mult).then_inc(rnn_step, 1)
            pool.wait_ge(scanned, KH)
            pool.wait_ge(gelu_ready, 1)
            pool.tensor_tensor(yr, yr, xg, ALU.mult).then_inc(rnn_step, 1)

        @block.tensor
        def _(pe):
            def begin(g):
                n = GI2[g]
                if n >= NPS:
                    prev = G2[n - NPS]
                    if prev in AI2:
                        pe.wait_ge(act_out, AI2[prev])
                    else:
                        pe.wait_ge(vec_out, VI2[prev])

            def panel(name, i):
                n = WI2[name, i]
                pe.wait_ge(w_ready[n % RING], 16 * (n // RING + 1))
                return ring[:, n % RING, :].rearrange("p (k n) -> p k n", k=KD)

            def sums(g, name, banks=1, n=SEQ):
                begin(g)
                per = KD // banks
                for c in range(KD):
                    pe.wait_ge(sq_ready, norm_at(name) + c + 1)
                    mm = pe.matmul(pst(g)[:, c // per, 0:n], ones[:, :], sq[:, c, 0:n], start=c % per == 0, stop=c % per == per - 1)
                mm.then_inc(mm_done, 1)

            def two(g, name, i, rhs):
                w = panel(name, i)
                begin(g)
                for b in range(2):
                    for k in range(KD):
                        mm = pe.matmul(pst(g)[:, b, :], w[:, k, b * P:b * P + P], rhs[:, k, :], start=k == 0, stop=k == KD - 1)
                mm.then_inc(mm_done, 1)

            pe.wait_ge(T.lw_ready, 16 * (LAYERS + 1))
            sums(("nm",), "mem", n=MEM)
            pe.wait_ge(norm_ready, norm_at("mem") + KD)
            for q in range(2):
                g = ("kx", q)
                begin(g)
                for m in range(4):
                    w = panel("xk", 2 * q + m // 2)
                    for k in range(KD):
                        mm = pe.matmul(pflat(g)[:, m * MEM:m * MEM + MEM], w[:, k, m % 2 * P:m % 2 * P + P], memn[:, k, :],
                                       start=k == 0, stop=k == KD - 1)
                mm.then_inc(mm_done, 1)
            sums(("n", 0), "first")
            sums(("n", 1), "ln1")
            pe.wait_ge(norm_ready, norm_at("ln1") + KD)
            for j, name in enumerate(("xr", "xg", "qa", "ka")):
                for c in range(2):
                    two((name, c), "win2", 2 * j + c, xn)
            begin(("va", 0))
            begin(("va", 1))
            for half in range(2):
                w = panel("win2", 8 + half)
                for i in range(TT):
                    for k in range(KD):
                        mm = pe.matmul(pst(("va", i // 2))[:, i % 2, half * 256:half * 256 + 256], xn[:, k, i * P:i * P + P], w[:, k, :],
                                       start=k == 0, stop=k == KD - 1)
                    if half and i % 2:
                        mm.then_inc(mm_done, 1)

            pe.wait_ge(loaded, 16 * 2)
            pe.wait_ge(conv_step, CONV)
            for c in range(KH):
                g = ("gt", c)
                begin(g)
                for b in range(2):
                    mm = pe.matmul(pst(g)[:, b, :], wab[:, b * KH + c, :], xc[:, c, :], start=True, stop=True)
                mm.then_inc(mm_done, 1)

            def scores(h):
                rows = slice(64 * (h % 2), 64 * (h % 2) + 64)
                for g, tiles in ((("sA", h), (3, 2)), (("sB", h), (1, 0))):
                    begin(g)
                    for b, i in enumerate(tiles):
                        mm = pe.matmul(pst(g)[:, b, 0:(i + 1) * P], qa[rows, h // 2, i * P:i * P + P], ka[rows, h // 2, 0:(i + 1) * P],
                                       start=True, stop=True)
                    mm.then_inc(mm_done, 1)

            def turn(h):
                pe.wait_ge(probs_ready, 4 * h + 4)
                for g, js in ((("tA", h), (0, 1)), (("tB", h), (2, 3))):
                    begin(g)
                    for b, j in enumerate(js):
                        for i in range(j, TT):
                            o = SOFF[i] + j * P
                            mm = pe.transpose(pst(g)[:, b, i * P:i * P + P], sbuf[:, h % 2, o:o + P], ident[:, :])
                    mm.then_inc(mm_done, 1)

            def attend(h):
                g = ("at", h)
                begin(g)
                pe.wait_ge(act_out, AI2["tB", h])
                for j in range(TT):
                    mm = pe.matmul(pst(g)[0:64, 0, j * P:SEQ], va[:, j, h * 64:h * 64 + 64], pT[:, j, j * P:SEQ],
                                   start=j == 0, stop=j == TT - 1)
                mm.then_inc(mm_done, 1)

            pe.wait_ge(act_out, AI2["ka", 1])
            pe.wait_ge(vec_out, VI2["va", 1])
            scores(0)
            scores(1)
            for h in range(AH):
                turn(h)
                if h + 2 < AH:
                    scores(h + 2)
                attend(h)

            sums(("n", 2), "mixed", banks=2)
            pe.wait_ge(norm_ready, norm_at("mixed") + KD)
            for m in range(4):
                two(("o", m), "wout2", m, xn)
            begin(("vx", 0))
            begin(("vx", 1))
            for q in range(4):
                w = panel("xv", q)
                for j in range(2):
                    for k in range(KD):
                        mm = pe.matmul(pflat(("vx", j))[:, q * 256:q * 256 + 256], memn[:, k, j * P:j * P + P], w[:, k, :],
                                       start=k == 0, stop=k == KD - 1)
                    if q == 3:
                        mm.then_inc(mm_done, 1)
            sums(("n", 3), "ln2")
            pe.wait_ge(norm_ready, norm_at("ln2") + KD)
            for m in range(4):
                two(("qx", m), "xq", m, xn)

            def cross_scores(h):
                g = ("sx", h)
                begin(g)
                for i in range(TT):
                    for c in range(2):
                        mm = pe.matmul(pflat(g)[:, i * MEM:i * MEM + MEM], qx[:, 2 * h + c, i * P:i * P + P], kx[:, 2 * h + c, :],
                                       start=c == 0, stop=c == 1)
                mm.then_inc(mm_done, 1)

            def cross_turn(h):
                g = ("tx", h)
                pe.wait_ge(probs_ready, 4 * AH + 4 * h + 4)
                begin(g)
                for j in range(2):
                    for i in range(TT):
                        mm = pe.transpose(pst(g)[:, j, i * P:i * P + P], sbuf[:, h % 2, i * MEM + j * P:i * MEM + j * P + P], ident[:, :])
                mm.then_inc(mm_done, 1)

            def cross_attend(h):
                g = ("ax", h)
                begin(g)
                pe.wait_ge(act_out, AI2["tx", h])
                for b in range(2):
                    for j in range(2):
                        mm = pe.matmul(pst(g)[:, b, :], vx[:, j, h * 256 + b * P:h * 256 + b * P + P], pT[:, j, :],
                                       start=j == 0, stop=j == 1)
                mm.then_inc(mm_done, 1)

            pe.wait_ge(act_out, AI2["qx", 3])
            pe.wait_ge(vec_out, VI2["vx", 1])
            cross_scores(0)
            cross_scores(1)
            for h in range(XH):
                cross_turn(h)
                if h + 2 < XH:
                    cross_scores(h + 2)
                cross_attend(h)
            pe.wait_ge(vec_out, VI2["ax", XH - 1])
            for m in range(4):
                two(("xo", m), "xo", m, ox)

            sums(("n", 4), "ln3")
            g = ("lg",)
            begin(g)
            pe.wait_ge(norm_ready, norm_at("ln3") + KD)
            for i in range(TT):
                for k in range(KD):
                    mm = pe.matmul(pst(g)[:, 0, i * NL:i * NL + NL], xn[:, k, i * P:i * P + P], wr[:, k, :], start=k == 0, stop=k == KD - 1)
            mm.then_inc(mm_done, 1)
            for name, src in (("ht", xn), ("xt", x)):
                for i in range(TT):
                    g = (name, i)
                    begin(g)
                    for k in range(KD):
                        mm = pe.transpose(pflat(g)[:, k * P:k * P + P], src[:, k, i * P:i * P + P], ident[:, :])
                    mm.then_inc(mm_done, 1)

        @block.vector
        def _(dve):
            def wait_mm(g):
                dve.wait_ge(mm_done, GI2[g] + 1)

            def norm(name, out, src, w, r=lambda k: 0, n=SEQ):
                dve.wait_ge(rstd_ready, NORMS.index(name) + 1)
                for k in range(KD):
                    dve.scalar_tensor_tensor(out[:, k, 0:n], src[:, k, 0:n], w(k), rstd[:, r(k), 0:n], ALU.mult, ALU.mult).then_inc(norm_ready, 1)

            def copy(g, out, src):
                wait_mm(g)
                dve.tensor_copy(out, src).then_inc(vec_out, 1)

            dve.wait_ge(loaded, 16 * 2)
            dve.wait_ge(mem_loaded, 16)
            dve.wait_ge(pad_ready, 1)
            dve.wait_ge(mask_ready, 1)
            dve.wait_ge(T.lw_ready, 16 * (LAYERS + 1))
            norm("mem", memn, memT, lambda k: col("mem", k), n=MEM)
            norm("first", x, x, lambda k: lw[:, k:k + 1])
            dve.wait_ge(norm_ready, norm_at("first") + KD)

            lam = vec[:, V2["lam"][0]:V2["lam"][0] + KH]
            absl, e, z, z2, acc, res = (nsp[:, i, :] for i in range(6))
            steps = [0]

            def step(ins):
                steps[0] += 1
                ins.then_inc(sp_step, 1)
                dve.wait_ge(sp_step, steps[0])

            step(dve.scalar_tensor_tensor(absl, lam, -1.0, lam, ALU.mult, ALU.max))
            dve.wait_ge(sp_exp, 1)
            step(dve.tensor_scalar(z2, e, 2.0, None, ALU.add))
            step(dve.reciprocal(z2, z2))
            step(dve.tensor_tensor(z, e, z2, ALU.mult))
            step(dve.tensor_tensor(z2, z, z, ALU.mult))
            step(dve.tensor_scalar(acc, z2, 1.0 / 17, None, ALU.mult))
            for odd in (15, 13, 11, 9, 7, 5, 3):
                step(dve.scalar_tensor_tensor(acc, acc, 1.0 / odd, z2, ALU.add, ALU.mult))
            step(dve.scalar_tensor_tensor(acc, acc, 1.0, z, ALU.add, ALU.mult))
            step(dve.tensor_scalar(res, lam, -1.0, 0.0, ALU.mult, ALU.max))
            step(dve.scalar_tensor_tensor(res, acc, 2.0, res, ALU.mult, ALU.add))
            step(dve.tensor_scalar(res, res, -8.0, None, ALU.mult))
            T.sp_steps = steps[0]

            norm("ln1", xn, x, lambda k: col("ln1", k))
            for c in range(2):
                copy(("xr", c), xr[:, 2 * c:2 * c + 2, 3:3 + SEQ], pst(("xr", c))[:, :, :])
            for c in range(2):
                copy(("xg", c), xg[:, 2 * c:2 * c + 2, :], pst(("xg", c))[:, :, :])
            dve.wait_ge(vec_out, VI2["xr", 1])
            for c in range(KH):
                last = dve.tensor_scalar(xc[:, c, :], xr[:, c, 3:3 + SEQ], col("cw", 3 * KH + c), col("cb", c), ALU.mult, ALU.add)
            last.then_inc(conv_step, 1)
            for j in range(CONV - 1):
                dve.wait_ge(conv_step, j + 1)
                for c in range(KH):
                    last = dve.scalar_tensor_tensor(xc[:, c, :], xr[:, c, j:j + SEQ], col("cw", j * KH + c), xc[:, c, :],
                                                    ALU.mult, ALU.add)
                last.then_inc(conv_step, 1)
            for c in range(2):
                copy(("va", c), va[:, 2 * c:2 * c + 2, :], pst(("va", c))[:, :, :])

            def biased(h):
                for g, tiles in ((("sA", h), (3, 2)), (("sB", h), (1, 0))):
                    wait_mm(g)
                    for b, i in enumerate(tiles):
                        n = (i + 1) * P
                        last = dve.tensor_tensor_reduce(sbuf[:, h % 2, SOFF[i]:SOFF[i] + n], pst(g)[:, b, 0:n], bias[:, h, SEQ - n:SEQ],
                                                        1.0, -3e38, ALU.add, ALU.max, mx[:, 4 * h + i:4 * h + i + 1])
                    last.then_inc(vec_out, 1)
                dve.wait_ge(vec_out, VI2["sB", h])
                dve.tensor_scalar(nmx[:, 4 * h:4 * h + 4], mx[:, 4 * h:4 * h + 4], -1.0, None, ALU.mult).then_inc(nmax_ready, 1)

            def normalise(h, n, places):
                if h < AH:
                    dve.wait_ge(exp_done, 4 * h + 4)
                else:
                    dve.wait_ge(act_out, AI2["sx", h - AH])
                dve.reciprocal(rinv[:, 4 * h:4 * h + 4], rsum[:, 4 * h:4 * h + 4]).then_inc(inv_ready, 1)
                dve.wait_ge(inv_ready, h + 1)
                for i in range(TT):
                    p = sbuf[:, n, places[i][0]:places[i][0] + places[i][1]]
                    dve.tensor_scalar(p, p, rinv[:, 4 * h + i:4 * h + i + 1], None, ALU.mult).then_inc(probs_ready, 1)

            places = [(SOFF[i], (i + 1) * P) for i in range(TT)]

            def attended(h):
                rows = slice(64 * (h % 2), 64 * (h % 2) + 64)
                copy(("at", h), xn[rows, KH + h // 2, :], pst(("at", h))[0:64, 0, :])

            def decay():
                dve.wait_ge(decay_ready, KH)
                dve.wait_ge(mm_done, GI2["va", 1] + 1)
                dve.tensor_scalar(yr, th, -2.0, TINY, ALU.mult, ALU.max).then_inc(m2_ready, 1)

            def scan():
                dve.wait_ge(rnn_step, 3)
                for c in range(KH):
                    dve.tensor_tensor_scan(yr[:, c, :], aa[:, c, :], gi[:, c, :], 0.0, ALU.mult, ALU.add).then_inc(scanned, 1)

            biased(0)
            decay()
            biased(1)
            normalise(0, 0, places)
            for h in range(AH):
                if h + 1 < AH:
                    normalise(h + 1, (h + 1) % 2, places)
                if h + 2 < AH:
                    biased(h + 2)
                attended(h)
                if h == 1:
                    scan()
            norm("mixed", xn, xn, lambda k: col("gnr", k) if k < KH else col("gna", k - KH), lambda k: k // KH)

            def add(g, m):
                wait_mm(g)
                dve.tensor_tensor(x[:, 2 * m:2 * m + 2, :], pst(g)[:, :, :], x[:, 2 * m:2 * m + 2, :], ALU.add).then_inc(vec_out, 1)

            for m in range(4):
                add(("o", m), m)
            for j in range(2):
                copy(("vx", j), vx[:, j, :], pflat(("vx", j)))
            norm("ln2", xn, x, lambda k: col("ln2", k))

            def cross_max(h):
                wait_mm(("sx", h))
                n = 4 * (AH + h)
                dve.tensor_reduce(nmx[:, n:n + 4], pflat(("sx", h)).rearrange("p (i n) -> p i n", i=TT), AX.X, ALU.max,
                                  negate=True).then_inc(nmax_ready, 1)

            xplaces = [(i * MEM, MEM) for i in range(TT)]
            cross_max(0)
            cross_max(1)
            normalise(AH, 0, xplaces)
            for h in range(XH):
                if h + 1 < XH:
                    normalise(AH + h + 1, (h + 1) % 2, xplaces)
                if h + 2 < XH:
                    cross_max(h + 2)
                copy(("ax", h), ox[:, 2 * h:2 * h + 2, :], pst(("ax", h))[:, :, :])
            for m in range(4):
                add(("xo", m), m)
            norm("ln3", xn, x, lambda k: col("ln3", k))
            wait_mm(("lg",))
            dve.tensor_tensor(T.logits[:, :], pst(("lg",))[:, 0, 0:TT * NL], rb[:, :], ALU.add).then_inc(vec_out, 1)
            for i in range(TT):
                copy(("xt", i), T.xtok[:, i, :], pflat(("xt", i)))

        @block.scalar
        def _(act):
            def wait_mm(g):
                act.wait_ge(mm_done, GI2[g] + 1)

            def square(name, k, src, n=SEQ):
                act.activation(sq[:, k, 0:n], src[:, k, 0:n], ACT.Square).then_inc(sq_ready, 1)

            def rms(g, size, banks=1, n=SEQ):
                wait_mm(g)
                out = rstd[:, 0:banks, 0:n]
                act.activation(out, pst(g)[:, 0:banks, 0:n], ACT.Ln, bias=eps[:, :], scale=1.0 / size).then_inc(act_out, 1)
                act.wait_ge(act_out, AI2[g])
                act.activation(out, out, ACT.Exp, scale=-0.5).then_inc(rstd_ready, 1)

            def copy(g, out, src, scale=1.0):
                wait_mm(g)
                act.activation(out, src, ACT.Copy, scale=scale).then_inc(act_out, 1)

            act.wait_ge(mem_loaded, 16)
            act.wait_ge(T.lw_ready, 16 * (LAYERS + 1))
            for k in range(KD):
                square("mem", k, memT, MEM)
            rms(("nm",), D, n=MEM)
            act.wait_ge(norm_ready, KD)
            for k in range(KD):
                square("first", k, x)
            for q in range(2):
                copy(("kx", q), kx[:, 4 * q:4 * q + 4, :].rearrange("p m n -> p (m n)"), pflat(("kx", q)))
            rms(("n", 0), D)
            for k in range(KD):
                act.wait_ge(norm_ready, norm_at("first") + k + 1)
                square("ln1", k, x)
            act.wait_ge(sp_step, 1)
            act.activation(nsp[:, 1, :], nsp[:, 0, :], ACT.Exp, scale=-1.0).then_inc(sp_exp, 1)
            rms(("n", 1), D)
            for c in range(2):
                copy(("qa", c), qa[:, 2 * c:2 * c + 2, :], pst(("qa", c))[:, :, :], scale=64 ** -0.5)
            for c in range(2):
                copy(("ka", c), ka[:, 2 * c:2 * c + 2, :], pst(("ka", c))[:, :, :])
            for c in range(KH):
                g = ("gt", c)
                wait_mm(g)
                act.activation(r[:, c, :], pst(g)[:, 0, :], ACT.Sigmoid, bias=col("ba", c))
                act.activation(gi[:, c, :], pst(g)[:, 1, :], ACT.Sigmoid, bias=col("bx", c)).then_inc(act_out, 1)
            act.wait_ge(act_out, AI2["gt", KH - 1])
            act.wait_ge(sp_step, T.sp_steps)
            for c in range(KH):
                act.activation(th[:, c, :], r[:, c, :], ACT.Tanh, scale=nsp[:, 5, c:c + 1]).then_inc(decay_ready, 1)
            for c in range(KH):
                act.activation(aa[:, c, :], r[:, c, :], ACT.Exp, scale=nsp[:, 5, c:c + 1])

            def exponentials(h):
                act.wait_ge(nmax_ready, h + 1)
                for i in range(TT):
                    p = sbuf[:, h % 2, SOFF[i]:SOFF[i] + (i + 1) * P]
                    act.activation(p, p, ACT.Exp, bias=nmx[:, 4 * h + i:4 * h + i + 1],
                                   accum_out=rsum[:, 4 * h + i:4 * h + i + 1]).then_inc(exp_done, 1)

            def turned(h):
                for g, js in ((("tA", h), (0, 1)), (("tB", h), (2, 3))):
                    wait_mm(g)
                    for b, j in enumerate(js):
                        last = act.activation(pT[:, j, j * P:SEQ], pst(g)[:, b, j * P:SEQ], ACT.Copy)
                    last.then_inc(act_out, 1)

            def root():
                act.wait_ge(m2_ready, 1)
                act.activation(yr, yr, ACT.Ln).then_inc(logs_ready, 1)
                act.activation(th, th, ACT.Ln, scale=-1.0, bias=ones[:, 0:1]).then_inc(logs_ready, 1)

            def gelu():
                act.wait_ge(rnn_step, 2)
                act.activation(yr, yr, ACT.Exp, scale=0.5).then_inc(root_ready, 1)
                act.wait_ge(vec_out, VI2["xg", 1])
                act.activation(xg, xg, ACT.Gelu_apprx_tanh).then_inc(gelu_ready, 1)

            exponentials(0)
            root()
            exponentials(1)
            gelu()
            for h in range(AH):
                turned(h)
                if h + 2 < AH:
                    exponentials(h + 2)
            act.wait_ge(rnn_step, 4)
            for k in range(KH):
                square("mixed", k, xn)
            for k in range(KH, KD):
                act.wait_ge(vec_out, VI2["at", 2 * (k - KH) + 1])
                square("mixed", k, xn)
            rms(("n", 2), DH, banks=2)
            for k in range(KD):
                act.wait_ge(vec_out, VI2["o", k // 2])
                square("ln2", k, x)
            rms(("n", 3), D)
            for m in range(4):
                copy(("qx", m), qx[:, 2 * m:2 * m + 2, :], pst(("qx", m))[:, :, :], scale=256 ** -0.5)

            def cross_exponentials(h):
                n = 4 * (AH + h)
                act.wait_ge(nmax_ready, AH + h + 1)
                for i in range(TT):
                    last = act.activation(sbuf[:, h % 2, i * MEM:i * MEM + MEM], pflat(("sx", h))[:, i * MEM:i * MEM + MEM], ACT.Exp,
                                          bias=nmx[:, n + i:n + i + 1], accum_out=rsum[:, n + i:n + i + 1])
                last.then_inc(act_out, 1)

            cross_exponentials(0)
            cross_exponentials(1)
            for h in range(XH):
                copy(("tx", h), pT[:, 0:2, :], pst(("tx", h))[:, :, :])
                if h + 2 < XH:
                    cross_exponentials(h + 2)
            for k in range(KD):
                act.wait_ge(vec_out, VI2["xo", k // 2])
                square("ln3", k, x)
            rms(("n", 4), D)
            for i in range(TT):
                copy(("ht", i), T.htok[:, i, :], pflat(("ht", i)))


CAP = 64
PAIRS = NE // 2
EPG = NE // NGRP
FE = 512
KF = FE // P
ROUNDS_MAX = SEQ // CAP

G3 = [("x", 0), ("x", 1), ("st",), ("g", 0), ("g", 1), ("d", 0), ("d", 1), ("y", 0), ("y", 1)] + [("o", n) for n in range(8)]
BANK = {g: n % 8 for n, g in enumerate(G3)}
BANK["o", 7] = 3
ACT_OWNS3 = [("x", 0), ("d", 0), ("d", 1), ("y", 0), ("y", 1)]
GI3 = {g: n for n, g in enumerate(G3)}
AI3 = {g: n + 1 for n, g in enumerate(ACT_OWNS3)}
VI3 = {g: n + 1 for n, g in enumerate(g for g in G3 if g not in ACT_OWNS3)}
NG3, NA3, NV3 = len(G3), len(AI3), len(VI3)


def experts(nc, dram, T, sem, out):
    ctx = ExitStack()
    with ctx:
        def sb(name, shape, dt=F32):
            return ctx.enter_context(nc.sbuf_tensor(name, shape, dt))

        htok, acc, ident, ones, eps, logits = T.htok, T.xtok, T.ident, T.ones, T.eps, T.logits
        weights = [[sb(f"w_{n}{e}", [P, 8 * FE]) for n in ("gate", "up", "down")] for e in range(2)]
        lg = logits[:, :].rearrange("p (i n) -> p i n", i=TT)
        G4 = [P, TT, NGRP]
        G32 = [P, TT, NE]
        iota_g = sb("iota_g", G4)
        iota_e = sb("iota_e", G32)
        slot = sb("slot", [P, TT, CAP])
        before = sb("before", [P, P])
        steps8 = sb("steps8", [P, ROUNDS_MAX - 1])
        gmax, gsum, gidx, m1, m2, i1, w1, w2, e2, den = (sb(n, [P, TT]) for n in
                                                         ("gmax", "gsum", "gidx", "m1", "m2", "i1", "w1", "w2", "e2", "den"))
        ge = sb("ge", G4)
        gone = sb("gone", G4)
        le = sb("le", G32)
        one1 = sb("one1", G32)
        one2 = sb("one2", G32)
        tmp = sb("tmp", G32)
        tmp2 = sb("tmp2", G32)
        chosen = sb("chosen", G32)
        wcomb = sb("wcomb", [P, TT, NE + 2])
        rank = sb("rank", [P, TT, NE + 2])
        cmax = sb("cmax", [P, 1])
        rounds = sb("rounds", [P, 1], mybir.dt.int32)
        sel = sb("sel", [P, TT, 2 * CAP])
        selw = sb("selw", [P, TT, 2 * CAP])
        selT = sb("selT", [P, SEQ])
        xe = sb("xe", [P, KD, 2 * CAP])
        sg = sb("sg", [P, 2, KF, CAP])
        he = sb("he", [P, 2, KF, CAP])
        yT = sb("yT", [P, KD, 2 * CAP])
        ys = sb("ys", [P, D])
        fw = sb("fw", [P, D])
        sqo = sb("sqo", [P, D])
        ssum = sb("ssum", [P, TT])

        w_loaded = [[sem(f"w_loaded{e}{j}") for j in range(3)] for e in range(2)]
        mm_done = sem("mm3_done")
        vec_out = sem("vec3_out")
        act_out = sem("act3_out")
        const_made = sem("const3_made")
        fw_loaded = sem("fw_loaded")
        route_step = sem("route_step")
        group_exp = sem("group_exp")
        pair_exp = sem("pair_exp")
        ranks_done = sem("ranks_done")
        rounds_ready = sem("rounds_ready")
        sel_made = sem("sel_made")
        sel_ready = sem("sel_ready")
        rank_moved = sem("rank_moved")
        silu_done = sem("silu3_done")
        ss_done = sem("ss_done")
        rstd_done = sem("rstd3_done")
        out_ready = sem("out_ready")
        stored = sem("stored")

        def bank(g):
            return T.ps[BANK[g] // 2][:, BANK[g] % 2, :]

        block = ctx.enter_context(nc.Block())

        @block.sync
        def _(sp):
            def load(pair, it):
                for j, (name, last) in enumerate((("eg", "g"), ("eu", "g"), ("ed", "d"))):
                    for e in range(2):
                        sp.wait_ge(mm_done, it * NG3 + GI3[last, e] + 1)
                        k = KF if name == "ed" else KD
                        src = dram[name][bass.ds(pair * 2 + e, 1), :, :].rearrange("a (k p) n -> p (a k) n", p=P)
                        sp.dma_start(weights[e][j][:, :].rearrange("p (k n) -> p k n", k=k), src).then_inc(w_loaded[e][j], 16)

            with sp.Fori(0, PAIRS) as pair:
                load(pair, pair)
            sp.wait_ge(rounds_ready, 1)
            n_rounds = sp.value_load(rounds[0:1, 0:1], min_val=1, max_val=ROUNDS_MAX)
            with sp.If(n_rounds > 1):
                with sp.Fori(1, n_rounds) as rnd:
                    with sp.Fori(0, PAIRS) as pair:
                        load(pair, rnd * PAIRS + pair)
            for i in range(TT):
                sp.wait_ge(out_ready, i + 1)
                sp.dma_start(out[0, i * P:i * P + P, :], acc[:, i, :]).then_inc(stored, 16)
            sp.wait_ge(stored, 16 * TT)

        @block.gpsimd
        def _(pool):
            pool.dma_start(fw[:, :], dram["fw"].partition_broadcast(P)).then_inc(fw_loaded, 16)
            pool.iota(iota_g[:, :, :], pattern=[[0, TT], [1, NGRP]], base=0, channel_multiplier=0,
                      allow_small_or_imprecise_dtypes=True).then_inc(const_made, 1)
            pool.iota(iota_e[:, :, :], pattern=[[0, TT], [1, NE]], base=0, channel_multiplier=0,
                      allow_small_or_imprecise_dtypes=True).then_inc(const_made, 1)
            pool.iota(slot[:, :, :], pattern=[[0, TT], [1, CAP]], base=0, channel_multiplier=0,
                      allow_small_or_imprecise_dtypes=True).then_inc(const_made, 1)
            pool.iota(steps8[:, :], pattern=[[CAP, ROUNDS_MAX - 1]], base=CAP, channel_multiplier=0,
                      allow_small_or_imprecise_dtypes=True).then_inc(const_made, 1)
            pool.memset(wcomb[:, :, NE:], 0.0).then_inc(const_made, 1)
            pool.memset(rank[:, :, NE:], CAP - 1.0).then_inc(const_made, 1)
            pool.memset(before[:, :], 1.0).then_inc(const_made, 1)
            pool.wait_ge(const_made, 7)
            pool.affine_select(out=before[:, :], in_=before[:, :], compare_op=ALU.is_gt, fill=0.0, base=0,
                               pattern=[[1, P]], channel_multiplier=-1).then_inc(const_made, 1)

        @block.vector
        def _(dve):
            dve.sem_inc(vec_out, NV3)
            steps = [0]

            def step(ins):
                steps[0] += 1
                ins.then_inc(route_step, 1)
                dve.wait_ge(route_step, steps[0])

            def over(a, shape):
                return a[:, :].unsqueeze(2).broadcast_to(shape)

            tt, stt, ts = dve.tensor_tensor, dve.scalar_tensor_tensor, dve.tensor_scalar
            dve.wait_ge(const_made, 8)
            step(dve.tensor_reduce(gmax[:, :], lg[:, :, 0:NGRP], AX.X, ALU.max))
            step(tt(ge[:, :, :], lg[:, :, 0:NGRP], over(gmax, G4), ALU.subtract))
            T.route_group = steps[0]
            step(tt(gone[:, :, :], lg[:, :, 0:NGRP], over(gmax, G4), ALU.is_equal))
            step(ts(gone[:, :, :], gone[:, :, :], -100.0, 100.0, ALU.mult, ALU.add))
            step(tt(gone[:, :, :], gone[:, :, :], iota_g[:, :, :], ALU.add))
            step(dve.tensor_reduce(gidx[:, :], gone[:, :, :], AX.X, ALU.min))
            step(tt(gone[:, :, :], iota_g[:, :, :], over(gidx, G4), ALU.is_equal))
            step(ts(gone[:, :, :], gone[:, :, :], 1e30, -1e30, ALU.mult, ALU.add))
            for q in range(NGRP):
                s = slice(q * EPG, q * EPG + EPG)
                step(tt(le[:, :, s], lg[:, :, NGRP + q * EPG:NGRP + q * EPG + EPG],
                        gone[:, :, q:q + 1].broadcast_to([P, TT, EPG]), ALU.add))

            def best(m, one):
                step(dve.tensor_reduce(m[:, :], le[:, :, :], AX.X, ALU.max))
                step(tt(tmp[:, :, :], le[:, :, :], over(m, G32), ALU.is_equal))
                step(ts(tmp[:, :, :], tmp[:, :, :], -100.0, 100.0, ALU.mult, ALU.add))
                step(tt(tmp[:, :, :], tmp[:, :, :], iota_e[:, :, :], ALU.add))
                step(dve.tensor_reduce(i1[:, :], tmp[:, :, :], AX.X, ALU.min))
                step(tt(one[:, :, :], iota_e[:, :, :], over(i1, G32), ALU.is_equal))

            best(m1, one1)
            step(stt(le[:, :, :], one1[:, :, :], -3e30, le[:, :, :], ALU.mult, ALU.add))
            best(m2, one2)
            step(tt(chosen[:, :, :], one1[:, :, :], one2[:, :, :], ALU.add))
            T.route_chosen = steps[0]
            step(tt(m2[:, :], m2[:, :], m1[:, :], ALU.subtract))
            T.route_pair = steps[0]
            dve.wait_ge(group_exp, 1)
            step(dve.tensor_reduce(gsum[:, :], ge[:, :, :], AX.X, ALU.add))
            dve.wait_ge(pair_exp, 1)
            step(ts(den[:, :], e2[:, :], 1.0, None, ALU.add))
            step(tt(den[:, :], den[:, :], gsum[:, :], ALU.mult))
            step(dve.reciprocal(w1[:, :], den[:, :]))
            step(tt(w2[:, :], w1[:, :], e2[:, :], ALU.mult))
            step(tt(tmp[:, :, :], one1[:, :, :], over(w1, G32), ALU.mult))
            step(tt(tmp2[:, :, :], one2[:, :, :], over(w2, G32), ALU.mult))
            step(tt(wcomb[:, :, 0:NE], tmp[:, :, :], tmp2[:, :, :], ALU.add))
            dve.wait_ge(ranks_done, 1)
            step(stt(tmp[:, :, :], T.ps[0][:, 0, 0:TT * NE].rearrange("p (i n) -> p i n", i=TT), 1.0, chosen[:, :, :], ALU.add, ALU.mult))
            step(ts(rank[:, :, 0:NE], tmp[:, :, :], CAP - 1.0, None, ALU.add))
            step(dve.tensor_reduce(cmax[:, :], T.ps[0][:, 1, 0:NE], AX.X, ALU.max))
            step(ts(steps8[:, :], steps8[:, :], cmax[:, 0:1], None, ALU.is_lt))
            step(dve.tensor_reduce(cmax[:, :], steps8[:, :], AX.X, ALU.add))
            dve.tensor_scalar(rounds[:, :], cmax[:, :], 1.0, None, ALU.add).then_inc(rounds_ready, 1)
            dve.wait_ge(rounds_ready, 1)
            n_rounds = dve.value_load(rounds[0:1, 0:1], min_val=1, max_val=ROUNDS_MAX)

            def select(first, count):
                for e in range(2):
                    r = rank[:, :, bass.ds(first + e, 1)].broadcast_to([P, TT, CAP])
                    last = dve.tensor_tensor(sel[:, :, e * CAP:e * CAP + CAP], slot[:, :, :], r, ALU.is_equal)
                last.then_inc(sel_made, 1)
                dve.wait_ge(sel_made, count)
                for e in range(2):
                    w = wcomb[:, :, bass.ds(first + e, 1)].broadcast_to([P, TT, CAP])
                    last = dve.tensor_tensor(selw[:, :, e * CAP:e * CAP + CAP], sel[:, :, e * CAP:e * CAP + CAP], w, ALU.mult)
                last.then_inc(sel_ready, 1)

            with dve.Fori(0, n_rounds) as rnd:
                per = PAIRS + 1
                dve.wait_ge(vec_out, rnd * (PAIRS * NV3) + NV3)
                dve.tensor_scalar(rank[:, :, :], rank[:, :, :], -float(CAP), None, ALU.add).then_inc(rank_moved, 1)
                dve.wait_ge(rank_moved, rnd + 1)
                select(0, rnd * per + 1)
                with dve.Fori(0, PAIRS) as pair:
                    it = rnd * PAIRS + pair

                    def wait_mm(g):
                        dve.wait_ge(mm_done, (it + 1) * NG3 + GI3[g] + 1)

                    wait_mm(("x", 1))
                    dve.tensor_copy(xe[:, 4:8, :], bank(("x", 1)).rearrange("p (k n) -> p k n", k=4)).then_inc(vec_out, 1)
                    wait_mm(("st",))
                    dve.tensor_copy(selT[:, :], bank(("st",))).then_inc(vec_out, 1)
                    for e in range(2):
                        wait_mm(("g", e))
                        dve.wait_ge(silu_done, it * 2 + e + 1)
                        dve.tensor_tensor(he[:, e, :, :], sg[:, e, :, :],
                                          bank(("g", e))[:, KF * CAP:2 * KF * CAP].rearrange("p (f n) -> p f n", f=KF), ALU.mult).then_inc(vec_out, 1)
                        if e == 0:
                            select(pair * 2 + 2, rnd * per + pair + 2)
                    for n in range(8):
                        half, i = n // TT, n % TT
                        wait_mm(("o", n))
                        a = acc[:, i, half * 512:half * 512 + 512]
                        dve.tensor_tensor(a, bank(("o", n)), a, ALU.add).then_inc(vec_out, 1)

            dve.wait_ge(fw_loaded, 16)
            dve.wait_ge(rstd_done, 1)
            for i in range(TT):
                stt(acc[:, i, :], acc[:, i, :], ssum[:, i:i + 1], fw[:, :], ALU.mult, ALU.mult).then_inc(out_ready, 1)

        @block.tensor
        def _(pe):
            pe.sem_inc(mm_done, NG3)
            pe.wait_ge(const_made, 8)
            pe.wait_ge(route_step, T.route_chosen)
            for i in range(TT):
                for j in range(i + 1):
                    pe.matmul(T.ps[0][:, 0, i * NE:i * NE + NE], ones[:, :] if j < i else before[:, :], chosen[:, j, :],
                              start=j == 0, stop=j == i)
            for j in range(TT):
                mm = pe.matmul(T.ps[0][:, 1, 0:NE], ones[:, :], chosen[:, j, :], start=j == 0, stop=j == TT - 1)
            mm.then_inc(ranks_done, 1)
            pe.wait_ge(rounds_ready, 1)
            n_rounds = pe.value_load(rounds[0:1, 0:1], min_val=1, max_val=ROUNDS_MAX)
            with pe.Fori(0, n_rounds) as rnd, pe.Fori(0, PAIRS) as pair:
                it = rnd * PAIRS + pair

                def begin(g):
                    same = [q for q in G3 if BANK[q] == BANK[g]]
                    prev = same[same.index(g) - 1]
                    back = 1 if GI3[prev] < GI3[g] else 0
                    if prev in AI3:
                        pe.wait_ge(act_out, (it + back) * NA3 + AI3[prev])
                    else:
                        pe.wait_ge(vec_out, (it + back) * NV3 + VI3[prev])

                def weight(e, j, k):
                    pe.wait_ge(w_loaded[e][j], (it + 1) * 16)
                    return weights[e][j][:, :].rearrange("p (k n) -> p k n", k=k)

                pe.wait_ge(sel_ready, rnd * (PAIRS + 1) + pair + 1)
                for half in range(2):
                    g = ("x", half)
                    begin(g)
                    for c in range(4):
                        k = half * 4 + c
                        for i in range(TT):
                            mm = pe.matmul(bank(g)[:, c * P:c * P + P], htok[:, i, k * P:k * P + P], sel[:, i, :],
                                           start=i == 0, stop=i == TT - 1)
                    mm.then_inc(mm_done, 1)
                g = ("st",)
                begin(g)
                for i in range(TT):
                    mm = pe.transpose(bank(g)[:, i * P:i * P + P], selw[:, i, :], ident[:, :])
                mm.then_inc(mm_done, 1)
                pe.wait_ge(act_out, (it + 1) * NA3 + AI3["x", 0])
                pe.wait_ge(vec_out, (it + 1) * NV3 + VI3["x", 1])
                for e in range(2):
                    g = ("g", e)
                    begin(g)
                    for j in range(2):
                        w = weight(e, j, KD)
                        for f in range(KF):
                            o = (j * KF + f) * CAP
                            for k in range(KD):
                                mm = pe.matmul(bank(g)[:, o:o + CAP], w[:, k, f * P:f * P + P], xe[:, k, e * CAP:e * CAP + CAP],
                                               start=k == 0, stop=k == KD - 1)
                    mm.then_inc(mm_done, 1)
                for e in range(2):
                    g = ("d", e)
                    begin(g)
                    w = weight(e, 2, KF)
                    pe.wait_ge(vec_out, (it + 1) * NV3 + VI3["g", e])
                    for c in range(KD):
                        for f in range(KF):
                            mm = pe.matmul(bank(g)[:, c * CAP:c * CAP + CAP], w[:, f, c * P:c * P + P], he[:, e, f, :],
                                           start=f == 0, stop=f == KF - 1)
                    mm.then_inc(mm_done, 1)
                pe.wait_ge(act_out, (it + 1) * NA3 + AI3["d", 1])
                for half in range(2):
                    g = ("y", half)
                    begin(g)
                    for c in range(4):
                        mm = pe.transpose(bank(g)[:, c * P:c * P + P], yT[:, half * 4 + c, :], ident[:, :])
                    mm.then_inc(mm_done, 1)
                pe.wait_ge(vec_out, (it + 1) * NV3 + VI3["st",])
                for n in range(8):
                    g = ("o", n)
                    half, i = n // TT, n % TT
                    begin(g)
                    if i == 0:
                        pe.wait_ge(act_out, (it + 1) * NA3 + AI3["y", half])
                    pe.matmul(bank(g), selT[:, i * P:i * P + P], ys[:, half * 512:half * 512 + 512],
                              start=True, stop=True).then_inc(mm_done, 1)

        @block.scalar
        def _(act):
            act.sem_inc(act_out, NA3)
            act.wait_ge(route_step, T.route_group)
            act.activation(ge[:, :, :], ge[:, :, :], ACT.Exp).then_inc(group_exp, 1)
            act.wait_ge(route_step, T.route_pair)
            act.activation(e2[:, :], m2[:, :], ACT.Exp).then_inc(pair_exp, 1)
            act.wait_ge(rounds_ready, 1)
            n_rounds = act.value_load(rounds[0:1, 0:1], min_val=1, max_val=ROUNDS_MAX)
            with act.Fori(0, n_rounds) as rnd, act.Fori(0, PAIRS) as pair:
                it = rnd * PAIRS + pair

                def wait_mm(g):
                    act.wait_ge(mm_done, (it + 1) * NG3 + GI3[g] + 1)

                wait_mm(("x", 0))
                act.activation(xe[:, 0:4, :], bank(("x", 0)).rearrange("p (k n) -> p k n", k=4), ACT.Copy).then_inc(act_out, 1)
                for e in range(2):
                    wait_mm(("g", e))
                    act.activation(sg[:, e, :, :], bank(("g", e))[:, 0:KF * CAP].rearrange("p (f n) -> p f n", f=KF), ACT.Silu).then_inc(silu_done, 1)
                for e in range(2):
                    wait_mm(("d", e))
                    act.activation(yT[:, :, e * CAP:e * CAP + CAP], bank(("d", e)).rearrange("p (c n) -> p c n", c=KD), ACT.Copy).then_inc(act_out, 1)
                for half in range(2):
                    wait_mm(("y", half))
                    act.activation(ys[:, half * 512:half * 512 + 512], bank(("y", half)), ACT.Copy).then_inc(act_out, 1)
            act.wait_ge(vec_out, n_rounds * (PAIRS * NV3) + NV3)
            for i in range(TT):
                last = act.activation(sqo[:, :], acc[:, i, :], ACT.Square, accum_out=ssum[:, i:i + 1])
                last.then_inc(ss_done, 1)
                act.wait_ge(ss_done, i + 1)
            act.activation(ssum[:, :], ssum[:, :], ACT.Ln, bias=eps[:, :], scale=1.0 / D).then_inc(ss_done, 1)
            act.wait_ge(ss_done, TT + 1)
            act.activation(ssum[:, :], ssum[:, :], ACT.Exp, scale=-0.5).then_inc(rstd_done, 1)


def build(nc, dram, out):
    T = Tiles()
    with ExitStack() as ctx:
        def sb(name, shape):
            return ctx.enter_context(nc.sbuf_tensor(name, shape, F32))

        def sem(name):
            return ctx.enter_context(nc.semaphore(name))

        T.hT = sb("hT", [P, KD, L])
        T.ring = sb("ring", [P, RING, PANEL])
        T.ones = sb("ones", [P, P])
        T.ident = sb("ident", [P, P])
        T.eps = sb("eps", [P, 1])
        T.lw = sb("lw", [P, LW])
        T.ps = [ctx.enter_context(nc.psum_tensor(f"ps{i}", [P, 2, 512], F32)) for i in range(NPS)]
        T.logits = sb("logits", [P, TT * NL])
        T.htok = T.ring[:, 0:2, :].rearrange("p a (b n) -> p (a b) n", b=2)
        T.xtok = T.ring[:, 2:4, :].rearrange("p a (b n) -> p (a b) n", b=2)
        T.setup = sem("setup")
        T.N_SETUP = 4
        T.lw_ready = sem("lw_ready")
        with nc.Block() as block:
            @block.gpsimd
            def _(pool):
                pool.memset(T.ones[:, :], 1.0).then_inc(T.setup, 1)
                pool.memset(T.eps[:, :], EPS).then_inc(T.setup, 1)
                pool.memset(T.ident[:, :], 0.0).then_inc(T.setup, 1)
                pool.wait_ge(T.setup, 3)
                pool.affine_select(out=T.ident[:, :], in_=T.ident[:, :], compare_op=ALU.not_equal, fill=1.0,
                                   base=0, pattern=[[-1, P]], channel_multiplier=1).then_inc(T.setup, 1)
        first_block(nc, dram, T, sem)
        second_block(nc, dram, T, sem)
        experts(nc, dram, T, sem, out)


def kernel(**inputs):
    import numpy as np
    import concourse.bacc as bacc
    from concourse.bass_utils import run_bass_kernel_spmd

    a = {k: np.asarray(x) for k, x in inputs.items()}

    def rows(x):
        return x.reshape(-1, P).T

    def cols(*parts):
        return np.concatenate(parts, axis=-1)

    def diag(x):
        n = x.shape[0]
        y = np.zeros((n // 2, P, P), x.dtype)
        y[:, :64, :64], y[:, 64:, 64:] = x[0::2], x[1::2]
        return cols(*y)

    arrays = {}
    arrays["hT"] = np.concatenate([a["meta_tokens"], a["x"][0]], axis=0).T
    w = a["w_in"]
    arrays["win"] = cols(w[..., 1024:1664], w[..., 1664:1728], w[..., 0:256], w[..., 512:768],
                         w[..., 256:512], w[..., 768:1024], w[..., 1728:2240])
    w = a["w_uq"].reshape(LAYERS, QR, HEADS, P + ROPE)
    arrays["wuq"] = cols(w[..., :P].reshape(LAYERS, QR, -1), w[..., P:P + 32].reshape(LAYERS, QR, -1),
                         w[..., P + 32:].reshape(LAYERS, QR, -1))
    w = a["w_ukv"].reshape(LAYERS, KVR, HEADS, 2 * P)
    arrays["wukv"] = cols(w[..., :P].reshape(LAYERS, KVR, -1), w[..., P:].reshape(LAYERS, KVR, -1))
    arrays["wout"] = a["w_out"]
    small = [cols(rows(a["norm_w"][l]), rows(a["pool_scale"][l]), rows(a["q_norm_w"][l]), rows(a["kv_norm_w"][l]),
                  diag(a["fourier_w"][l]), diag(a["pool_w"][l])) for l in range(LAYERS)]
    last = np.zeros_like(small[0])
    last[:, 0:KD] = rows(a["final_norm_w"])
    last[:, LW_VEC:LW_WR] = cols(rows(a["ln1_w_2"]), *(rows(a["conv_w_2"][0, j]) for j in range(CONV)), rows(a["conv_b_2"]), rows(a["rnn_ba_2"]),
                         rows(a["rnn_bx_2"]), rows(a["rnn_lambda_2"]), rows(a["gn_rnn_w_2"]), rows(a["gn_att_w_2"]), rows(a["ln2_w_2"]),
                         rows(a["mem_norm_w_2"]), rows(a["ln3_w_2"]))
    last[:, LW_WR:LW_RB] = cols(a["router_group_w_2"][0], *a["router_expert_w_2"][0]).reshape(KD, P, NL).transpose(1, 0, 2).reshape(P, -1)
    last[:, LW_RB:LW_RB + TT * NL] = np.tile(cols(a["router_group_b_2"][0], *a["router_expert_b_2"][0]), TT)
    arrays["lw"] = np.stack(small + [last])

    arrays["memT"] = a["mem_2"][0].T
    for name, source in (("xk", "xk_w_2"), ("xv", "xv_w_2"), ("xq", "xq_w_2"), ("xo", "xo_w_2"), ("win2", "w_in_2"), ("wout2", "w_out_2")):
        arrays[name] = a[source][0]
    arrays["wab"] = cols(diag(a["rnn_wa_2"][0]), diag(a["rnn_wx_2"][0])).reshape(P, 2 * KH, P)
    distance = np.arange(P)[:, None] + (SEQ - P) - np.arange(SEQ)[None, :]
    arrays["bias"] = a["rel_bias_2"][0][:, np.clip(distance, -P, P) + P]

    arrays["eg"], arrays["eu"], arrays["ed"] = a["expert_gate_w_2"][0], a["expert_up_w_2"][0], a["expert_down_w_2"][0]
    arrays["fw"] = a["final_norm_w_2"]

    n = np.arange(L)
    angle = 2 * np.pi * ((n[:, None] * n[None, :]) % L) / L
    tables = np.zeros((4, NT * P, LH))
    for half in range(2):
        tables[2 * half, :L] = np.cos(angle)[:, half * LH:half * LH + LH]
        tables[2 * half + 1, :L] = np.sin(angle)[:, half * LH:half * LH + LH]
    arrays["dft"] = tables.astype(np.float32)
    c = np.arange(64)
    angle = 2 * np.pi * ((c[:, None] * c[None, :]) % 64) / 64
    both = np.zeros((P, 2, P))
    for b in range(2):
        s = slice(64 * b, 64 * b + 64)
        both[s, 0, s] = np.cos(angle) / math.sqrt(L * 64)
        both[s, 1, s] = -np.sin(angle) / math.sqrt(L * 64)
    arrays["cdsd"] = both.astype(np.float32)
    inv = (1.0 / (np.float32(10000.0) ** (np.arange(0, ROPE, 2, dtype=np.float32) / np.float32(ROPE)))).astype(np.float32)
    angle = n.astype(np.float32)[:, None] * inv[None, :]
    arrays["rope"] = np.stack([np.tile(np.cos(angle).T, (4, 1)), np.tile(np.sin(angle).T, (4, 1))], axis=1).astype(np.float32)
    count = np.zeros((P, 2, L))
    for g, win in enumerate((2, 4, 8, 16)):
        have = np.clip(n + win // 2, 0, L) - np.clip(n - win // 2, 0, L)
        count[64 * (g % 2):64 * (g % 2) + 64, g // 2] = 1.0 / have
    arrays["cnt"] = count.astype(np.float32)

    nc = bacc.Bacc("TRN2", target_bir_lowering=False, num_devices=1)
    dram, fed = {}, {}
    for name, x in arrays.items():
        fed[f"in_{name}"] = np.ascontiguousarray(x)
        dram[name] = nc.dram_tensor(f"in_{name}", x.shape, mybir.dt.from_np(x.dtype), kind="ExternalInput").ap()
    out = nc.dram_tensor("out_0", (1, SEQ, D), F32, kind="ExternalOutput").ap()
    build(nc, dram, out)
    r = run_bass_kernel_spmd(nc, [fed], core_ids=[0])
    return r.results[0]["out_0"]
```

```python
import math
from contextlib import ExitStack

import concourse.bass as bass
from concourse import mybir

F32 = mybir.dt.float32
ALU = mybir.AluOpType
ACT = mybir.ActivationFunctionType
AX = mybir.AxisListType

P = 128
D = 1024
KD = D // P
SEQ = 512
META = 16
L = SEQ + META
LH = L // 2
LAYERS = 2
LT = [(i * P, min(P, L - i * P)) for i in range(-(-L // P))]
NT = len(LT)
HEADS = 4
QR, KVR = 384, 256
KQ, KKV = QR // P, KVR // P
ROPE = 64
EPS = 1e-6
SCALE1 = (P + ROPE) ** -0.5

RING = 4
PANEL = 2048
PAIR = 1024
NPS = 4

def first_groups():
    g = [("u", 0), ("u", 1), ("rs", 0), ("u", 2), ("u", 3), ("u", 4), ("kr", 0), ("fi", 0), ("fi", 1),
         ("rs", 1), ("rs", 2), ("pi", 0), ("pi", 1)]
    g += [("ga", m) for m in range(8)]
    g += [("q", h) for h in range(HEADS)] + [("qr", 0), ("qr", 1)]
    g += [("kn", h) for h in range(HEADS)] + [("v", i) for i in range(3)]
    g += [("ab", 0)] + [("pq", i) for i in range(NT)] + [("yf", 0), ("yf", 1), ("yp", 0), ("yp", 1)]
    def s(h): return [("s", h, i) for i in range(NT)]
    def t(h): return [("t", h, j) for j in range(NT)]
    g += s(0) + s(1) + t(0) + s(2) + [("a", 0)] + t(1) + s(3) + [("a", 1)] + t(2) + [("a", 2)] + t(3) + [("a", 3)]
    g += [("o", m) for m in range(8)]
    return g

G1 = first_groups()
assert len(G1) % NPS == 0
ACT_OWNS1 = ("rs", "q", "kn", "v", "pq", "s", "t")
V1 = [g for g in G1 if g[0] not in ACT_OWNS1]
A1 = [g for g in G1 if g[0] in ACT_OWNS1]
GI1 = {g: n for n, g in enumerate(G1)}
VI1 = {g: n + 1 for n, g in enumerate(V1)}
AI1 = {g: n + 1 for n, g in enumerate(A1)}
NG1, NV1, NA1 = len(G1), len(V1), len(A1)

W1 = ([("win", i) for i in range(9)] + [("wuq", 0), ("wuq", 1), ("wukv", 0)]
      + [("dft", i) for i in range(4)] + [("wout", i) for i in range(4)])
NW1 = len(W1)
WI1 = {w: n for n, w in enumerate(W1)}
assert NW1 % RING == 0
W1_LAST = ([("u", 1), ("u", 3), ("kr", 0), ("fi", 1), ("pi", 1), ("ga", 1), ("ga", 3), ("ga", 5), ("ga", 7)]
           + [("q", 3), ("qr", 1), ("v", 2)] + [("yf", 1)] * 4 + [("o", 1), ("o", 3), ("o", 5), ("o", 7)])
WIN_COLS = [(0, 256), (256, 256), (512, 192)] + [(704 + 256 * i, 256) for i in range(6)]
LW_NORM, LW_POOL, LW_Q, LW_KV, LW_FW, LW_PW = 0, 8, 10, 13, 15, 271
LW = 527


MEM = 256
DH = 512
KH = DH // P
AH = 8
XH = 4
TT = SEQ // P
NE, NGRP = 32, 4
NL = NGRP + NE
CONV = 4


def second_groups():
    g = [("kx", 0), ("n", 1), ("kx", 1)]
    g += [(n, c) for n in ("xr", "xg", "qa", "ka", "va") for c in range(2)]
    g += [("gt", c) for c in range(KH)]
    def s(h): return [("sA", h), ("sB", h)]
    def t(h): return [("tA", h), ("tB", h)]
    g += s(0) + [("kx", 2)] + s(1) + [("kx", 3)]
    for h in range(AH):
        g += t(h) + (s(h + 2) if h + 2 < AH else []) + [("at", h)]
    g += [("n", 2), ("vx", 0)] + [("o", m) for m in range(4)] + [("vx", 1), ("n", 3), ("vx", 2)]
    g += [("qx", m) for m in range(4)] + [("sx", 0), ("sx", 1)]
    for h in range(XH):
        g += [("tx", h)] + ([("sx", h + 2)] if h + 2 < XH else []) + [("ax", h)]
    g += [("xo", m) for m in range(4)] + [("n", 4), ("lg",)]
    g += [("ht", i) for i in range(TT)] + [("xt", i) for i in range(TT)]
    return g


G2 = second_groups()
ACT_OWNS2 = ("n", "kx", "qa", "ka", "gt", "tA", "tB", "qx", "sx", "tx", "ht")
GI2 = {g: n for n, g in enumerate(G2)}
VI2 = {g: n + 1 for n, g in enumerate(g for g in G2 if g[0] not in ACT_OWNS2)}
AI2 = {g: n + 1 for n, g in enumerate(g for g in G2 if g[0] in ACT_OWNS2)}
W2 = ([("xk", 0), ("xk", 1)] + [("win2", i) for i in range(10)] + [("xk", 2), ("xk", 3), ("xv", 0), ("xv", 1)]
      + [("wout2", i) for i in range(4)] + [("xv", 2), ("xv", 3)] + [("xq", i) for i in range(4)] + [("xo", i) for i in range(4)])
WI2 = {w: n for n, w in enumerate(W2)}
W2_LAST = ([("kx", 0), ("kx", 1)]
           + [(n, c) for n in ("xr", "xg", "qa", "ka") for c in range(2)] + [("va", 1)] * 2
           + [("kx", 2), ("kx", 3), ("vx", 0), ("vx", 0)] + [("o", m) for m in range(4)] + [("vx", 1), ("vx", 2)] + [("qx", m) for m in range(4)] + [("xo", m) for m in range(4)])
V2 = {}
for _name, _n in (("ln1", KD), ("cw", CONV * KH), ("cb", KH), ("ba", KH), ("bx", KH), ("lam", KH), ("gnr", KH), ("gna", KH),
                  ("ln2", KD), ("mem", KD), ("ln3", KD)):
    V2[_name] = sum(n for _, n in V2.values()), _n
NV2 = sum(n for _, n in V2.values())
LW_VEC = KD
LW_WR = LW_VEC + NV2
LW_RB = LW_WR + KD * NL
assert LW_RB + TT * NL <= LW
SOFF = {3: 0, 2: 512, 1: 896, 0: 1152}
SBW = 1280
NORMS = ["first", "ln1", "mixed", "ln2", "ln3"]
TINY = 1e-18


def panel_view(ring, n):
    return ring[:, n % RING, :].rearrange("p (k n) -> p k n", k=KD)


def panel_source(dram, name, i):
    return dram[name][:, 256 * i:256 * i + 256].rearrange("(k p) n -> p k n", p=P)


class Tiles:
    pass


def first_block(nc, dram, T, sem):
    ctx = ExitStack()
    with ctx:
        def sb(name, shape):
            return ctx.enter_context(nc.sbuf_tensor(name, shape, F32))

        hT, ring, ones, ident, eps, lw, ps = T.hT, T.ring, T.ones, T.ident, T.eps, T.lw, T.ps
        xw = sb("xw", [P, KD, L])
        mix = xw
        gate = sb("gate", [P, 8, L])
        sq = gate
        rstd = T.rstd
        cq = sb("cq", [P, KQ + KKV, L])
        krE = sb("krE", [P, L])
        krO = sb("krO", [P, L])
        rt = sb("rt", [P, 4, L])
        qn, kn = T.qn, T.kn
        qr = sb("qr", [P, 2, L])
        v = sb("v", [P, 6, HEADS * P])
        ab = sb("ab", [P, 2, 256])
        pq = sb("pq", [P, NT, 2, 256])
        PW = L + 32
        pin = sb("pin", [P, 2, PW])
        rope = sb("rope", [P, 2, L])
        cnt = sb("cnt", [P, 2, L])
        cdsd = sb("cdsd", [P, 2, P])
        pbuf = sb("pbuf", [P, 2 * NT * L])
        probs = pbuf[:, :].rearrange("p (b i n) -> p b i n", b=2, i=NT)
        s2 = pbuf[:, 0:2 * PW].rearrange("p (c n) -> p c n", c=2)
        s4 = pbuf[:, 2 * PW:4 * PW].rearrange("p (c n) -> p c n", c=2)
        s8 = pbuf[:, 4 * PW:5 * PW]
        pr = pbuf[:, 5 * PW:5 * PW + 2 * L].rearrange("p (c n) -> p c n", c=2)
        fin = pbuf[:, 5 * PW + 2 * L:5 * PW + 4 * L].rearrange("p (c n) -> p c n", c=2)
        pT = sb("pT", [P, NT, L])
        T.mem_sq = pT[:, :, :].rearrange("p j n -> p (j n)")[:, 0:KD * MEM].rearrange("p (k n) -> p k n", k=KD)
        nmax = sb("nmax", [P, HEADS * NT])
        rsum = sb("rsum", [P, HEADS * NT])
        rinv = sb("rinv", [P, HEADS * NT])
        qws = sb("qws", [P, KQ])

        mm_done = sem("mm_done")
        vec_out = sem("vec_out")
        act_out = sem("act_out")
        w_ready = T.w_ready
        lw_ready = T.lw_ready
        h_loaded = [sem(f"h_loaded{k}") for k in range(KD // 2)]
        const_ready = sem("const_ready")
        zeroed = sem("zeroed")
        sq_ready = sem("sq_ready")
        rstd_ready = sem("rstd_ready")
        xw_ready = sem("xw_ready")
        cn_ready = sem("cn_ready")
        k_step = sem("k_step")
        kr_ready = sem("kr_ready")
        qr_ready = sem("qr_ready")
        qws_ready = sem("qws_ready")
        pool_step = sem("pool_step")
        silu_done = sem("silu_done")
        max_ready = sem("max_ready")
        inv_ready = sem("inv_ready")
        probs_ready = sem("probs_ready")

        NSQ = KD + KQ + KKV
        NPOOL = 9
        NEXP = HEADS * NT

        def pst(g):
            return ps[GI1[g] % NPS]

        def phalf(g, p0=0, p1=P):
            return pst(g)[p0:p1, :, 0:LH]

        def pflat(g):
            return pst(g)[:, :, :].rearrange("p a n -> p (a n)")

        def two(ap):
            return ap.rearrange("p (a n) -> p a n", a=2)

        block = ctx.enter_context(nc.Block())

        @block.sync
        def _(sp):
            for k in range(KD // 2):
                sp.dma_start(hT[:, 2 * k:2 * k + 2, :], dram["hT"][2 * k * P:2 * (k + 1) * P].rearrange("(k p) n -> p k n", p=P)
                             ).then_inc(h_loaded[k], 16)
            with sp.Fori(0, LAYERS) as layer:
                for n, (name, i) in enumerate(W1):
                    slot = ring[:, n % RING, :]
                    if n < RING:
                        sp.wait_ge(mm_done, layer * NG1 + GI1[W1_LAST[n - RING]] + 1)
                    else:
                        sp.wait_ge(mm_done, (layer + 1) * NG1 + GI1[W1_LAST[n - RING]] + 1)
                    if name == "dft":
                        src = dram["dft"][i].rearrange("(k p) n -> p k n", p=P)
                        dst = slot[:, 0:NT * LH].rearrange("p (k n) -> p k n", k=NT)
                    else:
                        k = {"win": KD, "wuq": KQ, "wukv": KKV, "wout": KD}[name]
                        c0, c = {"win": WIN_COLS, "wuq": [(0, 512), (512, 256)], "wukv": [(0, 1024)],
                                 "wout": [(256 * m, 256) for m in range(4)]}[name][i]
                        src = dram[name][bass.ds(layer, 1), :, c0:c0 + c].rearrange("a (k p) n -> p (a k) n", p=P)
                        dst = slot[:, 0:k * c].rearrange("p (k n) -> p k n", k=k)
                    sp.dma_start(dst, src).then_inc(w_ready[n % RING], 16)
            sp.wait_ge(mm_done, LAYERS * NG1 + GI1["s", HEADS - 1, NT - 1] + 1)
            sp.dma_start(T.memT, dram["memT"].rearrange("(k p) n -> p k n", p=P)).then_inc(T.mem_loaded, 16)
            for n, (name, i) in enumerate(W2[:RING]):
                sp.wait_ge(mm_done, LAYERS * NG1 + GI1[W1_LAST[n - RING]] + 1)
                sp.dma_start(panel_view(ring, n), panel_source(dram, name, i)).then_inc(w_ready[n % RING], 16)

        @block.gpsimd
        def _(pool):
            pool.dma_start(lw[:, :], dram["lw"][0]).then_inc(lw_ready, 16)
            pool.wait_ge(h_loaded[-1], 16)
            pool.dma_start(rope[:, :, :], dram["rope"]).then_inc(const_ready, 16)
            pool.dma_start(cnt[:, :, :], dram["cnt"]).then_inc(const_ready, 16)
            pool.dma_start(cdsd[:, :, :], dram["cdsd"]).then_inc(const_ready, 16)
            pool.memset(krE[:, :], 0.0).then_inc(zeroed, 1)
            pool.memset(krO[:, :], 0.0).then_inc(zeroed, 1)
            pool.memset(pin[:, :, 0:16], 0.0).then_inc(zeroed, 1)
            pool.memset(pin[:, :, 16 + L:PW], 0.0).then_inc(zeroed, 1)
            pool.wait_ge(zeroed, 4)
            pool.wait_ge(const_ready, 48)
            with pool.Fori(0, LAYERS) as layer:
                W = slice(16, 16 + L)

                def step(n):
                    pool.wait_ge(pool_step, layer * NPOOL + n)

                pool.wait_ge(vec_out, (layer + 1) * NV1 + VI1["pi", 1])
                pool.tensor_tensor(s2[:, :, 1:PW], pin[:, :, 1:PW], pin[:, :, 0:PW - 1], ALU.add).then_inc(pool_step, 1)
                step(1)
                pool.tensor_tensor(s4[:, :, 2:PW - 1], s2[:, :, 3:PW], s2[:, :, 1:PW - 2], ALU.add).then_inc(pool_step, 1)
                step(2)
                pool.tensor_tensor(s8[:, 4:PW - 3], s4[:, 1, 6:PW - 1], s4[:, 1, 2:PW - 5], ALU.add).then_inc(pool_step, 1)
                step(3)
                pool.tensor_tensor(pr[64:128, 1, :], s8[64:128, 20:20 + L], s8[64:128, 12:12 + L], ALU.add).then_inc(pool_step, 1)
                step(4)
                pool.tensor_tensor(pr[0:64, 0, :], s2[0:64, 0, W], cnt[0:64, 0, :], ALU.mult).then_inc(pool_step, 1)
                step(5)
                pool.tensor_tensor(pr[64:128, 0, :], s4[64:128, 0, W], cnt[64:128, 0, :], ALU.mult).then_inc(pool_step, 1)
                step(6)
                pool.tensor_tensor(pr[0:64, 1, :], s8[0:64, W], cnt[0:64, 1, :], ALU.mult).then_inc(pool_step, 1)
                step(7)
                pool.tensor_tensor(pr[64:128, 1, :], pr[64:128, 1, :], cnt[64:128, 1, :], ALU.mult).then_inc(pool_step, 1)
                step(8)
                pool.tensor_tensor(pr[:, :, :], pr[:, :, :], pin[:, :, W], ALU.subtract).then_inc(pool_step, 1)
                pool.wait_ge(vec_out, (layer + 1) * NV1 + VI1["yp", 1])
                pool.dma_start(lw[:, :], dram["lw"][bass.ds(layer + 1, 1), :, :].rearrange("a p n -> (a p) n")).then_inc(lw_ready, 16)

        @block.tensor
        def _(pe):
            pe.sem_inc(mm_done, NG1)
            pe.wait_ge(T.setup, T.N_SETUP)
            with pe.Fori(0, LAYERS) as layer:

                def begin(g):
                    prev = G1[(GI1[g] - NPS) % NG1]
                    s, idx, per = (act_out, AI1, NA1) if prev in AI1 else (vec_out, VI1, NV1)
                    pe.wait_ge(s, (layer + (0 if GI1[g] < NPS else 1)) * per + idx[prev])

                def panel(name, i):
                    n = WI1[name, i]
                    pe.wait_ge(w_ready[n % RING], (layer * (NW1 // RING) + n // RING + 1) * 16)
                    return ring[:, n % RING, :]

                def vec(g):
                    pe.wait_ge(vec_out, (layer + 1) * NV1 + VI1[g])

                def act(g):
                    pe.wait_ge(act_out, (layer + 1) * NA1 + AI1[g])

                def project(g, w, k, rhs, m=P, chunk_ready=False):
                    begin(g)
                    for c in range(k):
                        if chunk_ready:
                            pe.wait_ge(xw_ready, layer * KD + c + 1)
                        for a in range(2):
                            mm = pe.matmul(pst(g)[0:m, a, 0:LH], w[:, c, :], rhs[:, c, a * LH:a * LH + LH],
                                           start=c == 0, stop=c == k - 1)
                    mm.then_inc(mm_done, 1)

                def sums(g, c0, k, ready):
                    begin(g)
                    for c in range(k):
                        pe.wait_ge(sq_ready, layer * NSQ + ready + c)
                        for a in range(2):
                            mm = pe.matmul(pst(g)[:, a, 0:LH], ones[:, :], sq[:, c0 + c, a * LH:a * LH + LH],
                                           start=c == 0, stop=c == k - 1)
                    mm.then_inc(mm_done, 1)

                chunks = [("u", 0), ("u", 1), ("u", 2), ("u", 3), ("u", 4), ("kr", 0), ("fi", 0), ("fi", 1),
                          ("pi", 0), ("pi", 1)] + [("ga", m) for m in range(8)]
                for n, g in enumerate(chunks):
                    width = WIN_COLS[n // 2][1]
                    w = panel("win", n // 2)[:, 0:KD * width].rearrange("p (k n) -> p k n", k=KD)
                    m = 64 if g[0] == "kr" else P
                    project(g, w[:, :, n % 2 * P:n % 2 * P + m], KD, xw, m, chunk_ready=n == 0)
                    if g == ("u", 1):
                        sums(("rs", 0), 0, KD, 1)
                    if g == ("fi", 1):
                        sums(("rs", 1), 0, KQ, 1 + KD)
                        sums(("rs", 2), KQ, KKV, 1 + KD + KQ)

                pe.wait_ge(cn_ready, layer * (KQ + KKV) + KQ + KKV)
                w = panel("wuq", 0)[:, 0:KQ * 512].rearrange("p (k n) -> p k n", k=KQ)
                for h in range(HEADS):
                    project(("q", h), w[:, :, h * P:h * P + P], KQ, cq)
                w = panel("wuq", 1)[:, 0:KQ * 256].rearrange("p (k n) -> p k n", k=KQ)
                for c in range(2):
                    project(("qr", c), w[:, :, c * P:c * P + P], KQ, cq)
                w = panel("wukv", 0).rearrange("p (k n) -> p k n", k=KKV)
                for h in range(HEADS):
                    project(("kn", h), w[:, :, h * P:h * P + P], KKV, cq[:, KQ:, :])
                for g in range(3):
                    begin(("v", g))
                    for b, (t0, m) in enumerate(LT[2 * g:2 * g + 2]):
                        for c in range(KKV):
                            mm = pe.matmul(pst(("v", g))[0:m, b, :], cq[:, KQ + c, t0:t0 + m], w[:, c, 512:1024],
                                           start=c == 0, stop=c == KKV - 1)
                    mm.then_inc(mm_done, 1)

                begin(("ab", 0))
                pe.wait_ge(lw_ready, layer * 16 + 16)
                pe.wait_ge(const_ready, 48)
                for c in range(2):
                    for f in range(2):
                        mm = pe.matmul(pst(("ab", 0))[:, c, f * P:f * P + P], cdsd[:, f, :],
                                       lw[:, LW_FW + c * P:LW_FW + c * P + P], start=True, stop=True)
                mm.then_inc(mm_done, 1)
                vec(("ab", 0))
                for i, (t0, m) in enumerate(LT):
                    begin(("pq", i))
                    for c in range(2):
                        mm = pe.matmul(pst(("pq", i))[0:m, c, 0:256], fin[:, c, t0:t0 + m], ab[:, c, :],
                                       start=True, stop=True)
                    mm.then_inc(mm_done, 1)
                act(("pq", NT - 1))
                begin(("yf", 0))
                begin(("yf", 1))
                for a in range(2):
                    for f in range(2):
                        tab = panel("dft", 2 * a + f)[:, 0:NT * LH].rearrange("p (k n) -> p k n", k=NT)
                        for c in range(2):
                            for i, (t0, m) in enumerate(LT):
                                mm = pe.matmul(pst(("yf", c))[:, a, 0:LH], pq[0:m, i, c, f * P:f * P + P],
                                               tab[0:m, i, :], start=f == 0 and i == 0, stop=f == 1 and i == NT - 1)
                            if a == 1 and f == 1:
                                mm.then_inc(mm_done, 1)

                pe.wait_ge(pool_step, layer * NPOOL + NPOOL)
                for c in range(2):
                    g = ("yp", c)
                    begin(g)
                    for a in range(2):
                        mm = pe.matmul(pst(g)[:, a, 0:LH], lw[:, LW_PW + c * P:LW_PW + c * P + P],
                                       pr[:, c, a * LH:a * LH + LH], start=True, stop=True)
                    mm.then_inc(mm_done, 1)

                def scores(h):
                    kr = krO if h % 2 else krE
                    for i, (t0, m) in enumerate(LT):
                        g = ("s", h, i)
                        begin(g)
                        for a in range(2):
                            keys = slice(a * LH, a * LH + LH)
                            pe.matmul(pst(g)[0:m, a, 0:LH], qn[:, h, t0:t0 + m], kn[:, h, keys], start=True, stop=False)
                            mm = pe.matmul(pst(g)[0:m, a, 0:LH], qr[:, h // 2, t0:t0 + m], kr[:, keys], start=False, stop=True)
                        mm.then_inc(mm_done, 1)

                def turn(h):
                    pe.wait_ge(probs_ready, layer * NEXP + h * NT + NT)
                    for j, (k0, kj) in enumerate(LT):
                        g = ("t", h, j)
                        begin(g)
                        for i, (t0, m) in enumerate(LT):
                            mm = pe.transpose(pflat(g)[0:kj, t0:t0 + m], probs[0:m, h % 2, i, k0:k0 + kj], ident[0:m, 0:m])
                        mm.then_inc(mm_done, 1)

                def attend(h):
                    g = ("a", h)
                    begin(g)
                    act(("t", h, NT - 1))
                    for j, (k0, kj) in enumerate(LT):
                        for a in range(2):
                            mm = pe.matmul(pst(g)[:, a, 0:LH], v[0:kj, j, h * P:h * P + P], pT[0:kj, j, a * LH:a * LH + LH],
                                           start=j == 0, stop=j == NT - 1)
                    mm.then_inc(mm_done, 1)

                act(("v", 2))
                pe.wait_ge(kr_ready, layer + 1)
                pe.wait_ge(qr_ready, layer + 1)
                scores(0)
                scores(1)
                turn(0)
                scores(2)
                attend(0)
                turn(1)
                scores(3)
                attend(1)
                turn(2)
                attend(2)
                turn(3)
                attend(3)

                vec(("a", HEADS - 1))
                for m in range(KD):
                    w = panel("wout", m // 2).rearrange("p (k n) -> p k n", k=KD)
                    project(("o", m), w[:, :, m % 2 * P:m % 2 * P + P], KD, mix)

            pe.wait_ge(vec_out, LAYERS * NV1 + VI1["o", 4])
            for c in range(KD):
                pe.wait_ge(sq_ready, LAYERS * NSQ + c + 1)
                mm = pe.matmul(ps[0][:, 0, 0:MEM], ones[:, :], T.mem_sq[:, c, :], start=c == 0, stop=c == KD - 1)
            mm.then_inc(mm_done, 1)
            pe.wait_ge(vec_out, LAYERS * NV1 + VI1["o", 5])
            for c in range(KD):
                pe.wait_ge(sq_ready, LAYERS * NSQ + KD + c + 1)
                for a in range(2):
                    mm = pe.matmul(ps[1][:, a, 0:LH], ones[:, :], sq[:, c, a * LH:a * LH + LH], start=c == 0, stop=c == KD - 1)
            mm.then_inc(mm_done, 1)

        @block.vector
        def _(dve):
            dve.sem_inc(vec_out, NV1)
            with dve.Fori(0, LAYERS) as layer:

                def wait_mm(g):
                    dve.wait_ge(mm_done, (layer + 1) * NG1 + GI1[g] + 1)

                def wait_own(g):
                    dve.wait_ge(vec_out, (layer + 1) * NV1 + VI1[g])

                def normed(g, out, r):
                    wait_mm(g)
                    dve.tensor_tensor(two(out), phalf(g), two(rstd[:, r, :]), ALU.mult).then_inc(vec_out, 1)

                dve.wait_ge(vec_out, (layer + 1) * NV1)
                dve.wait_ge(lw_ready, layer * 16 + 16)
                for k in range(KD):
                    dve.wait_ge(h_loaded[k // 2], 16)
                    dve.tensor_scalar(xw[:, k, :], hT[:, k, :], lw[:, LW_NORM + k:LW_NORM + k + 1], None, ALU.mult).then_inc(xw_ready, 1)
                dve.tensor_scalar(qws[:, :], lw[:, LW_Q:LW_Q + KQ], SCALE1, None, ALU.mult).then_inc(qws_ready, 1)
                dve.wait_ge(rstd_ready, layer * 3 + 1)
                for k in range(5):
                    normed(("u", k), cq[:, k, :], 0)

                dve.wait_ge(const_ready, 48)
                dve.wait_ge(zeroed, 4)
                g = ("kr", 0)
                wait_mm(g)
                dve.tensor_tensor(two(rt[0:32, 0, :]), phalf(g, 0, 32), two(rstd[0:32, 0, :]), ALU.mult)
                dve.tensor_tensor(two(rt[0:32, 1, :]), phalf(g, 32, 64), two(rstd[32:64, 0, :]), ALU.mult).then_inc(vec_out, 1)
                wait_own(g)
                dve.tensor_tensor(rt[0:32, 2, :], rt[0:32, 0, :], rope[0:32, 0, :], ALU.mult)
                dve.tensor_tensor(rt[0:32, 3, :], rt[0:32, 1, :], rope[0:32, 1, :], ALU.mult).then_inc(k_step, 1)
                dve.wait_ge(k_step, layer * 3 + 1)
                dve.tensor_tensor(krE[0:32, :], rt[0:32, 2, :], rt[0:32, 3, :], ALU.subtract)
                dve.tensor_tensor(krO[64:96, :], rt[0:32, 2, :], rt[0:32, 3, :], ALU.subtract).then_inc(k_step, 1)
                dve.wait_ge(k_step, layer * 3 + 2)
                dve.tensor_tensor(rt[0:32, 2, :], rt[0:32, 1, :], rope[0:32, 0, :], ALU.mult)
                dve.tensor_tensor(rt[0:32, 3, :], rt[0:32, 0, :], rope[0:32, 1, :], ALU.mult).then_inc(k_step, 1)
                dve.wait_ge(k_step, layer * 3 + 3)
                dve.tensor_tensor(krE[32:64, :], rt[0:32, 2, :], rt[0:32, 3, :], ALU.add)
                dve.tensor_tensor(krO[96:128, :], rt[0:32, 2, :], rt[0:32, 3, :], ALU.add).then_inc(kr_ready, 1)

                for c in range(2):
                    normed(("fi", c), fin[:, c, :], 0)
                for c in range(2):
                    normed(("pi", c), pin[:, c, 16:16 + L], 0)

                dve.wait_ge(qws_ready, layer + 1)
                dve.wait_ge(rstd_ready, layer * 3 + 2)
                for k in range(KQ):
                    dve.scalar_tensor_tensor(cq[:, k, :], cq[:, k, :], qws[:, k:k + 1], rstd[:, 1, :], ALU.mult, ALU.mult).then_inc(cn_ready, 1)
                dve.wait_ge(rstd_ready, layer * 3 + 3)
                for k in range(KKV):
                    dve.scalar_tensor_tensor(cq[:, KQ + k, :], cq[:, KQ + k, :], lw[:, LW_KV + k:LW_KV + k + 1], rstd[:, 2, :],
                                             ALU.mult, ALU.mult).then_inc(cn_ready, 1)
                for m in range(8):
                    normed(("ga", m), gate[:, m, :], 0)

                for c, order in ((0, (0, 1)), (1, (1, 0))):
                    g = ("qr", c)
                    wait_mm(g)
                    dve.tensor_tensor(two(rt[:, 2 * c, :]), phalf(g), two(rope[:, order[0], :]), ALU.mult)
                    dve.tensor_tensor(two(rt[:, 2 * c + 1, :]), phalf(g), two(rope[:, order[1], :]), ALU.mult).then_inc(vec_out, 1)
                wait_own(("qr", 1))
                for h in range(HEADS):
                    src, to = slice(32 * h, 32 * h + 32), 64 * (h % 2)
                    dve.tensor_tensor(qr[to:to + 32, h // 2, :], rt[src, 0, :], rt[src, 2, :], ALU.subtract)
                    last = dve.tensor_tensor(qr[to + 32:to + 64, h // 2, :], rt[src, 1, :], rt[src, 3, :], ALU.add)
                last.then_inc(qr_ready, 1)

                wait_mm(("ab", 0))
                dve.tensor_copy(ab[:, :, :], pst(("ab", 0))[:, :, 0:256]).then_inc(vec_out, 1)
                for c in range(2):
                    g = ("yf", c)
                    wait_mm(g)
                    dve.wait_ge(silu_done, layer * 8 + c + 1)
                    dve.tensor_tensor(two(mix[:, c, :]), phalf(g), two(gate[:, c, :]), ALU.mult).then_inc(vec_out, 1)
                for c in range(2):
                    g = ("yp", c)
                    wait_mm(g)
                    dve.wait_ge(silu_done, layer * 8 + c + 3)
                    dve.scalar_tensor_tensor(two(mix[:, 2 + c, :]), phalf(g), lw[:, LW_POOL + c:LW_POOL + c + 1], two(gate[:, 2 + c, :]),
                                             ALU.mult, ALU.mult).then_inc(vec_out, 1)
                dve.wait_ge(silu_done, layer * 8 + 8)

                def maximum(h, i):
                    g, m, n = ("s", h, i), LT[i][1], h * NT + i
                    wait_mm(g)
                    dve.tensor_reduce(nmax[0:m, n:n + 1], phalf(g, 0, m), AX.XY, ALU.max, negate=True).then_inc(max_ready, 1)

                def normalise(h, i):
                    m, n = LT[i][1], h * NT + i
                    dve.wait_ge(act_out, (layer + 1) * NA1 + AI1["s", h, i])
                    dve.reciprocal(rinv[0:m, n:n + 1], rsum[0:m, n:n + 1]).then_inc(inv_ready, 1)
                    dve.wait_ge(inv_ready, layer * NEXP + n + 1)
                    dve.tensor_scalar(probs[0:m, h % 2, i, :], probs[0:m, h % 2, i, :], rinv[0:m, n:n + 1], None,
                                      ALU.mult).then_inc(probs_ready, 1)

                def softmax(h):
                    for i in range(NT):
                        maximum(h, i)
                        if i:
                            normalise(h, i - 1)
                    normalise(h, NT - 1)

                def gated(h):
                    wait_mm(("a", h))
                    dve.tensor_tensor(two(mix[:, 4 + h, :]), phalf(("a", h)), two(gate[:, 4 + h, :]), ALU.mult).then_inc(vec_out, 1)

                softmax(0)
                softmax(1)
                softmax(2)
                gated(0)
                softmax(3)
                for h in range(1, HEADS):
                    gated(h)
                for m in range(KD):
                    wait_mm(("o", m))
                    dve.tensor_tensor(two(hT[:, m, :]), phalf(("o", m)), two(hT[:, m, :]), ALU.add).then_inc(vec_out, 1)

            dve.wait_ge(lw_ready, 16 * (LAYERS + 1))
            dve.wait_ge(rstd_ready, LAYERS * 3 + 1)
            for k in range(KD):
                c = LW_VEC + V2["mem"][0] + k
                dve.scalar_tensor_tensor(T.memn[:, k, :], T.memT[:, k, :], lw[:, c:c + 1], rstd[:, 1, 0:MEM],
                                         ALU.mult, ALU.mult).then_inc(T.memn_ready, 1)

        @block.scalar
        def _(act):
            act.sem_inc(act_out, NA1)
            act.wait_ge(T.setup, T.N_SETUP)
            with act.Fori(0, LAYERS) as layer:

                def wait_mm(g):
                    act.wait_ge(mm_done, (layer + 1) * NG1 + GI1[g] + 1)

                def wait_vec(g):
                    act.wait_ge(vec_out, (layer + 1) * NV1 + VI1[g])

                def rms(r, size):
                    g = ("rs", r)
                    wait_mm(g)
                    act.activation(two(rstd[:, r, :]), phalf(g), ACT.Ln, bias=eps[:, :], scale=1.0 / size).then_inc(act_out, 1)
                    act.wait_ge(act_out, (layer + 1) * NA1 + AI1[g])
                    act.activation(rstd[:, r, :], rstd[:, r, :], ACT.Exp, scale=-0.5).then_inc(rstd_ready, 1)

                def copy(g, out, src):
                    wait_mm(g)
                    act.activation(out, src, ACT.Copy).then_inc(act_out, 1)

                for k in range(KD):
                    act.wait_ge(h_loaded[k // 2], 16)
                    act.wait_ge(vec_out, layer * NV1 + VI1["o", k])
                    act.activation(sq[:, k, :], hT[:, k, :], ACT.Square).then_inc(sq_ready, 1)
                rms(0, D)
                for k in range(KQ + KKV):
                    wait_vec(("u", k))
                    act.activation(sq[:, k, :], cq[:, k, :], ACT.Square).then_inc(sq_ready, 1)
                rms(1, QR)
                rms(2, KVR)
                for m in range(8):
                    wait_vec(("ga", m))
                    act.activation(gate[:, m, :], gate[:, m, :], ACT.Silu).then_inc(silu_done, 1)
                for h in range(HEADS):
                    copy(("q", h), two(qn[:, h, :]), phalf(("q", h)))
                for h in range(HEADS):
                    copy(("kn", h), two(kn[:, h, :]), phalf(("kn", h)))
                for i in range(2):
                    copy(("v", i), v[:, 2 * i:2 * i + 2, :], pst(("v", i))[:, :, :])
                copy(("v", 2), v[0:LT[-1][1], NT - 1, :], pst(("v", 2))[0:LT[-1][1], 0, :])
                for i, (t0, m) in enumerate(LT):
                    copy(("pq", i), pq[0:m, i, :, :], pst(("pq", i))[0:m, :, 0:256])

                def exponentials(h):
                    for i, (t0, m) in enumerate(LT):
                        n = h * NT + i
                        act.wait_ge(max_ready, layer * NEXP + n + 1)
                        act.activation(two(probs[0:m, h % 2, i, :]), phalf(("s", h, i), 0, m), ACT.Exp, bias=nmax[0:m, n:n + 1],
                                       accum_out=rsum[0:m, n:n + 1]).then_inc(act_out, 1)

                def turned(h):
                    for j, (k0, kj) in enumerate(LT):
                        copy(("t", h, j), pT[0:kj, j, :], pflat(("t", h, j))[0:kj, 0:L])

                exponentials(0)
                exponentials(1)
                turned(0)
                exponentials(2)
                turned(1)
                exponentials(3)
                turned(2)
                turned(3)

            act.wait_ge(T.mem_loaded, 16)
            act.wait_ge(mm_done, LAYERS * NG1 + GI1["a", HEADS - 1] + 1)
            for k in range(KD):
                act.activation(T.mem_sq[:, k, :], T.memT[:, k, :], ACT.Square).then_inc(sq_ready, 1)
            for k in range(KD):
                act.wait_ge(vec_out, LAYERS * NV1 + VI1["o", k])
                act.activation(sq[:, k, :], hT[:, k, :], ACT.Square).then_inc(sq_ready, 1)
            for n, (src, out) in enumerate(((ps[0][:, 0, 0:MEM], rstd[:, 1, 0:MEM]), (ps[1][:, :, 0:LH], two(rstd[:, 0, :])))):
                act.wait_ge(mm_done, (LAYERS + 1) * NG1 + n + 1)
                act.activation(out, src, ACT.Ln, bias=eps[:, :], scale=1.0 / D).then_inc(act_out, 1)
                act.wait_ge(act_out, (LAYERS + 1) * NA1 + n + 1)
                act.activation(out, out, ACT.Exp, scale=-0.5).then_inc(rstd_ready, 1)


def second_block(nc, dram, T, sem):
    ctx = ExitStack()
    with ctx:
        def sb(name, shape):
            return ctx.enter_context(nc.sbuf_tensor(name, shape, F32))

        hT, ring, ones, ident, eps, lw, ps = T.hT, T.ring, T.ones, T.ident, T.eps, T.lw, T.ps
        x = hT[:, :, META:L]
        sq = sb("sq", [P, KD, SEQ])
        xn = sb("xn", [P, KD, SEQ])
        rstd = T.rstd[:, 1:3, 0:SEQ]
        memn = T.memn
        kx = sb("kx", [P, KD, MEM])
        vx = sb("vx", [P, 2, D])
        wide = sb("wide", [P, KH * (SEQ + 3) + KH * SEQ])
        xr = wide[:, 0:KH * (SEQ + 3)].rearrange("p (c n) -> p c n", c=KH)
        xg = wide[:, KH * (SEQ + 3):].rearrange("p (c n) -> p c n", c=KH)
        qx = wide[:, 0:KD * SEQ].rearrange("p (c n) -> p c n", c=KD)
        qa = sb("qa", [P, KH, SEQ])
        kaE = sb("kaE", [P, KH, SEQ])
        kaO = sb("kaO", [P, KH, SEQ])
        va = sb("va", [P, TT, DH])
        bias = sb("bias", [P, AH, SEQ])
        ox = bias
        sbuf = sb("sbuf", [P, 2, SBW])
        xc = sb("xc", [P, KH, SEQ])
        r = T.memT.rearrange("p (c b) n -> p c (b n)", c=KH)
        pT = r
        gi = vx[:, :, :].rearrange("p c (b n) -> p (c b) n", b=2)
        aa, th = sq[:, 0:KH, :], sq[:, KH:, :]
        yr = xn[:, 0:KH, :]
        vec = lw[:, LW_VEC:LW_VEC + NV2]
        wr = lw[:, LW_WR:LW_WR + KD * NL].rearrange("p (k n) -> p k n", k=KD)
        rb = lw[:, LW_RB:LW_RB + TT * NL]
        wab = sbuf[:, 1, 0:2 * KH * P].rearrange("p (c n) -> p c n", c=2 * KH)
        nsp = sb("nsp", [P, 6, KH])
        mx = sb("mx", [P, 4 * AH])
        nmx = sb("nmx", [P, 4 * (AH + XH)])
        rsum = sb("rsum2", [P, 4 * (AH + XH)])
        rinv = sb("rinv2", [P, 4 * (AH + XH)])

        mm_done = sem("mm2_done")
        vec_out = sem("vec2_out")
        act_out = sem("act2_out")
        w_ready = T.w_ready
        loaded = sem("loaded2")
        key_pad = sem("key_pad")
        sq_ready = sem("sq2_ready")
        rstd_ready = sem("rstd2_ready")
        norm_ready = sem("norm_ready")
        pad_ready = sem("pad_ready")
        mask_ready = sem("mask_ready")
        conv_step = sem("conv_step")
        sp_step = sem("sp_step")
        sp_exp = sem("sp_exp")
        decay_ready = sem("decay_ready")
        m2_ready = sem("m2_ready")
        logs_ready = sem("logs_ready")
        root_ready = sem("root_ready")
        gelu_ready = sem("gelu_ready")
        rnn_step = sem("rnn_step")
        scanned = sem("scanned")
        max_ready = sem("max2_ready")
        nmax_ready = sem("nmax_ready")
        exp_done = sem("exp2_done")
        inv_ready = sem("inv2_ready")
        probs_ready = sem("probs2_ready")

        def col(name, c):
            o = V2[name][0] + c
            return vec[:, o:o + 1]

        def pst(g):
            return ps[GI2[g] % NPS]

        def pflat(g):
            return pst(g)[:, :, :].rearrange("p a n -> p (a n)")

        def norm_at(name):
            return KD * NORMS.index(name)

        block = ctx.enter_context(nc.Block())

        @block.sync
        def _(sp):
            for n, (name, i) in enumerate(W2):
                if n >= RING:
                    sp.wait_ge(mm_done, GI2[W2_LAST[n - RING]] + 1)
                    sp.dma_start(panel_view(ring, n), panel_source(dram, name, i)).then_inc(w_ready[n % RING], 16)

        @block.gpsimd
        def _(pool):
            pool.dma_start(wab, dram["wab"]).then_inc(loaded, 16)
            pool.dma_start(bias[:, :, :], dram["bias"].rearrange("h p n -> p h n")).then_inc(loaded, 16)
            pool.memset(xr[:, :, 0:3], 0.0).then_inc(pad_ready, 1)
            pool.wait_ge(pad_ready, 1)
            pool.memset(kaE[64:128, :, :], 0.0).then_inc(key_pad, 1)
            pool.wait_ge(key_pad, 1)
            pool.memset(kaO[0:64, :, :], 0.0).then_inc(key_pad, 1)
            pool.wait_ge(key_pad, 2)
            pool.wait_ge(loaded, 16 * 2)
            pool.memset(bias[0:64, :, SEQ - 64:SEQ], -1e30).then_inc(mask_ready, 1)
            pool.wait_ge(act_out, AI2["gt", KH - 1])
            pool.tensor_tensor(gi, gi, xc[:, :, :], ALU.mult).then_inc(rnn_step, 1)
            pool.wait_ge(logs_ready, 2)
            pool.tensor_tensor(yr, yr, th, ALU.subtract).then_inc(rnn_step, 1)
            pool.wait_ge(root_ready, 1)
            pool.wait_ge(rnn_step, 2)
            pool.tensor_tensor(gi, gi, yr, ALU.mult).then_inc(rnn_step, 1)
            pool.wait_ge(scanned, KH)
            pool.wait_ge(gelu_ready, 1)
            pool.tensor_tensor(yr, yr, xg, ALU.mult).then_inc(rnn_step, 1)

        @block.tensor
        def _(pe):
            def begin(g):
                n = GI2[g]
                if n >= NPS:
                    prev = G2[n - NPS]
                    if prev in AI2:
                        pe.wait_ge(act_out, AI2[prev])
                    else:
                        pe.wait_ge(vec_out, VI2[prev])

            def panel(name, i):
                n = WI2[name, i]
                pe.wait_ge(w_ready[n % RING], 16 * (LAYERS * NW1 // RING + n // RING + 1))
                return panel_view(ring, n)

            def sums(g, name, banks=1, n=SEQ):
                begin(g)
                per = KD // banks
                for c in range(KD):
                    pe.wait_ge(sq_ready, norm_at(name) - KD + c + 1)
                    mm = pe.matmul(pst(g)[:, c // per, 0:n], ones[:, :], sq[:, c, 0:n], start=c % per == 0, stop=c % per == per - 1)
                mm.then_inc(mm_done, 1)

            def two(g, name, i, rhs):
                w = panel(name, i)
                begin(g)
                for b in range(2):
                    for k in range(KD):
                        mm = pe.matmul(pst(g)[:, b, :], w[:, k, b * P:b * P + P], rhs[:, k, :], start=k == 0, stop=k == KD - 1)
                mm.then_inc(mm_done, 1)

            def memory_keys(q):
                g = ("kx", q)
                w = panel("xk", q)
                begin(g)
                for m in range(2):
                    for k in range(KD):
                        mm = pe.matmul(pst(g)[:, 0, m * MEM:m * MEM + MEM], w[:, k, m * P:m * P + P], memn[:, k, :],
                                       start=k == 0, stop=k == KD - 1)
                mm.then_inc(mm_done, 1)

            def memory_values(g, quarters):
                begin(g)
                for b, q in enumerate(quarters):
                    w = panel("xv", q)
                    for j in range(2):
                        for k in range(KD):
                            mm = pe.matmul(pst(g)[:, j, b * 256:b * 256 + 256], memn[:, k, j * P:j * P + P], w[:, k, :],
                                           start=k == 0, stop=k == KD - 1)
                mm.then_inc(mm_done, 1)

            pe.wait_ge(T.lw_ready, 16 * (LAYERS + 1))
            pe.wait_ge(T.memn_ready, KD)
            memory_keys(0)
            sums(("n", 1), "ln1")
            memory_keys(1)
            pe.wait_ge(norm_ready, norm_at("ln1") + KD)
            for j, name in enumerate(("xr", "xg", "qa", "ka")):
                for c in range(2):
                    two((name, c), "win2", 2 * j + c, xn)
            begin(("va", 0))
            begin(("va", 1))
            for half in range(2):
                w = panel("win2", 8 + half)
                for i in range(TT):
                    for k in range(KD):
                        mm = pe.matmul(pst(("va", i // 2))[:, i % 2, half * 256:half * 256 + 256], xn[:, k, i * P:i * P + P], w[:, k, :],
                                       start=k == 0, stop=k == KD - 1)
                    if half and i % 2:
                        mm.then_inc(mm_done, 1)

            pe.wait_ge(loaded, 16 * 2)
            pe.wait_ge(conv_step, CONV)
            for c in range(KH):
                g = ("gt", c)
                begin(g)
                for b in range(2):
                    mm = pe.matmul(pst(g)[:, b, :], wab[:, b * KH + c, :], xc[:, c, :], start=True, stop=True)
                mm.then_inc(mm_done, 1)

            def scores(h):
                keys = kaO if h % 2 else kaE
                for g, tiles in ((("sA", h), (3, 2)), (("sB", h), (1, 0))):
                    begin(g)
                    for b, i in enumerate(tiles):
                        mm = pe.matmul(pst(g)[:, b, 0:(i + 1) * P], qa[:, h // 2, i * P:i * P + P], keys[:, h // 2, 0:(i + 1) * P],
                                       start=True, stop=True)
                    mm.then_inc(mm_done, 1)

            def turn(h):
                pe.wait_ge(probs_ready, 4 * h + 4)
                for g, js in ((("tA", h), (0, 1)), (("tB", h), (2, 3))):
                    begin(g)
                    for b, j in enumerate(js):
                        for i in range(j, TT):
                            o = SOFF[i] + j * P
                            mm = pe.transpose(pst(g)[:, b, i * P:i * P + P], sbuf[:, h % 2, o:o + P], ident[:, :])
                    mm.then_inc(mm_done, 1)

            def attend(h):
                g = ("at", h)
                begin(g)
                pe.wait_ge(act_out, AI2["tB", h])
                for j in range(TT):
                    mm = pe.matmul(pst(g)[0:64, 0, j * P:SEQ], va[:, j, h * 64:h * 64 + 64], pT[:, j, j * P:SEQ],
                                   start=j == 0, stop=j == TT - 1)
                mm.then_inc(mm_done, 1)

            pe.wait_ge(act_out, AI2["ka", 1])
            pe.wait_ge(vec_out, VI2["va", 1])
            pe.wait_ge(key_pad, 2)
            scores(0)
            memory_keys(2)
            scores(1)
            memory_keys(3)
            for h in range(AH):
                turn(h)
                if h + 2 < AH:
                    scores(h + 2)
                attend(h)

            sums(("n", 2), "mixed", banks=2)
            memory_values(("vx", 0), (0, 1))
            pe.wait_ge(norm_ready, norm_at("mixed") + KD)
            for m in range(4):
                two(("o", m), "wout2", m, xn)
            memory_values(("vx", 1), (2,))
            sums(("n", 3), "ln2")
            memory_values(("vx", 2), (3,))
            pe.wait_ge(norm_ready, norm_at("ln2") + KD)
            for m in range(4):
                two(("qx", m), "xq", m, xn)

            def cross_scores(h):
                g = ("sx", h)
                begin(g)
                for i in range(TT):
                    for c in range(2):
                        mm = pe.matmul(pflat(g)[:, i * MEM:i * MEM + MEM], qx[:, 2 * h + c, i * P:i * P + P], kx[:, 2 * h + c, :],
                                       start=c == 0, stop=c == 1)
                mm.then_inc(mm_done, 1)

            def cross_turn(h):
                g = ("tx", h)
                pe.wait_ge(probs_ready, 4 * AH + 4 * h + 4)
                begin(g)
                for j in range(2):
                    for i in range(TT):
                        mm = pe.transpose(pst(g)[:, j, i * P:i * P + P], sbuf[:, h % 2, i * MEM + j * P:i * MEM + j * P + P], ident[:, :])
                mm.then_inc(mm_done, 1)

            def cross_attend(h):
                g = ("ax", h)
                begin(g)
                pe.wait_ge(act_out, AI2["tx", h])
                for b in range(2):
                    for j in range(2):
                        mm = pe.matmul(pst(g)[:, b, :], vx[:, j, h * 256 + b * P:h * 256 + b * P + P], pT[:, j, :],
                                       start=j == 0, stop=j == 1)
                mm.then_inc(mm_done, 1)

            pe.wait_ge(act_out, AI2["qx", 3])
            pe.wait_ge(vec_out, VI2["vx", 2])
            cross_scores(0)
            cross_scores(1)
            for h in range(XH):
                cross_turn(h)
                if h + 2 < XH:
                    cross_scores(h + 2)
                cross_attend(h)
            pe.wait_ge(vec_out, VI2["ax", XH - 1])
            for m in range(4):
                two(("xo", m), "xo", m, ox)

            sums(("n", 4), "ln3")
            g = ("lg",)
            begin(g)
            pe.wait_ge(norm_ready, norm_at("ln3") + KD)
            for i in range(TT):
                for k in range(KD):
                    mm = pe.matmul(pst(g)[:, 0, i * NL:i * NL + NL], xn[:, k, i * P:i * P + P], wr[:, k, :], start=k == 0, stop=k == KD - 1)
            mm.then_inc(mm_done, 1)
            for name, src in (("ht", xn), ("xt", x)):
                for i in range(TT):
                    g = (name, i)
                    begin(g)
                    for k in range(KD):
                        mm = pe.transpose(pflat(g)[:, k * P:k * P + P], src[:, k, i * P:i * P + P], ident[:, :])
                    mm.then_inc(mm_done, 1)

        @block.vector
        def _(dve):
            def wait_mm(g):
                dve.wait_ge(mm_done, GI2[g] + 1)

            def norm(name, out, src, w, r=lambda k: 0):
                dve.wait_ge(rstd_ready, NORMS.index(name))
                for k in range(KD):
                    dve.scalar_tensor_tensor(out[:, k, :], src[:, k, :], w(k), rstd[:, r(k), :], ALU.mult, ALU.mult).then_inc(norm_ready, 1)

            def copy(g, out, src):
                wait_mm(g)
                dve.tensor_copy(out, src).then_inc(vec_out, 1)

            dve.wait_ge(T.lw_ready, 16 * (LAYERS + 1))
            for k in range(KD):
                dve.scalar_tensor_tensor(x[:, k, :], x[:, k, :], lw[:, k:k + 1], T.rstd[:, 0, META:L], ALU.mult, ALU.mult
                                         ).then_inc(norm_ready, 1)
            dve.wait_ge(norm_ready, norm_at("first") + KD)

            lam = vec[:, V2["lam"][0]:V2["lam"][0] + KH]
            absl, e, z, z2, acc, res = (nsp[:, i, :] for i in range(6))
            steps = [0]

            def step(ins):
                steps[0] += 1
                ins.then_inc(sp_step, 1)
                dve.wait_ge(sp_step, steps[0])

            step(dve.scalar_tensor_tensor(absl, lam, -1.0, lam, ALU.mult, ALU.max))
            dve.wait_ge(sp_exp, 1)
            step(dve.tensor_scalar(z2, e, 2.0, None, ALU.add))
            step(dve.reciprocal(z2, z2))
            step(dve.tensor_tensor(z, e, z2, ALU.mult))
            step(dve.tensor_tensor(z2, z, z, ALU.mult))
            step(dve.tensor_scalar(acc, z2, 1.0 / 17, None, ALU.mult))
            for odd in (15, 13, 11, 9, 7, 5, 3):
                step(dve.scalar_tensor_tensor(acc, acc, 1.0 / odd, z2, ALU.add, ALU.mult))
            step(dve.scalar_tensor_tensor(acc, acc, 1.0, z, ALU.add, ALU.mult))
            step(dve.tensor_scalar(res, lam, -1.0, 0.0, ALU.mult, ALU.max))
            step(dve.scalar_tensor_tensor(res, acc, 2.0, res, ALU.mult, ALU.add))
            step(dve.tensor_scalar(res, res, -8.0, None, ALU.mult))
            T.sp_steps = steps[0]

            norm("ln1", xn, x, lambda k: col("ln1", k))
            for c in range(2):
                copy(("xr", c), xr[:, 2 * c:2 * c + 2, 3:3 + SEQ], pst(("xr", c))[:, :, :])
            for c in range(2):
                copy(("xg", c), xg[:, 2 * c:2 * c + 2, :], pst(("xg", c))[:, :, :])
            dve.wait_ge(pad_ready, 1)
            dve.wait_ge(vec_out, VI2["xr", 1])
            for c in range(KH):
                last = dve.tensor_scalar(xc[:, c, :], xr[:, c, 3:3 + SEQ], col("cw", 3 * KH + c), col("cb", c), ALU.mult, ALU.add)
            last.then_inc(conv_step, 1)
            for j in range(CONV - 1):
                dve.wait_ge(conv_step, j + 1)
                for c in range(KH):
                    last = dve.scalar_tensor_tensor(xc[:, c, :], xr[:, c, j:j + SEQ], col("cw", j * KH + c), xc[:, c, :],
                                                    ALU.mult, ALU.add)
                last.then_inc(conv_step, 1)
            for c in range(2):
                copy(("va", c), va[:, 2 * c:2 * c + 2, :], pst(("va", c))[:, :, :])

            def biased(h):
                for g, tiles in ((("sA", h), (3, 2)), (("sB", h), (1, 0))):
                    wait_mm(g)
                    for b, i in enumerate(tiles):
                        n = (i + 1) * P
                        last = dve.tensor_tensor_reduce(sbuf[:, h % 2, SOFF[i]:SOFF[i] + n], pst(g)[:, b, 0:n], bias[:, h, SEQ - n:SEQ],
                                                        1.0, -3e38, ALU.add, ALU.max, mx[:, 4 * h + i:4 * h + i + 1])
                    last.then_inc(vec_out, 1)
                dve.wait_ge(vec_out, VI2["sB", h])
                dve.tensor_scalar(nmx[:, 4 * h:4 * h + 4], mx[:, 4 * h:4 * h + 4], -1.0, None, ALU.mult).then_inc(nmax_ready, 1)

            def normalise(h, n, places):
                if h < AH:
                    dve.wait_ge(exp_done, 4 * h + 4)
                else:
                    dve.wait_ge(act_out, AI2["sx", h - AH])
                dve.reciprocal(rinv[:, 4 * h:4 * h + 4], rsum[:, 4 * h:4 * h + 4]).then_inc(inv_ready, 1)
                dve.wait_ge(inv_ready, h + 1)
                for i in range(TT):
                    p = sbuf[:, n, places[i][0]:places[i][0] + places[i][1]]
                    dve.tensor_scalar(p, p, rinv[:, 4 * h + i:4 * h + i + 1], None, ALU.mult).then_inc(probs_ready, 1)

            places = [(SOFF[i], (i + 1) * P) for i in range(TT)]

            def attended(h):
                rows = slice(64 * (h % 2), 64 * (h % 2) + 64)
                copy(("at", h), xn[rows, KH + h // 2, :], pst(("at", h))[0:64, 0, :])

            def decay():
                dve.wait_ge(decay_ready, KH)
                dve.wait_ge(mm_done, GI2["va", 1] + 1)
                dve.tensor_scalar(yr, th, -2.0, TINY, ALU.mult, ALU.max).then_inc(m2_ready, 1)

            def scan():
                dve.wait_ge(rnn_step, 3)
                for c in range(KH):
                    dve.tensor_tensor_scan(yr[:, c, :], aa[:, c, :], gi[:, c, :], 0.0, ALU.mult, ALU.add).then_inc(scanned, 1)

            dve.wait_ge(mask_ready, 1)
            biased(0)
            decay()
            biased(1)
            normalise(0, 0, places)
            for h in range(AH):
                if h + 1 < AH:
                    normalise(h + 1, (h + 1) % 2, places)
                if h + 2 < AH:
                    biased(h + 2)
                attended(h)
                if h == 3:
                    scan()
            norm("mixed", xn, xn, lambda k: col("gnr", k) if k < KH else col("gna", k - KH), lambda k: k // KH)

            def add(g, m):
                wait_mm(g)
                dve.tensor_tensor(x[:, 2 * m:2 * m + 2, :], pst(g)[:, :, :], x[:, 2 * m:2 * m + 2, :], ALU.add).then_inc(vec_out, 1)

            copy(("vx", 0), vx[:, :, 0:512], pst(("vx", 0))[:, :, :])
            for m in range(4):
                add(("o", m), m)
            copy(("vx", 1), vx[:, :, 512:768], pst(("vx", 1))[:, :, 0:256])
            norm("ln2", xn, x, lambda k: col("ln2", k))
            copy(("vx", 2), vx[:, :, 768:1024], pst(("vx", 2))[:, :, 0:256])

            def cross_max(h):
                wait_mm(("sx", h))
                n = 4 * (AH + h)
                dve.tensor_reduce(nmx[:, n:n + 4], pflat(("sx", h)).rearrange("p (i n) -> p i n", i=TT), AX.X, ALU.max,
                                  negate=True).then_inc(nmax_ready, 1)

            xplaces = [(i * MEM, MEM) for i in range(TT)]
            cross_max(0)
            cross_max(1)
            normalise(AH, 0, xplaces)
            for h in range(XH):
                if h + 1 < XH:
                    normalise(AH + h + 1, (h + 1) % 2, xplaces)
                if h + 2 < XH:
                    cross_max(h + 2)
                copy(("ax", h), ox[:, 2 * h:2 * h + 2, :], pst(("ax", h))[:, :, :])
            for m in range(4):
                add(("xo", m), m)
            norm("ln3", xn, x, lambda k: col("ln3", k))
            wait_mm(("lg",))
            dve.tensor_tensor(T.logits[:, :], pst(("lg",))[:, 0, 0:TT * NL], rb[:, :], ALU.add).then_inc(vec_out, 1)
            for i in range(TT):
                copy(("xt", i), T.xtok[:, i, :], pflat(("xt", i)))

        @block.scalar
        def _(act):
            def wait_mm(g):
                act.wait_ge(mm_done, GI2[g] + 1)

            def square(name, k, src, n=SEQ):
                act.activation(sq[:, k, 0:n], src[:, k, 0:n], ACT.Square).then_inc(sq_ready, 1)

            def rms(g, size, banks=1, n=SEQ):
                wait_mm(g)
                out = rstd[:, 0:banks, 0:n]
                act.activation(out, pst(g)[:, 0:banks, 0:n], ACT.Ln, bias=eps[:, :], scale=1.0 / size).then_inc(act_out, 1)
                act.wait_ge(act_out, AI2[g])
                act.activation(out, out, ACT.Exp, scale=-0.5).then_inc(rstd_ready, 1)

            def copy(g, out, src, scale=1.0):
                wait_mm(g)
                act.activation(out, src, ACT.Copy, scale=scale).then_inc(act_out, 1)

            def memory_keys(q):
                copy(("kx", q), kx[:, 2 * q:2 * q + 2, :].rearrange("p m n -> p (m n)"), pst(("kx", q))[:, 0, :])

            act.wait_ge(T.lw_ready, 16 * (LAYERS + 1))
            for k in range(KD):
                act.wait_ge(norm_ready, norm_at("first") + k + 1)
                square("ln1", k, x)
            memory_keys(0)
            act.wait_ge(sp_step, 1)
            act.activation(nsp[:, 1, :], nsp[:, 0, :], ACT.Exp, scale=-1.0).then_inc(sp_exp, 1)
            rms(("n", 1), D)
            memory_keys(1)
            for c in range(2):
                copy(("qa", c), qa[:, 2 * c:2 * c + 2, :], pst(("qa", c))[:, :, :], scale=64 ** -0.5)
            for c in range(2):
                g = ("ka", c)
                wait_mm(g)
                act.activation(kaE[0:64, 2 * c:2 * c + 2, :], pst(g)[0:64, :, :], ACT.Copy)
                act.activation(kaO[64:128, 2 * c:2 * c + 2, :], pst(g)[64:128, :, :], ACT.Copy).then_inc(act_out, 1)
            for c in range(KH):
                g = ("gt", c)
                wait_mm(g)
                act.activation(r[:, c, :], pst(g)[:, 0, :], ACT.Sigmoid, bias=col("ba", c))
                act.activation(gi[:, c, :], pst(g)[:, 1, :], ACT.Sigmoid, bias=col("bx", c)).then_inc(act_out, 1)
            act.wait_ge(act_out, AI2["gt", KH - 1])
            act.wait_ge(sp_step, T.sp_steps)
            for c in range(KH):
                act.activation(th[:, c, :], r[:, c, :], ACT.Tanh, scale=nsp[:, 5, c:c + 1]).then_inc(decay_ready, 1)
            for c in range(KH):
                act.activation(aa[:, c, :], r[:, c, :], ACT.Exp, scale=nsp[:, 5, c:c + 1]).then_inc(decay_ready, 1)

            def exponentials(h):
                act.wait_ge(nmax_ready, h + 1)
                for i in range(TT):
                    p = sbuf[:, h % 2, SOFF[i]:SOFF[i] + (i + 1) * P]
                    act.activation(p, p, ACT.Exp, bias=nmx[:, 4 * h + i:4 * h + i + 1],
                                   accum_out=rsum[:, 4 * h + i:4 * h + i + 1]).then_inc(exp_done, 1)

            def turned(h):
                for g, js in ((("tA", h), (0, 1)), (("tB", h), (2, 3))):
                    wait_mm(g)
                    for b, j in enumerate(js):
                        last = act.activation(pT[:, j, j * P:SEQ], pst(g)[:, b, j * P:SEQ], ACT.Copy)
                    last.then_inc(act_out, 1)

            def root():
                act.wait_ge(m2_ready, 1)
                act.activation(yr, yr, ACT.Ln).then_inc(logs_ready, 1)
                act.activation(th, th, ACT.Ln, scale=-1.0, bias=ones[:, 0:1]).then_inc(logs_ready, 1)

            def root_exp():
                act.wait_ge(rnn_step, 2)
                act.activation(yr, yr, ACT.Exp, scale=0.5).then_inc(root_ready, 1)

            def gelu():
                act.wait_ge(vec_out, VI2["xg", 1])
                act.activation(xg, xg, ACT.Gelu_apprx_tanh).then_inc(gelu_ready, 1)

            exponentials(0)
            memory_keys(2)
            exponentials(1)
            memory_keys(3)
            act.wait_ge(decay_ready, 2 * KH)
            for h in range(AH):
                turned(h)
                if h < 3:
                    (root, root_exp, gelu)[h]()
                if h + 2 < AH:
                    exponentials(h + 2)
            act.wait_ge(rnn_step, 4)
            for k in range(KH):
                square("mixed", k, xn)
            for k in range(KH, KD):
                act.wait_ge(vec_out, VI2["at", 2 * (k - KH) + 1])
                square("mixed", k, xn)
            rms(("n", 2), DH, banks=2)
            for k in range(KD):
                act.wait_ge(vec_out, VI2["o", k // 2])
                square("ln2", k, x)
            rms(("n", 3), D)
            for m in range(4):
                copy(("qx", m), qx[:, 2 * m:2 * m + 2, :], pst(("qx", m))[:, :, :], scale=256 ** -0.5)

            def cross_exponentials(h):
                n = 4 * (AH + h)
                act.wait_ge(nmax_ready, AH + h + 1)
                for i in range(TT):
                    last = act.activation(sbuf[:, h % 2, i * MEM:i * MEM + MEM], pflat(("sx", h))[:, i * MEM:i * MEM + MEM], ACT.Exp,
                                          bias=nmx[:, n + i:n + i + 1], accum_out=rsum[:, n + i:n + i + 1])
                last.then_inc(act_out, 1)

            cross_exponentials(0)
            cross_exponentials(1)
            for h in range(XH):
                copy(("tx", h), pT[:, 0:2, :], pst(("tx", h))[:, :, :])
                if h + 2 < XH:
                    cross_exponentials(h + 2)
            for k in range(KD):
                act.wait_ge(vec_out, VI2["xo", k // 2])
                square("ln3", k, x)
            rms(("n", 4), D)
            for i in range(TT):
                copy(("ht", i), T.htok[:, i, :], pflat(("ht", i)))


CAP = 64
PAIRS = NE // 2
EPG = NE // NGRP
FE = 512
KF = FE // P
ROUNDS_MAX = SEQ // CAP

G3 = ([("x", 0), ("x", 1)] + [("o", n) for n in range(4)] + [("gt",), ("up",)] + [("o", n) for n in range(4, 8)]
      + [("ht",), ("st",), ("y", 0), ("y", 1)])
BANK = {g: n % 8 for n, g in enumerate(G3)}
ACT_OWNS3 = [("x", 0), ("gt",), ("ht",), ("y", 0), ("y", 1)]
GI3 = {g: n for n, g in enumerate(G3)}
AI3 = {g: n + 1 for n, g in enumerate(ACT_OWNS3)}
VI3 = {g: n + 1 for n, g in enumerate(g for g in G3 if g not in ACT_OWNS3)}
NG3, NA3, NV3 = len(G3), len(AI3), len(VI3)


def experts(nc, dram, T, sem, out):
    ctx = ExitStack()
    with ctx:
        def sb(name, shape, dt=F32):
            return ctx.enter_context(nc.sbuf_tensor(name, shape, dt))

        htok, acc, ident, ones, eps, logits = T.htok, T.xtok, T.ident, T.ones, T.eps, T.logits
        weights = [[sb(f"w_{n}{e}", [P, 8 * FE]) for n in ("gate", "up", "down")] for e in range(2)]
        lg = logits[:, :].rearrange("p (i n) -> p i n", i=TT)
        G4 = [P, TT, NGRP]
        G32 = [P, TT, NE]
        iota_g = sb("iota_g", G4)
        iota_e = sb("iota_e", G32)
        slot = sb("slot", [P, TT, CAP])
        before = sb("before", [P, P])
        steps8 = sb("steps8", [P, ROUNDS_MAX - 1])
        gmax, gsum, gidx, m1, m2, i1, w1, w2, e2, den = (sb(n, [P, TT]) for n in
                                                         ("gmax", "gsum", "gidx", "m1", "m2", "i1", "w1", "w2", "e2", "den"))
        ge = sb("ge", G4)
        gone = sb("gone", G4)
        le = sb("le", G32)
        one1 = sb("one1", G32)
        one2 = sb("one2", G32)
        tmp = sb("tmp", G32)
        tmp2 = sb("tmp2", G32)
        chosen = sb("chosen", G32)
        wcomb = sb("wcomb", [P, TT, NE + 2])
        rank = sb("rank", [P, TT, NE + 2])
        cmax = sb("cmax", [P, 1])
        rounds = sb("rounds", [P, 1], mybir.dt.int32)
        sel = sb("sel", [P, TT, 2 * CAP])
        selw = sb("selw", [P, TT, 2 * CAP])
        selT = sb("selT", [P, SEQ])
        xe = sb("xe", [P, KD, 2 * CAP])
        sg = sb("sg", [P, FE])
        he = sb("he", [P, FE])
        hT = sb("heT", [P, KF, 2 * CAP])
        ys = sb("ys", [P, D])
        fw = sb("fw", [P, D])
        sqo = sb("sqo", [P, D])
        ssum = sb("ssum", [P, TT])

        w_loaded = [[sem(f"w_loaded{e}{j}") for j in range(3)] for e in range(2)]
        mm_done = sem("mm3_done")
        vec_out = sem("vec3_out")
        act_out = sem("act3_out")
        const_made = sem("const3_made")
        fw_loaded = sem("fw_loaded")
        route_step = sem("route_step")
        group_exp = sem("group_exp")
        pair_exp = sem("pair_exp")
        ranks_done = sem("ranks_done")
        rounds_ready = sem("rounds_ready")
        sel_made = sem("sel_made")
        sel_ready = sem("sel_ready")
        rank_moved = sem("rank_moved")
        he_ready = sem("he_ready")
        ss_done = sem("ss_done")
        rstd_done = sem("rstd3_done")
        out_ready = sem("out_ready")
        stored = sem("stored")

        def bank(g):
            return T.ps[BANK[g] // 2][:, BANK[g] % 2, :]

        block = ctx.enter_context(nc.Block())

        @block.sync
        def _(sp):
            def load(pair, it):
                def matrix(e, j, name, k):
                    src = dram[name][bass.ds(pair * 2 + e, 1), :, :].rearrange("a (k p) n -> p (a k) n", p=P)
                    sp.dma_start(weights[e][j][:, :].rearrange("p (k n) -> p k n", k=k), src).then_inc(w_loaded[e][j], 16)

                for j, (name, k, last) in enumerate((("eg", KD, "gt"), ("eu", KD, "up"), ("ed", KF, "y"))):
                    g = (last, 1) if last == "y" else (last,)
                    sp.wait_ge(mm_done, it * NG3 + GI3[g] + 1)
                    for e in range(2):
                        matrix(e, j, name, k)

            with sp.Fori(0, PAIRS) as pair:
                load(pair, pair)
            sp.wait_ge(rounds_ready, 1)
            n_rounds = sp.value_load(rounds[0:1, 0:1], min_val=1, max_val=ROUNDS_MAX)
            with sp.If(n_rounds > 1):
                with sp.Fori(1, n_rounds) as rnd:
                    with sp.Fori(0, PAIRS) as pair:
                        load(pair, rnd * PAIRS + pair)
            for i in range(TT):
                sp.wait_ge(out_ready, i + 1)
                sp.dma_start(out[0, i * P:i * P + P, :], acc[:, i, :]).then_inc(stored, 16)
            sp.wait_ge(stored, 16 * TT)

        @block.gpsimd
        def _(pool):
            pool.dma_start(fw[:, :], dram["fw"].partition_broadcast(P)).then_inc(fw_loaded, 16)
            pool.iota(iota_g[:, :, :], pattern=[[0, TT], [1, NGRP]], base=0, channel_multiplier=0,
                      allow_small_or_imprecise_dtypes=True).then_inc(const_made, 1)
            pool.iota(iota_e[:, :, :], pattern=[[0, TT], [1, NE]], base=0, channel_multiplier=0,
                      allow_small_or_imprecise_dtypes=True).then_inc(const_made, 1)
            pool.iota(slot[:, :, :], pattern=[[0, TT], [1, CAP]], base=0, channel_multiplier=0,
                      allow_small_or_imprecise_dtypes=True).then_inc(const_made, 1)
            pool.iota(steps8[:, :], pattern=[[CAP, ROUNDS_MAX - 1]], base=CAP, channel_multiplier=0,
                      allow_small_or_imprecise_dtypes=True).then_inc(const_made, 1)
            pool.memset(wcomb[:, :, NE:], 0.0).then_inc(const_made, 1)
            pool.memset(rank[:, :, NE:], CAP - 1.0).then_inc(const_made, 1)
            pool.memset(before[:, :], 1.0).then_inc(const_made, 1)
            pool.memset(ys[:, :], 0.0).then_inc(const_made, 1)
            pool.memset(selT[:, :], 0.0).then_inc(const_made, 1)
            pool.wait_ge(const_made, 9)
            pool.affine_select(out=before[:, :], in_=before[:, :], compare_op=ALU.is_gt, fill=0.0, base=0,
                               pattern=[[1, P]], channel_multiplier=-1).then_inc(const_made, 1)

        @block.vector
        def _(dve):
            dve.sem_inc(vec_out, NV3)
            steps = [0]

            def step(ins):
                steps[0] += 1
                ins.then_inc(route_step, 1)
                dve.wait_ge(route_step, steps[0])

            def over(a, shape):
                return a[:, :].unsqueeze(2).broadcast_to(shape)

            tt, stt, ts = dve.tensor_tensor, dve.scalar_tensor_tensor, dve.tensor_scalar
            dve.wait_ge(const_made, 10)
            step(dve.tensor_reduce(gmax[:, :], lg[:, :, 0:NGRP], AX.X, ALU.max))
            step(tt(ge[:, :, :], lg[:, :, 0:NGRP], over(gmax, G4), ALU.subtract))
            T.route_group = steps[0]
            step(tt(gone[:, :, :], lg[:, :, 0:NGRP], over(gmax, G4), ALU.is_equal))
            step(ts(gone[:, :, :], gone[:, :, :], -100.0, 100.0, ALU.mult, ALU.add))
            step(tt(gone[:, :, :], gone[:, :, :], iota_g[:, :, :], ALU.add))
            step(dve.tensor_reduce(gidx[:, :], gone[:, :, :], AX.X, ALU.min))
            step(tt(gone[:, :, :], iota_g[:, :, :], over(gidx, G4), ALU.is_equal))
            step(ts(gone[:, :, :], gone[:, :, :], 1e30, -1e30, ALU.mult, ALU.add))
            for q in range(NGRP):
                s = slice(q * EPG, q * EPG + EPG)
                step(tt(le[:, :, s], lg[:, :, NGRP + q * EPG:NGRP + q * EPG + EPG],
                        gone[:, :, q:q + 1].broadcast_to([P, TT, EPG]), ALU.add))

            def best(m, one):
                step(dve.tensor_reduce(m[:, :], le[:, :, :], AX.X, ALU.max))
                step(tt(tmp[:, :, :], le[:, :, :], over(m, G32), ALU.is_equal))
                step(ts(tmp[:, :, :], tmp[:, :, :], -100.0, 100.0, ALU.mult, ALU.add))
                step(tt(tmp[:, :, :], tmp[:, :, :], iota_e[:, :, :], ALU.add))
                step(dve.tensor_reduce(i1[:, :], tmp[:, :, :], AX.X, ALU.min))
                step(tt(one[:, :, :], iota_e[:, :, :], over(i1, G32), ALU.is_equal))

            best(m1, one1)
            step(stt(le[:, :, :], one1[:, :, :], -3e30, le[:, :, :], ALU.mult, ALU.add))
            best(m2, one2)
            step(tt(chosen[:, :, :], one1[:, :, :], one2[:, :, :], ALU.add))
            T.route_chosen = steps[0]
            step(tt(m2[:, :], m2[:, :], m1[:, :], ALU.subtract))
            T.route_pair = steps[0]
            dve.wait_ge(group_exp, 1)
            step(dve.tensor_reduce(gsum[:, :], ge[:, :, :], AX.X, ALU.add))
            dve.wait_ge(pair_exp, 1)
            step(ts(den[:, :], e2[:, :], 1.0, None, ALU.add))
            step(tt(den[:, :], den[:, :], gsum[:, :], ALU.mult))
            step(dve.reciprocal(w1[:, :], den[:, :]))
            step(tt(w2[:, :], w1[:, :], e2[:, :], ALU.mult))
            step(tt(tmp[:, :, :], one1[:, :, :], over(w1, G32), ALU.mult))
            step(tt(tmp2[:, :, :], one2[:, :, :], over(w2, G32), ALU.mult))
            step(tt(wcomb[:, :, 0:NE], tmp[:, :, :], tmp2[:, :, :], ALU.add))
            dve.wait_ge(ranks_done, 1)
            step(stt(tmp[:, :, :], T.ps[0][:, 0, 0:TT * NE].rearrange("p (i n) -> p i n", i=TT), 1.0, chosen[:, :, :], ALU.add, ALU.mult))
            step(ts(rank[:, :, 0:NE], tmp[:, :, :], CAP - 1.0, None, ALU.add))
            step(dve.tensor_reduce(cmax[:, :], T.ps[0][:, 1, 0:NE], AX.X, ALU.max))
            step(ts(steps8[:, :], steps8[:, :], cmax[:, 0:1], None, ALU.is_lt))
            step(dve.tensor_reduce(cmax[:, :], steps8[:, :], AX.X, ALU.add))
            dve.tensor_scalar(rounds[:, :], cmax[:, :], 1.0, None, ALU.add).then_inc(rounds_ready, 1)
            dve.wait_ge(rounds_ready, 1)
            n_rounds = dve.value_load(rounds[0:1, 0:1], min_val=1, max_val=ROUNDS_MAX)

            def select(first, count):
                for e in range(2):
                    r = rank[:, :, bass.ds(first + e, 1)].broadcast_to([P, TT, CAP])
                    last = dve.tensor_tensor(sel[:, :, e * CAP:e * CAP + CAP], slot[:, :, :], r, ALU.is_equal)
                last.then_inc(sel_made, 1)
                dve.wait_ge(sel_made, count)
                for e in range(2):
                    w = wcomb[:, :, bass.ds(first + e, 1)].broadcast_to([P, TT, CAP])
                    last = dve.tensor_tensor(selw[:, :, e * CAP:e * CAP + CAP], sel[:, :, e * CAP:e * CAP + CAP], w, ALU.mult)
                last.then_inc(sel_ready, 1)

            with dve.Fori(0, n_rounds) as rnd:
                per = PAIRS + 1
                dve.wait_ge(vec_out, rnd * (PAIRS * NV3) + NV3)
                dve.tensor_scalar(rank[:, :, :], rank[:, :, :], -float(CAP), None, ALU.add).then_inc(rank_moved, 1)
                dve.wait_ge(rank_moved, rnd + 1)
                select(0, rnd * per + 1)
                with dve.Fori(0, PAIRS) as pair:
                    it = rnd * PAIRS + pair

                    def wait_mm(g):
                        dve.wait_ge(mm_done, (it + 1) * NG3 + GI3[g] + 1)

                    def add(n):
                        half, i = n // TT, n % TT
                        wait_mm(("o", n))
                        a = acc[:, i, half * 512:half * 512 + 512]
                        dve.tensor_tensor(a, bank(("o", n)), a, ALU.add).then_inc(vec_out, 1)

                    wait_mm(("x", 1))
                    dve.tensor_copy(xe[:, 4:8, :], bank(("x", 1)).rearrange("p (k n) -> p k n", k=4)).then_inc(vec_out, 1)
                    for n in range(4):
                        add(n)
                    wait_mm(("up",))
                    dve.wait_ge(act_out, (it + 1) * NA3 + AI3["gt",])
                    dve.tensor_tensor(he[:, :], sg[:, :], bank(("up",)), ALU.mult).then_inc(vec_out, 1)
                    for n in range(4, 8):
                        add(n)
                    wait_mm(("st",))
                    dve.tensor_copy(selT[:, :], bank(("st",))).then_inc(vec_out, 1)
                    select(pair * 2 + 2, rnd * per + pair + 2)

            done = n_rounds * PAIRS + 1
            dve.wait_ge(fw_loaded, 16)
            for n in range(8):
                i, half = n // 2, n % 2
                a = acc[:, i, half * 512:half * 512 + 512]
                dve.wait_ge(mm_done, done * NG3 + n + 1)
                dve.tensor_tensor(a, T.ps[n // 2][:, n % 2, :], a, ALU.add).then_inc(vec_out, 1)
            for i in range(TT):
                dve.wait_ge(rstd_done, i + 1)
                stt(acc[:, i, :], acc[:, i, :], ssum[:, i:i + 1], fw[:, :], ALU.mult, ALU.mult).then_inc(out_ready, 1)

        @block.tensor
        def _(pe):
            pe.sem_inc(mm_done, NG3)
            pe.wait_ge(const_made, 10)
            pe.wait_ge(route_step, T.route_chosen)
            for i in range(TT):
                for j in range(i + 1):
                    pe.matmul(T.ps[0][:, 0, i * NE:i * NE + NE], ones[:, :] if j < i else before[:, :], chosen[:, j, :],
                              start=j == 0, stop=j == i)
            for j in range(TT):
                mm = pe.matmul(T.ps[0][:, 1, 0:NE], ones[:, :], chosen[:, j, :], start=j == 0, stop=j == TT - 1)
            mm.then_inc(ranks_done, 1)
            pe.wait_ge(rounds_ready, 1)
            n_rounds = pe.value_load(rounds[0:1, 0:1], min_val=1, max_val=ROUNDS_MAX)
            with pe.Fori(0, n_rounds) as rnd, pe.Fori(0, PAIRS) as pair:
                it = rnd * PAIRS + pair

                def begin(g):
                    same = [q for q in G3 if BANK[q] == BANK[g]]
                    prev = same[same.index(g) - 1]
                    back = 1 if GI3[prev] < GI3[g] else 0
                    if prev in AI3:
                        pe.wait_ge(act_out, (it + back) * NA3 + AI3[prev])
                    else:
                        pe.wait_ge(vec_out, (it + back) * NV3 + VI3[prev])

                def weight(e, j, k):
                    pe.wait_ge(w_loaded[e][j], (it + 1) * 16)
                    return weights[e][j][:, :].rearrange("p (k n) -> p k n", k=k)

                pe.wait_ge(sel_ready, rnd * (PAIRS + 1) + pair + 1)
                for half in range(2):
                    g = ("x", half)
                    begin(g)
                    for c in range(4):
                        k = half * 4 + c
                        for i in range(TT):
                            mm = pe.matmul(bank(g)[:, c * P:c * P + P], htok[:, i, k * P:k * P + P], sel[:, i, :],
                                           start=i == 0, stop=i == TT - 1)
                    mm.then_inc(mm_done, 1)

                def scatter(n):
                    half, i = n // TT, n % TT
                    begin(("o", n))
                    pe.matmul(bank(("o", n)), selT[:, i * P:i * P + P], ys[:, half * 512:half * 512 + 512],
                              start=True, stop=True).then_inc(mm_done, 1)

                def both(g, j, lhs, k, col):
                    begin(g)
                    for c in range(k):
                        for e in range(2):
                            s = slice(e * CAP, e * CAP + CAP)
                            mm = pe.matmul(bank(g)[s, :], lhs[:, c, s], weight(e, j, k)[:, c, col:col + 512],
                                           start=c == 0, stop=c == k - 1)
                    mm.then_inc(mm_done, 1)

                pe.wait_ge(act_out, it * NA3 + AI3["y", 1])
                pe.wait_ge(vec_out, it * NV3 + VI3["st",])
                for n in range(4):
                    scatter(n)
                pe.wait_ge(act_out, (it + 1) * NA3 + AI3["x", 0])
                pe.wait_ge(vec_out, (it + 1) * NV3 + VI3["x", 1])
                both(("gt",), 0, xe, KD, 0)
                both(("up",), 1, xe, KD, 0)
                for n in range(4, 8):
                    scatter(n)
                begin(("ht",))
                pe.wait_ge(vec_out, (it + 1) * NV3 + VI3["up",])
                for f in range(KF):
                    mm = pe.transpose(bank(("ht",))[:, f * P:f * P + P], he[:, f * P:f * P + P], ident[:, :])
                mm.then_inc(mm_done, 1)
                begin(("st",))
                for i in range(TT):
                    mm = pe.transpose(bank(("st",))[:, i * P:i * P + P], selw[:, i, :], ident[:, :])
                mm.then_inc(mm_done, 1)
                pe.wait_ge(act_out, (it + 1) * NA3 + AI3["ht",])
                for half in range(2):
                    both(("y", half), 2, hT, KF, half * 512)
            done = n_rounds * PAIRS + 1
            pe.wait_ge(act_out, done * NA3)
            pe.wait_ge(vec_out, done * NV3)
            for n in range(8):
                i, half = n // 2, n % 2
                pe.matmul(T.ps[n // 2][:, n % 2, :], selT[:, i * P:i * P + P], ys[:, half * 512:half * 512 + 512],
                          start=True, stop=True).then_inc(mm_done, 1)

        @block.scalar
        def _(act):
            act.sem_inc(act_out, NA3)
            act.wait_ge(route_step, T.route_group)
            act.activation(ge[:, :, :], ge[:, :, :], ACT.Exp).then_inc(group_exp, 1)
            act.wait_ge(route_step, T.route_pair)
            act.activation(e2[:, :], m2[:, :], ACT.Exp).then_inc(pair_exp, 1)
            act.wait_ge(rounds_ready, 1)
            n_rounds = act.value_load(rounds[0:1, 0:1], min_val=1, max_val=ROUNDS_MAX)
            with act.Fori(0, n_rounds) as rnd, act.Fori(0, PAIRS) as pair:
                it = rnd * PAIRS + pair

                def wait_mm(g):
                    act.wait_ge(mm_done, (it + 1) * NG3 + GI3[g] + 1)

                wait_mm(("x", 0))
                act.activation(xe[:, 0:4, :], bank(("x", 0)).rearrange("p (k n) -> p k n", k=4), ACT.Copy).then_inc(act_out, 1)
                wait_mm(("gt",))
                act.activation(sg[:, :], bank(("gt",)), ACT.Silu).then_inc(act_out, 1)
                wait_mm(("ht",))
                act.activation(hT[:, :, :], bank(("ht",)).rearrange("p (f n) -> p f n", f=KF), ACT.Copy).then_inc(act_out, 1)
                for half in range(2):
                    wait_mm(("y", half))
                    act.activation(ys[:, half * 512:half * 512 + 512], bank(("y", half)), ACT.Copy).then_inc(act_out, 1)
            done = n_rounds * PAIRS + 1
            for i in range(TT):
                s = ssum[:, i:i + 1]
                act.wait_ge(vec_out, done * NV3 + 2 * i + 2)
                if i:
                    act.wait_ge(rstd_done, i)
                act.activation(sqo[:, :], acc[:, i, :], ACT.Square, accum_out=s).then_inc(ss_done, 1)
                act.wait_ge(ss_done, 2 * i + 1)
                act.activation(s, s, ACT.Ln, bias=eps[:, :], scale=1.0 / D).then_inc(ss_done, 1)
                act.wait_ge(ss_done, 2 * i + 2)
                act.activation(s, s, ACT.Exp, scale=-0.5).then_inc(rstd_done, 1)


def build(nc, dram, out):
    T = Tiles()
    with ExitStack() as ctx:
        def sb(name, shape):
            return ctx.enter_context(nc.sbuf_tensor(name, shape, F32))

        def sem(name):
            return ctx.enter_context(nc.semaphore(name))

        T.hT = sb("hT", [P, KD, L])
        T.rstd = sb("rstd", [P, 3, L])
        T.qn = sb("qn", [P, HEADS, L])
        T.kn = sb("kn", [P, HEADS, L])
        T.memT, T.memn = (t[:, :, :].rearrange("p h n -> p (h n)")[:, 0:KD * MEM].rearrange("p (k n) -> p k n", k=KD)
                          for t in (T.kn, T.qn))
        T.ring = sb("ring", [P, RING, PANEL])
        T.ones = sb("ones", [P, P])
        T.ident = sb("ident", [P, P])
        T.eps = sb("eps", [P, 1])
        T.lw = sb("lw", [P, LW])
        T.ps = [ctx.enter_context(nc.psum_tensor(f"ps{i}", [P, 2, 512], F32)) for i in range(NPS)]
        T.logits = sb("logits", [P, TT * NL])
        T.htok = T.ring[:, 0:2, :].rearrange("p a (b n) -> p (a b) n", b=2)
        T.xtok = T.ring[:, 2:4, :].rearrange("p a (b n) -> p (a b) n", b=2)
        T.setup = sem("setup")
        T.N_SETUP = 4
        T.lw_ready = sem("lw_ready")
        T.w_ready = [sem(f"w_ready{i}") for i in range(RING)]
        T.mem_loaded = sem("mem_loaded")
        T.memn_ready = sem("memn_ready")
        with nc.Block() as block:
            @block.gpsimd
            def _(pool):
                pool.memset(T.ones[:, :], 1.0).then_inc(T.setup, 1)
                pool.memset(T.eps[:, :], EPS).then_inc(T.setup, 1)
                pool.memset(T.ident[:, :], 0.0).then_inc(T.setup, 1)
                pool.wait_ge(T.setup, 3)
                pool.affine_select(out=T.ident[:, :], in_=T.ident[:, :], compare_op=ALU.not_equal, fill=1.0,
                                   base=0, pattern=[[-1, P]], channel_multiplier=1).then_inc(T.setup, 1)
        first_block(nc, dram, T, sem)
        second_block(nc, dram, T, sem)
        experts(nc, dram, T, sem, out)


def kernel(**inputs):
    import numpy as np
    import concourse.bacc as bacc
    from concourse.bass_utils import run_bass_kernel_spmd

    a = {k: np.asarray(x) for k, x in inputs.items()}

    def rows(x):
        return x.reshape(-1, P).T

    def cols(*parts):
        return np.concatenate(parts, axis=-1)

    def diag(x):
        n = x.shape[0]
        y = np.zeros((n // 2, P, P), x.dtype)
        y[:, :64, :64], y[:, 64:, 64:] = x[0::2], x[1::2]
        return cols(*y)

    arrays = {}
    arrays["hT"] = np.concatenate([a["meta_tokens"], a["x"][0]], axis=0).T
    w = a["w_in"]
    arrays["win"] = cols(w[..., 1024:1664], w[..., 1664:1728], w[..., 0:256], w[..., 512:768],
                         w[..., 256:512], w[..., 768:1024], w[..., 1728:2240])
    w = a["w_uq"].reshape(LAYERS, QR, HEADS, P + ROPE)
    arrays["wuq"] = cols(w[..., :P].reshape(LAYERS, QR, -1), w[..., P:P + 32].reshape(LAYERS, QR, -1),
                         w[..., P + 32:].reshape(LAYERS, QR, -1))
    w = a["w_ukv"].reshape(LAYERS, KVR, HEADS, 2 * P)
    arrays["wukv"] = cols(w[..., :P].reshape(LAYERS, KVR, -1), w[..., P:].reshape(LAYERS, KVR, -1))
    arrays["wout"] = a["w_out"]
    small = [cols(rows(a["norm_w"][l]), rows(a["pool_scale"][l]), rows(a["q_norm_w"][l]), rows(a["kv_norm_w"][l]),
                  diag(a["fourier_w"][l]), diag(a["pool_w"][l])) for l in range(LAYERS)]
    last = np.zeros_like(small[0])
    last[:, 0:KD] = rows(a["final_norm_w"])
    last[:, LW_VEC:LW_WR] = cols(rows(a["ln1_w_2"]), *(rows(a["conv_w_2"][0, j]) for j in range(CONV)), rows(a["conv_b_2"]), rows(a["rnn_ba_2"]),
                         rows(a["rnn_bx_2"]), rows(a["rnn_lambda_2"]), rows(a["gn_rnn_w_2"]), rows(a["gn_att_w_2"]), rows(a["ln2_w_2"]),
                         rows(a["mem_norm_w_2"]), rows(a["ln3_w_2"]))
    last[:, LW_WR:LW_RB] = cols(a["router_group_w_2"][0], *a["router_expert_w_2"][0]).reshape(KD, P, NL).transpose(1, 0, 2).reshape(P, -1)
    last[:, LW_RB:LW_RB + TT * NL] = np.tile(cols(a["router_group_b_2"][0], *a["router_expert_b_2"][0]), TT)
    arrays["lw"] = np.stack(small + [last])

    arrays["memT"] = a["mem_2"][0].T
    for name, source in (("xk", "xk_w_2"), ("xv", "xv_w_2"), ("xq", "xq_w_2"), ("xo", "xo_w_2"), ("win2", "w_in_2"), ("wout2", "w_out_2")):
        arrays[name] = a[source][0]
    arrays["wab"] = cols(diag(a["rnn_wa_2"][0]), diag(a["rnn_wx_2"][0])).reshape(P, 2 * KH, P)
    distance = np.arange(P)[:, None] + (SEQ - P) - np.arange(SEQ)[None, :]
    arrays["bias"] = a["rel_bias_2"][0][:, np.clip(distance, -P, P) + P]

    arrays["eg"], arrays["eu"], arrays["ed"] = a["expert_gate_w_2"][0], a["expert_up_w_2"][0], a["expert_down_w_2"][0]
    arrays["fw"] = a["final_norm_w_2"]

    n = np.arange(L)
    angle = 2 * np.pi * ((n[:, None] * n[None, :]) % L) / L
    tables = np.zeros((4, NT * P, LH))
    for half in range(2):
        tables[2 * half, :L] = np.cos(angle)[:, half * LH:half * LH + LH]
        tables[2 * half + 1, :L] = np.sin(angle)[:, half * LH:half * LH + LH]
    arrays["dft"] = tables.astype(np.float32)
    c = np.arange(64)
    angle = 2 * np.pi * ((c[:, None] * c[None, :]) % 64) / 64
    both = np.zeros((P, 2, P))
    for b in range(2):
        s = slice(64 * b, 64 * b + 64)
        both[s, 0, s] = np.cos(angle) / math.sqrt(L * 64)
        both[s, 1, s] = -np.sin(angle) / math.sqrt(L * 64)
    arrays["cdsd"] = both.astype(np.float32)
    inv = (1.0 / (np.float32(10000.0) ** (np.arange(0, ROPE, 2, dtype=np.float32) / np.float32(ROPE)))).astype(np.float32)
    angle = n.astype(np.float32)[:, None] * inv[None, :]
    arrays["rope"] = np.stack([np.tile(np.cos(angle).T, (4, 1)), np.tile(np.sin(angle).T, (4, 1))], axis=1).astype(np.float32)
    count = np.zeros((P, 2, L))
    for g, win in enumerate((2, 4, 8, 16)):
        have = np.clip(n + win // 2, 0, L) - np.clip(n - win // 2, 0, L)
        count[64 * (g % 2):64 * (g % 2) + 64, g // 2] = 1.0 / have
    arrays["cnt"] = count.astype(np.float32)

    nc = bacc.Bacc("TRN2", target_bir_lowering=False, num_devices=1)
    dram, fed = {}, {}
    for name, x in arrays.items():
        fed[f"in_{name}"] = np.ascontiguousarray(x)
        dram[name] = nc.dram_tensor(f"in_{name}", x.shape, mybir.dt.from_np(x.dtype), kind="ExternalInput").ap()
    out = nc.dram_tensor("out_0", (1, SEQ, D), F32, kind="ExternalOutput").ap()
    build(nc, dram, out)
    r = run_bass_kernel_spmd(nc, [fed], core_ids=[0])
    return r.results[0]["out_0"]
```

```python
import math
from contextlib import ExitStack

import concourse.bass as bass
from concourse import mybir

F32 = mybir.dt.float32
F32R = mybir.dt.float32r
ALU = mybir.AluOpType
ACT = mybir.ActivationFunctionType
AX = mybir.AxisListType

P = 128
D = 1024
KD = D // P
SEQ = 512
META = 16
L = SEQ + META
LH = L // 2
LAYERS = 2
LT = [(i * P, min(P, L - i * P)) for i in range(-(-L // P))]
NT = len(LT)
HEADS = 4
QR, KVR = 384, 256
KQ, KKV = QR // P, KVR // P
ROPE = 64
EPS = 1e-6
SCALE1 = (P + ROPE) ** -0.5

RING = 4
PANEL = 2048
NPS = 4

def first_groups():
    g = [("u", 0), ("u", 1), ("rs", 0), ("u", 2), ("u", 3), ("u", 4), ("kr", 0), ("fi", 0), ("fi", 1),
         ("rs", 1), ("rs", 2), ("pi", 0), ("pi", 1)]
    g += [("ga", m) for m in range(8)]
    g += [("q", h) for h in range(HEADS)] + [("qr", 0), ("qr", 1)]
    g += [("kn", h) for h in range(HEADS)] + [("v", i) for i in range(3)]
    g += [("ab", 0)] + [("pq", i) for i in range(NT)] + [("yf", 0), ("yf", 1), ("yp", 0), ("yp", 1)]
    def s(h): return [("s", h, i) for i in range(NT)]
    def t(h): return [("t", h, j) for j in range(NT)]
    g += s(0) + s(1) + t(0) + s(2) + [("a", 0)] + t(1) + s(3) + [("a", 1)] + t(2) + [("a", 2)] + t(3) + [("a", 3)]
    g += [("o", m) for m in range(8)]
    return g

G1 = first_groups()
assert len(G1) % NPS == 0
ACT_OWNS1 = ("rs", "q", "kn", "v", "pq", "s", "t")
V1 = [g for g in G1 if g[0] not in ACT_OWNS1]
A1 = [g for g in G1 if g[0] in ACT_OWNS1]
GI1 = {g: n for n, g in enumerate(G1)}
VI1 = {g: n + 1 for n, g in enumerate(V1)}
AI1 = {g: n + 1 for n, g in enumerate(A1)}
NG1, NV1, NA1 = len(G1), len(V1), len(A1)

W1 = ([("win", i) for i in range(9)] + [("wuq", 0), ("wuq", 1), ("wukv", 0)]
      + [("dft", i) for i in range(4)] + [("wout", i) for i in range(4)])
NW1 = len(W1)
WI1 = {w: n for n, w in enumerate(W1)}
assert NW1 % RING == 0
W1_USER = {("wuq", 0): ("q", 3), ("wuq", 1): ("qr", 1), ("wukv", 0): ("v", 2)} | {("dft", i): ("yf", 1) for i in range(4)}
WIN_CHUNKS = ([("u", m) for m in range(5)] + [("kr", 0), ("fi", 0), ("fi", 1), ("pi", 0), ("pi", 1)]
              + [("ga", m) for m in range(8)])
NWIN = len(WIN_CHUNKS)
SPLIT1 = WIN_CHUNKS + [("o", m) for m in range(8)]
NSPLIT = len(SPLIT1)
assert NSPLIT % 2 == 0
WIN_COLS = [(0, 256), (256, 256), (512, 192)] + [(704 + 256 * i, 256) for i in range(6)]
LW_NORM, LW_POOL, LW_Q, LW_KV, LW_FW, LW_PW = 0, 8, 10, 13, 15, 271
LW = 527


MEM = 256
DH = 512
KH = DH // P
AH = 8
XH = 4
TT = SEQ // P
NE, NGRP = 32, 4
NL = NGRP + NE
CONV = 4


CAP = 64
PAIRS = NE // 2
EPG = NE // NGRP
FE = 512
KF = FE // P
ROUNDS_MAX = SEQ // CAP


def second_groups():
    g = [("kx", 0), ("kx", 1), ("n", 1), ("kx", 2)]
    g += [(n, c) for n in ("xr", "xg", "qa", "ka", "va") for c in range(2)]
    g += [("gt", c) for c in range(KH)]
    def s(h): return [("sA", h), ("sB", h)]
    def t(h): return [("tA", h), ("tB", h)]
    g += s(0) + s(1) + [("kx", 3)]
    for h in range(AH):
        g += t(h) + (s(h + 2) if h + 2 < AH else []) + [("at", h)]
    g += [("vx", 0), ("n", 2), ("vx", 1)] + [("o", m) for m in range(4)] + [("vx", 2), ("n", 3), ("vx", 3)]
    g += [("qx", m) for m in range(4)] + [("sx", 0), ("sx", 1)]
    for h in range(XH):
        g += [("tx", h)] + ([("sx", h + 2)] if h + 2 < XH else []) + [("ax", h)]
    g += [("xo", m) for m in range(4)] + [("xt", 0), ("n", 4)] + [("xt", i) for i in range(1, TT)]
    g += [("lg",)] + [("ht", i) for i in range(TT)] + [("rank",)]
    return g


G2 = second_groups()
ACT_OWNS2 = ("n", "kx", "qa", "ka", "gt", "tA", "tB", "qx", "sx", "tx", "xt", "ht")
GI2 = {g: n for n, g in enumerate(G2)}
VI2 = {g: n + 1 for n, g in enumerate(g for g in G2 if g[0] not in ACT_OWNS2)}
AI2 = {g: n + 1 for n, g in enumerate(g for g in G2 if g[0] in ACT_OWNS2)}
W2 = ([("xk", 0), ("xk", 1), ("xk", 2)] + [("win2", i) for i in range(10)] + [("xk", 3), ("xv", 0), ("xv", 1)]
      + [("wout2", i) for i in range(4)] + [("xv", 2), ("xv", 3)] + [("xq", i) for i in range(4)] + [("xo", i) for i in range(4)])
WI2 = {w: n for n, w in enumerate(W2)}
def slot2(n):
    return n + 2 if n < 2 else n % 2


SPLIT2 = [g for g in G2 if g[0] in ("xr", "xg", "qa", "ka", "o", "qx", "xo") for _ in range(2)]
PANEL2 = {}
for _j, _g in enumerate(SPLIT2[::2]):
    PANEL2[_g] = ("win2", _j) if _j < 8 else (("wout2", "xq", "xo")[(_j - 8) // 4], _j % 4)
CHUNK2 = {panel: 2 * n for n, panel in enumerate(PANEL2.values())}
W2_USER = {("xk", i): ("kx", i) for i in range(4)} | {("xv", i): ("vx", i) for i in range(4)} | {("win2", 8): ("va", 1), ("win2", 9): ("va", 1)}
V2 = {}
for _name, _n in (("ln1", KD), ("cw", CONV * KH), ("cb", KH), ("ba", KH), ("bx", KH), ("lam", KH), ("gnr", KH), ("gna", KH),
                  ("ln2", KD), ("mem", KD), ("ln3", KD)):
    V2[_name] = sum(n for _, n in V2.values()), _n
NV2 = sum(n for _, n in V2.values())
LW_VEC = KD
LW_WR = LW_VEC + NV2
LW_RB = LW_WR + KD * NL
assert LW_RB + TT * NL <= LW
SOFF = {3: 0, 2: 512, 1: 896, 0: 1152}
SBW = 1280
NORMS = ["first", "ln1", "mixed", "ln2", "ln3"]
TINY = 1e-18


def panel_view(ring, n):
    return ring[:, slot2(n), :].rearrange("p (k n) -> p k n", k=KD)


def panel_source(dram, name, i):
    return dram[name][:, 256 * i:256 * i + 256].rearrange("(k p) n -> p k n", p=P)


class Tiles:
    pass


def first_block(nc, dram, T, sem):
    ctx = ExitStack()
    with ctx:
        def sb(name, shape, dt=F32):
            return ctx.enter_context(nc.sbuf_tensor(name, shape, dt))

        hT, ring, ones, ident, eps, lw, ps = T.hT, T.ring, T.ones, T.ident, T.eps, T.lw, T.ps
        x_hi = sb("x_hi", [P, KD, L], F32R)
        x_lo = T.x_lo
        w_split = sb("w_split", [P, 2, 2, KD * P], F32R)
        gate = T.area_u0[:, 0:8 * L].rearrange("p (m n) -> p m n", m=8)
        mix = gate
        sq = gate
        rstd = T.rstd
        cq = sb("cq", [P, KQ + KKV, L])
        krE = sb("krE", [P, L])
        krO = sb("krO", [P, L])
        rt = T.area_u1[:, 512:512 + 4 * L].rearrange("p (c n) -> p c n", c=4)
        qn, kn = T.qn, T.kn
        qr = sb("qr", [P, 2, L])
        v = T.area_g[:, 2 * NT * L:2 * NT * L + 6 * DH].rearrange("p (i n) -> p i n", i=6)
        ab = T.area_u1[:, 0:512].rearrange("p (c n) -> p c n", c=2)
        pq = T.area_u1[:, 512:512 + NT * 512].rearrange("p (i c n) -> p i c n", i=NT, c=2)
        PW = L + 32
        pin = T.area_u1[:, 512 + NT * 512:512 + NT * 512 + 2 * PW].rearrange("p (c n) -> p c n", c=2)
        rope = sb("rope", [P, 2, L])
        cnt = sb("cnt", [P, 2, L])
        cdsd = sb("cdsd", [P, 2, P])
        pbuf = T.area_g[:, 0:2 * NT * L]
        probs = pbuf[:, :].rearrange("p (b i n) -> p b i n", b=2, i=NT)
        s2 = pbuf[:, 0:2 * PW].rearrange("p (c n) -> p c n", c=2)
        s4 = pbuf[:, 2 * PW:4 * PW].rearrange("p (c n) -> p c n", c=2)
        s8 = pbuf[:, 4 * PW:5 * PW]
        pr = pbuf[:, 5 * PW:5 * PW + 2 * L].rearrange("p (c n) -> p c n", c=2)
        fin = pbuf[:, 5 * PW + 2 * L:5 * PW + 4 * L].rearrange("p (c n) -> p c n", c=2)
        pT = cq
        T.mem_sq = pT[:, :, :].rearrange("p j n -> p (j n)")[:, 0:KD * MEM].rearrange("p (k n) -> p k n", k=KD)
        nmax = sb("nmax", [P, HEADS * NT])
        rsum = sb("rsum", [P, HEADS * NT])
        rinv = sb("rinv", [P, HEADS * NT])
        qws = sb("qws", [P, KQ])

        mm_done = sem("mm_done")
        vec_out = sem("vec_out")
        act_out = sem("act_out")
        w_ready = T.w_ready
        lw_ready = T.lw_ready
        h_loaded = [sem(f"h_loaded{k}") for k in range(KD // 2)]
        const_ready = sem("const_ready")
        zeroed = sem("zeroed")
        sq_ready = sem("sq_ready")
        sum_step = sem("sum_step")
        hsum_step = sem("hsum_step")
        xhi_ready = sem("xhi_ready")
        whi_ready = sem("whi_ready")
        wlo_ready = sem("wlo_ready")
        mixhi_ready = sem("mixhi_ready")
        mix_ready = sem("mix_ready")
        rstd_ready = sem("rstd_ready")
        xw_ready = sem("xw_ready")
        cn_ready = sem("cn_ready")
        k_step = sem("k_step")
        kr_ready = sem("kr_ready")
        qr_ready = sem("qr_ready")
        qws_ready = sem("qws_ready")
        pool_step = sem("pool_step")
        silu_done = sem("silu_done")
        max_ready = sem("max_ready")
        inv_ready = sem("inv_ready")
        probs_ready = sem("probs_ready")

        NSQ = KD + KQ + KKV
        SUMS = {1: (0, KQ, KD, 0), 2: (KQ, KKV, KD + KQ, KQ - 1)}
        NSUM = KQ + KKV - 2
        NPOOL = 9
        NEXP = HEADS * NT

        def raw(n):
            name, i = ("win", n // 2) if n < NWIN else ("wout", (n - NWIN) // 2)
            width = WIN_COLS[i][1] if name == "win" else 256
            m = 64 if SPLIT1[n] == ("kr", 0) else P
            w = ring[:, WI1[name, i] % RING, 0:KD * width].rearrange("p (k n) -> p k n", k=KD)
            return w[:, :, n % 2 * P:n % 2 * P + m]

        def split(n, part):
            m = 64 if SPLIT1[n] == ("kr", 0) else P
            return w_split[:, n % 2, part, :].rearrange("p (k n) -> p k n", k=KD)[:, :, 0:m]

        def pst(g):
            return ps[GI1[g] % NPS]

        def phalf(g, p0=0, p1=P):
            return pst(g)[p0:p1, :, 0:LH]

        def pflat(g):
            return pst(g)[:, :, :].rearrange("p a n -> p (a n)")

        def two(ap):
            return ap.rearrange("p (a n) -> p a n", a=2)

        block = ctx.enter_context(nc.Block())

        @block.sync
        def _(sp):
            def wait_slot(n, layer):
                name, i = W1[n - RING]
                back = layer + (0 if n < RING else 1)
                if name in ("win", "wout"):
                    last = 2 * i + 1 + (NWIN if name == "wout" else 0)
                    sp.wait_ge(wlo_ready, back * NSPLIT + last + 1)
                else:
                    sp.wait_ge(mm_done, back * NG1 + GI1[W1_USER[name, i]] + 1)

            with sp.Fori(0, LAYERS) as layer:
                for n, (name, i) in enumerate(W1):
                    if n == 1:
                        sp.wait_ge(h_loaded[-1], 16)
                    slot = ring[:, n % RING, :]
                    wait_slot(n, layer)
                    if name == "dft":
                        src = dram["dft"][i].rearrange("(k p) n -> p k n", p=P)
                        dst = slot[:, 0:NT * LH].rearrange("p (k n) -> p k n", k=NT)
                    else:
                        k = {"win": KD, "wuq": KQ, "wukv": KKV, "wout": KD}[name]
                        c0, c = {"win": WIN_COLS, "wuq": [(0, 512), (512, 256)], "wukv": [(0, 1024)],
                                 "wout": [(256 * m, 256) for m in range(4)]}[name][i]
                        src = dram[name][bass.ds(layer, 1), :, c0:c0 + c].rearrange("a (k p) n -> p (a k) n", p=P)
                        dst = slot[:, 0:k * c].rearrange("p (k n) -> p k n", k=k)
                    sp.dma_start(dst, src).then_inc(w_ready[n % RING], 16)
            sp.wait_ge(mm_done, LAYERS * NG1 + GI1["a", HEADS - 1] + 1)
            sp.dma_start(T.mem_in, dram["memT"].rearrange("(k p) n -> p k n", p=P)).then_inc(T.mem_loaded, 16)
            for n in (2, 3, 0, 1):
                name, i = W2[n]
                wait_slot(slot2(n), LAYERS)
                sp.dma_start(panel_view(ring, n), panel_source(dram, name, i)).then_inc(w_ready[slot2(n)], 16)

        @block.gpsimd
        def _(pool):
            pool.dma_start(lw[:, :], dram["lw"][0]).then_inc(lw_ready, 16)
            pool.wait_ge(h_loaded[-1], 16)
            pool.dma_start(rope[:, :, :], dram["rope"]).then_inc(const_ready, 16)
            pool.dma_start(cnt[:, :, :], dram["cnt"]).then_inc(const_ready, 16)
            pool.dma_start(cdsd[:, :, :], dram["cdsd"]).then_inc(const_ready, 16)
            pool.memset(krE[:, :], 0.0).then_inc(zeroed, 1)
            pool.memset(krO[:, :], 0.0).then_inc(zeroed, 1)
            pool.memset(pin[:, :, 0:16], 0.0).then_inc(zeroed, 1)
            pool.memset(pin[:, :, 16 + L:PW], 0.0).then_inc(zeroed, 1)
            pool.wait_ge(zeroed, 4)

            def add_squares(squares, adds):
                for c in range(1, KD):
                    pool.wait_ge(sq_ready, squares + c + 1)
                    if c > 1:
                        pool.wait_ge(hsum_step, adds + c - 1)
                    pool.tensor_tensor(sq[:, 0, :], sq[:, 0, :], sq[:, c, :], ALU.add).then_inc(hsum_step, 1)

            with pool.Fori(0, LAYERS) as layer:
                add_squares(layer * NSQ, layer * (KD - 1))
                W = slice(16, 16 + L)

                def step(n):
                    pool.wait_ge(pool_step, layer * NPOOL + n)

                pool.wait_ge(const_ready, 48)
                pool.wait_ge(vec_out, (layer + 1) * NV1 + VI1["pi", 1])
                pool.tensor_tensor(s2[:, :, 1:PW], pin[:, :, 1:PW], pin[:, :, 0:PW - 1], ALU.add).then_inc(pool_step, 1)
                step(1)
                pool.tensor_tensor(s4[:, :, 2:PW - 1], s2[:, :, 3:PW], s2[:, :, 1:PW - 2], ALU.add).then_inc(pool_step, 1)
                step(2)
                pool.tensor_tensor(s8[:, 4:PW - 3], s4[:, 1, 6:PW - 1], s4[:, 1, 2:PW - 5], ALU.add).then_inc(pool_step, 1)
                step(3)
                pool.tensor_tensor(pr[64:128, 1, :], s8[64:128, 20:20 + L], s8[64:128, 12:12 + L], ALU.add).then_inc(pool_step, 1)
                step(4)
                pool.tensor_tensor(pr[0:64, 0, :], s2[0:64, 0, W], cnt[0:64, 0, :], ALU.mult).then_inc(pool_step, 1)
                step(5)
                pool.tensor_tensor(pr[64:128, 0, :], s4[64:128, 0, W], cnt[64:128, 0, :], ALU.mult).then_inc(pool_step, 1)
                step(6)
                pool.tensor_tensor(pr[0:64, 1, :], s8[0:64, W], cnt[0:64, 1, :], ALU.mult).then_inc(pool_step, 1)
                step(7)
                pool.tensor_tensor(pr[64:128, 1, :], pr[64:128, 1, :], cnt[64:128, 1, :], ALU.mult).then_inc(pool_step, 1)
                step(8)
                pool.tensor_tensor(pr[:, :, :], pr[:, :, :], pin[:, :, W], ALU.subtract).then_inc(pool_step, 1)
                pool.wait_ge(vec_out, (layer + 1) * NV1 + VI1["yp", 1])
                pool.dma_start(lw[:, :], dram["lw"][bass.ds(layer + 1, 1), :, :].rearrange("a p n -> (a p) n")).then_inc(lw_ready, 16)
            add_squares(LAYERS * NSQ + KD, LAYERS * (KD - 1))

        @block.tensor
        def _(pe):
            pe.sem_inc(mm_done, NG1)
            pe.wait_ge(T.setup, T.N_SETUP)
            with pe.Fori(0, LAYERS) as layer:

                def begin(g):
                    prev = G1[(GI1[g] - NPS) % NG1]
                    s, idx, per = (act_out, AI1, NA1) if prev in AI1 else (vec_out, VI1, NV1)
                    pe.wait_ge(s, (layer + (0 if GI1[g] < NPS else 1)) * per + idx[prev])

                def panel(name, i):
                    n = WI1[name, i]
                    pe.wait_ge(w_ready[n % RING], (layer * (NW1 // RING) + n // RING + 1) * 16)
                    return ring[:, n % RING, :]

                def vec(g):
                    pe.wait_ge(vec_out, (layer + 1) * NV1 + VI1[g])

                def act(g):
                    pe.wait_ge(act_out, (layer + 1) * NA1 + AI1[g])

                def project(g, w, k, rhs):
                    begin(g)
                    for c in range(k):
                        for a in range(2):
                            mm = pe.matmul(pst(g)[:, a, 0:LH], w[:, c, :], rhs[:, c, a * LH:a * LH + LH],
                                           start=c == 0, stop=c == k - 1)
                    mm.then_inc(mm_done, 1)

                def project_split(g, ready=None):
                    n = SPLIT1.index(g)
                    m = 64 if g == ("kr", 0) else P
                    begin(g)
                    pe.wait_ge(wlo_ready, (layer + 1) * NSPLIT + n + 1)
                    for c in range(KD):
                        if ready is not None:
                            pe.wait_ge(ready, layer * KD + c + 1)
                        for t, (part, x) in enumerate(((0, x_hi), (0, x_lo), (1, x_hi))):
                            for a in range(2):
                                mm = pe.matmul(pst(g)[0:m, a, 0:LH], split(n, part)[:, c, :], x[:, c, a * LH:a * LH + LH],
                                               start=c == 0 and t == 0, stop=c == KD - 1 and t == 2)
                    mm.then_inc(mm_done, 1)

                def sums(r):
                    g = ("rs", r)
                    begin(g)
                    if r == 0:
                        c0 = 0
                        pe.wait_ge(hsum_step, layer * (KD - 1) + KD - 1)
                    else:
                        c0, k, _, adds = SUMS[r]
                        pe.wait_ge(sum_step, layer * NSUM + adds + k - 1)
                    for a in range(2):
                        mm = pe.matmul(pst(g)[:, a, 0:LH], ones[:, :], sq[:, c0, a * LH:a * LH + LH], start=True, stop=True)
                    mm.then_inc(mm_done, 1)

                for n, g in enumerate(WIN_CHUNKS):
                    project_split(g, xw_ready if n == 0 else None)
                    if g == ("u", 1):
                        sums(0)
                    if g == ("fi", 1):
                        sums(1)
                        sums(2)

                pe.wait_ge(cn_ready, layer * (KQ + KKV) + KQ + KKV)
                w = panel("wuq", 0)[:, 0:KQ * 512].rearrange("p (k n) -> p k n", k=KQ)
                for h in range(HEADS):
                    project(("q", h), w[:, :, h * P:h * P + P], KQ, cq)
                w = panel("wuq", 1)[:, 0:KQ * 256].rearrange("p (k n) -> p k n", k=KQ)
                for c in range(2):
                    project(("qr", c), w[:, :, c * P:c * P + P], KQ, cq)
                w = panel("wukv", 0).rearrange("p (k n) -> p k n", k=KKV)
                for h in range(HEADS):
                    project(("kn", h), w[:, :, h * P:h * P + P], KKV, cq[:, KQ:, :])
                for g in range(3):
                    begin(("v", g))
                    for b, (t0, m) in enumerate(LT[2 * g:2 * g + 2]):
                        for c in range(KKV):
                            mm = pe.matmul(pst(("v", g))[0:m, b, :], cq[:, KQ + c, t0:t0 + m], w[:, c, 512:1024],
                                           start=c == 0, stop=c == KKV - 1)
                    mm.then_inc(mm_done, 1)

                begin(("ab", 0))
                pe.wait_ge(lw_ready, layer * 16 + 16)
                pe.wait_ge(const_ready, 48)
                for c in range(2):
                    for f in range(2):
                        mm = pe.matmul(pst(("ab", 0))[:, c, f * P:f * P + P], cdsd[:, f, :],
                                       lw[:, LW_FW + c * P:LW_FW + c * P + P], start=True, stop=True)
                mm.then_inc(mm_done, 1)
                vec(("ab", 0))
                for i, (t0, m) in enumerate(LT):
                    begin(("pq", i))
                    for c in range(2):
                        mm = pe.matmul(pst(("pq", i))[0:m, c, 0:256], fin[:, c, t0:t0 + m], ab[:, c, :],
                                       start=True, stop=True)
                    mm.then_inc(mm_done, 1)
                act(("pq", NT - 1))
                begin(("yf", 0))
                begin(("yf", 1))
                for a in range(2):
                    for f in range(2):
                        tab = panel("dft", 2 * a + f)[:, 0:NT * LH].rearrange("p (k n) -> p k n", k=NT)
                        for c in range(2):
                            for i, (t0, m) in enumerate(LT):
                                mm = pe.matmul(pst(("yf", c))[:, a, 0:LH], pq[0:m, i, c, f * P:f * P + P],
                                               tab[0:m, i, :], start=f == 0 and i == 0, stop=f == 1 and i == NT - 1)
                            if a == 1 and f == 1:
                                mm.then_inc(mm_done, 1)

                pe.wait_ge(pool_step, layer * NPOOL + NPOOL)
                for c in range(2):
                    g = ("yp", c)
                    begin(g)
                    for a in range(2):
                        mm = pe.matmul(pst(g)[:, a, 0:LH], lw[:, LW_PW + c * P:LW_PW + c * P + P],
                                       pr[:, c, a * LH:a * LH + LH], start=True, stop=True)
                    mm.then_inc(mm_done, 1)

                def scores(h):
                    kr = krO if h % 2 else krE
                    for i, (t0, m) in enumerate(LT):
                        g = ("s", h, i)
                        begin(g)
                        for a in range(2):
                            keys = slice(a * LH, a * LH + LH)
                            pe.matmul(pst(g)[0:m, a, 0:LH], qn[:, h, t0:t0 + m], kn[:, h, keys], start=True, stop=False)
                            mm = pe.matmul(pst(g)[0:m, a, 0:LH], qr[:, h // 2, t0:t0 + m], kr[:, keys], start=False, stop=True)
                        mm.then_inc(mm_done, 1)

                def turn(h):
                    pe.wait_ge(probs_ready, layer * NEXP + h * NT + NT)
                    for j, (k0, kj) in enumerate(LT):
                        g = ("t", h, j)
                        begin(g)
                        for i, (t0, m) in enumerate(LT):
                            mm = pe.transpose(pflat(g)[0:kj, t0:t0 + m], probs[0:m, h % 2, i, k0:k0 + kj], ident[0:m, 0:m])
                        mm.then_inc(mm_done, 1)

                def attend(h):
                    g = ("a", h)
                    begin(g)
                    act(("t", h, NT - 1))
                    for j, (k0, kj) in enumerate(LT):
                        for a in range(2):
                            mm = pe.matmul(pst(g)[:, a, 0:LH], v[0:kj, j, h * P:h * P + P], pT[0:kj, j, a * LH:a * LH + LH],
                                           start=j == 0, stop=j == NT - 1)
                    mm.then_inc(mm_done, 1)

                act(("v", 2))
                pe.wait_ge(kr_ready, layer + 1)
                pe.wait_ge(qr_ready, layer + 1)
                scores(0)
                scores(1)
                turn(0)
                scores(2)
                attend(0)
                turn(1)
                scores(3)
                attend(1)
                turn(2)
                attend(2)
                turn(3)
                attend(3)

                for m in range(KD):
                    project_split(("o", m), mix_ready if m == 0 else None)

            pe.wait_ge(vec_out, LAYERS * NV1 + VI1["o", 4])
            for c in range(KD):
                pe.wait_ge(sq_ready, LAYERS * NSQ + c + 1)
                mm = pe.matmul(ps[0][:, 0, 0:MEM], ones[:, :], T.mem_sq[:, c, :], start=c == 0, stop=c == KD - 1)
            mm.then_inc(mm_done, 1)
            pe.wait_ge(vec_out, LAYERS * NV1 + VI1["o", 5])
            pe.wait_ge(hsum_step, LAYERS * (KD - 1) + KD - 1)
            for a in range(2):
                mm = pe.matmul(ps[1][:, a, 0:LH], ones[:, :], sq[:, 0, a * LH:a * LH + LH], start=True, stop=True)
            mm.then_inc(mm_done, 1)

        @block.vector
        def _(dve):
            dve.sem_inc(vec_out, NV1)
            dve.sem_inc(wlo_ready, NSPLIT)

            def add_squares(r, squares, adds):
                c0, k, squares0, adds0 = SUMS[r]
                for c in range(1, k):
                    dve.wait_ge(sq_ready, squares + squares0 + c + 1)
                    if c > 1:
                        dve.wait_ge(sum_step, adds + adds0 + c - 1)
                    dve.tensor_tensor(sq[:, c0, :], sq[:, c0, :], sq[:, c0 + c, :], ALU.add).then_inc(sum_step, 1)

            with dve.Fori(0, LAYERS) as layer:

                def wait_mm(g):
                    dve.wait_ge(mm_done, (layer + 1) * NG1 + GI1[g] + 1)

                def wait_own(g):
                    dve.wait_ge(vec_out, (layer + 1) * NV1 + VI1[g])

                def normed(g, out, r):
                    wait_mm(g)
                    dve.tensor_tensor(two(out), phalf(g), two(rstd[:, r, :]), ALU.mult).then_inc(vec_out, 1)

                def rest(n):
                    dve.wait_ge(whi_ready, layer * NSPLIT + n + 1)
                    dve.tensor_tensor(split(n, 1), raw(n), split(n, 0).bitcast(F32), ALU.subtract).then_inc(wlo_ready, 1)

                dve.wait_ge(vec_out, (layer + 1) * NV1)
                dve.wait_ge(lw_ready, layer * 16 + 16)
                rest(0)
                for k in range(KD):
                    dve.wait_ge(xhi_ready, layer * KD + k + 1)
                    dve.scalar_tensor_tensor(x_lo[:, k, :], hT[:, k, :], lw[:, LW_NORM + k:LW_NORM + k + 1], x_hi[:, k, :].bitcast(F32),
                                             ALU.mult, ALU.subtract).then_inc(xw_ready, 1)
                rest(1)
                dve.tensor_scalar(qws[:, :], lw[:, LW_Q:LW_Q + KQ], SCALE1, None, ALU.mult).then_inc(qws_ready, 1)
                rest(2)
                rest(3)
                dve.wait_ge(rstd_ready, layer * 3 + 1)
                for k in range(5):
                    if k >= 2:
                        rest(k + 2)
                    normed(("u", k), cq[:, k, :], 0)
                rest(7)

                dve.wait_ge(const_ready, 48)
                dve.wait_ge(zeroed, 4)
                g = ("kr", 0)
                wait_mm(g)
                dve.tensor_tensor(two(rt[0:32, 0, :]), phalf(g, 0, 32), two(rstd[0:32, 0, :]), ALU.mult)
                dve.tensor_tensor(two(rt[0:32, 1, :]), phalf(g, 32, 64), two(rstd[32:64, 0, :]), ALU.mult).then_inc(vec_out, 1)
                wait_own(g)
                dve.tensor_tensor(rt[0:32, 2, :], rt[0:32, 0, :], rope[0:32, 0, :], ALU.mult)
                dve.tensor_tensor(rt[0:32, 3, :], rt[0:32, 1, :], rope[0:32, 1, :], ALU.mult).then_inc(k_step, 1)
                dve.wait_ge(k_step, layer * 3 + 1)
                dve.tensor_tensor(krE[0:32, :], rt[0:32, 2, :], rt[0:32, 3, :], ALU.subtract)
                dve.tensor_tensor(krO[64:96, :], rt[0:32, 2, :], rt[0:32, 3, :], ALU.subtract).then_inc(k_step, 1)
                dve.wait_ge(k_step, layer * 3 + 2)
                dve.tensor_tensor(rt[0:32, 2, :], rt[0:32, 1, :], rope[0:32, 0, :], ALU.mult)
                dve.tensor_tensor(rt[0:32, 3, :], rt[0:32, 0, :], rope[0:32, 1, :], ALU.mult).then_inc(k_step, 1)
                dve.wait_ge(k_step, layer * 3 + 3)
                dve.tensor_tensor(krE[32:64, :], rt[0:32, 2, :], rt[0:32, 3, :], ALU.add)
                dve.tensor_tensor(krO[96:128, :], rt[0:32, 2, :], rt[0:32, 3, :], ALU.add).then_inc(kr_ready, 1)

                rest(8)
                add_squares(1, layer * NSQ, layer * NSUM)
                add_squares(2, layer * NSQ, layer * NSUM)
                normed(("fi", 0), fin[:, 0, :], 0)
                rest(9)
                normed(("fi", 1), fin[:, 1, :], 0)
                for c in range(2):
                    rest(10 + c)
                    normed(("pi", c), pin[:, c, 16:16 + L], 0)

                dve.wait_ge(qws_ready, layer + 1)
                dve.wait_ge(rstd_ready, layer * 3 + 2)
                for k in range(KQ):
                    dve.scalar_tensor_tensor(cq[:, k, :], cq[:, k, :], qws[:, k:k + 1], rstd[:, 1, :], ALU.mult, ALU.mult).then_inc(cn_ready, 1)
                dve.wait_ge(rstd_ready, layer * 3 + 3)
                for k in range(KKV):
                    dve.scalar_tensor_tensor(cq[:, KQ + k, :], cq[:, KQ + k, :], lw[:, LW_KV + k:LW_KV + k + 1], rstd[:, 2, :],
                                             ALU.mult, ALU.mult).then_inc(cn_ready, 1)
                for m in range(8):
                    if 12 + m < NWIN:
                        rest(12 + m)
                    normed(("ga", m), gate[:, m, :], 0)

                for c, order in ((0, (0, 1)), (1, (1, 0))):
                    g = ("qr", c)
                    wait_mm(g)
                    dve.tensor_tensor(two(rt[:, 2 * c, :]), phalf(g), two(rope[:, order[0], :]), ALU.mult)
                    dve.tensor_tensor(two(rt[:, 2 * c + 1, :]), phalf(g), two(rope[:, order[1], :]), ALU.mult).then_inc(vec_out, 1)
                wait_own(("qr", 1))
                for h in range(HEADS):
                    src, to = slice(32 * h, 32 * h + 32), 64 * (h % 2)
                    dve.tensor_tensor(qr[to:to + 32, h // 2, :], rt[src, 0, :], rt[src, 2, :], ALU.subtract)
                    last = dve.tensor_tensor(qr[to + 32:to + 64, h // 2, :], rt[src, 1, :], rt[src, 3, :], ALU.add)
                last.then_inc(qr_ready, 1)

                wait_mm(("ab", 0))
                dve.tensor_copy(ab[:, :, :], pst(("ab", 0))[:, :, 0:256]).then_inc(vec_out, 1)
                for c in range(2):
                    g = ("yf", c)
                    wait_mm(g)
                    dve.wait_ge(silu_done, layer * 8 + c + 1)
                    dve.tensor_tensor(two(mix[:, c, :]), phalf(g), two(gate[:, c, :]), ALU.mult).then_inc(vec_out, 1)
                for c in range(2):
                    g = ("yp", c)
                    wait_mm(g)
                    dve.wait_ge(silu_done, layer * 8 + c + 3)
                    dve.scalar_tensor_tensor(two(mix[:, 2 + c, :]), phalf(g), lw[:, LW_POOL + c:LW_POOL + c + 1], two(gate[:, 2 + c, :]),
                                             ALU.mult, ALU.mult).then_inc(vec_out, 1)
                dve.wait_ge(silu_done, layer * 8 + 8)

                def maximum(h, i):
                    g, m, n = ("s", h, i), LT[i][1], h * NT + i
                    wait_mm(g)
                    dve.tensor_reduce(nmax[0:m, n:n + 1], phalf(g, 0, m), AX.XY, ALU.max, negate=True).then_inc(max_ready, 1)

                def normalise(h, i):
                    m, n = LT[i][1], h * NT + i
                    dve.wait_ge(act_out, (layer + 1) * NA1 + AI1["s", h, i])
                    dve.reciprocal(rinv[0:m, n:n + 1], rsum[0:m, n:n + 1]).then_inc(inv_ready, 1)
                    dve.wait_ge(inv_ready, layer * NEXP + n + 1)
                    dve.tensor_scalar(probs[0:m, h % 2, i, :], probs[0:m, h % 2, i, :], rinv[0:m, n:n + 1], None,
                                      ALU.mult).then_inc(probs_ready, 1)

                def softmax(h):
                    for i in range(NT):
                        maximum(h, i)
                        if i:
                            normalise(h, i - 1)
                    normalise(h, NT - 1)

                def gated(h):
                    wait_mm(("a", h))
                    dve.tensor_tensor(two(mix[:, 4 + h, :]), phalf(("a", h)), two(gate[:, 4 + h, :]), ALU.mult).then_inc(vec_out, 1)

                softmax(0)
                softmax(1)
                softmax(2)
                gated(0)
                softmax(3)

                def mix_rest(c):
                    dve.wait_ge(mixhi_ready, layer * KD + c + 1)
                    dve.tensor_tensor(x_lo[:, c, :], mix[:, c, :], x_hi[:, c, :].bitcast(F32), ALU.subtract).then_inc(mix_ready, 1)

                gated(1)
                rest(NWIN)
                for c in range(2):
                    mix_rest(c)
                gated(2)
                for c in range(2, 5):
                    mix_rest(c)
                rest(NWIN + 1)
                mix_rest(5)
                mix_rest(6)
                gated(3)
                mix_rest(7)
                for m in range(KD):
                    if m + 2 < KD:
                        rest(NWIN + m + 2)
                    wait_mm(("o", m))
                    dve.tensor_tensor(two(hT[:, m, :]), phalf(("o", m)), two(hT[:, m, :]), ALU.add).then_inc(vec_out, 1)

            dve.wait_ge(lw_ready, 16 * (LAYERS + 1))
            dve.wait_ge(rstd_ready, LAYERS * 3 + 1)
            for k in range(KD):
                c = LW_VEC + V2["mem"][0] + k
                dve.scalar_tensor_tensor(T.memn[:, k, :], T.mem_in[:, k, :], lw[:, c:c + 1], rstd[:, 1, 0:MEM],
                                         ALU.mult, ALU.mult).then_inc(T.memn_ready, 1)

        @block.scalar
        def _(act):
            for k in range(KD // 2):
                act.dma_start(hT[:, 2 * k:2 * k + 2, :], dram["hT"][2 * k * P:2 * (k + 1) * P].rearrange("(k p) n -> p k n", p=P)
                              ).then_inc(h_loaded[k], 16)
            act.sem_inc(act_out, NA1)
            act.wait_ge(T.setup, T.N_SETUP)
            with act.Fori(0, LAYERS) as layer:

                def wait_mm(g):
                    act.wait_ge(mm_done, (layer + 1) * NG1 + GI1[g] + 1)

                def wait_vec(g):
                    act.wait_ge(vec_out, (layer + 1) * NV1 + VI1[g])

                def rms(r, size):
                    g = ("rs", r)
                    wait_mm(g)
                    act.activation(two(rstd[:, r, :]), phalf(g), ACT.Ln, bias=eps[:, :], scale=1.0 / size).then_inc(act_out, 1)
                    act.wait_ge(act_out, (layer + 1) * NA1 + AI1[g])
                    act.activation(rstd[:, r, :], rstd[:, r, :], ACT.Exp, scale=-0.5).then_inc(rstd_ready, 1)

                def copy(g, out, src):
                    wait_mm(g)
                    act.activation(out, src, ACT.Copy).then_inc(act_out, 1)

                def rounded(n):
                    name, i = ("win", n // 2) if n < NWIN else ("wout", (n - NWIN) // 2)
                    at = WI1[name, i]
                    act.wait_ge(w_ready[at % RING], (layer * (NW1 // RING) + at // RING + 1) * 16)
                    act.wait_ge(mm_done, (layer + (0 if n < 2 else 1)) * NG1 + GI1[SPLIT1[n - 2]] + 1)
                    act.activation(split(n, 0), raw(n), ACT.Copy).then_inc(whi_ready, 1)

                for k in range(KD):
                    if k == KD - 2:
                        rounded(0)
                    act.wait_ge(h_loaded[k // 2], 16)
                    act.wait_ge(vec_out, layer * NV1 + VI1["o", k])
                    act.activation(sq[:, k, :], hT[:, k, :], ACT.Square).then_inc(sq_ready, 1)
                act.wait_ge(lw_ready, layer * 16 + 16)
                for k in range(KD):
                    act.activation(x_hi[:, k, :], hT[:, k, :], ACT.Copy, scale=lw[:, LW_NORM + k:LW_NORM + k + 1]).then_inc(xhi_ready, 1)
                for n in (1, 2, 3):
                    rounded(n)
                rms(0, D)

                def square(k):
                    wait_vec(("u", k))
                    act.activation(sq[:, k, :], cq[:, k, :], ACT.Square).then_inc(sq_ready, 1)

                rounded(4)
                square(0)
                square(1)
                rounded(5)
                square(2)
                rounded(6)
                square(3)
                square(4)
                for n in (7, 8, 9):
                    rounded(n)
                rms(1, QR)
                rms(2, KVR)
                rounded(10)
                rounded(11)
                for m in range(8):
                    if 12 + m < NWIN:
                        rounded(12 + m)
                    wait_vec(("ga", m))
                    act.activation(gate[:, m, :], gate[:, m, :], ACT.Silu).then_inc(silu_done, 1)
                for h in range(HEADS):
                    copy(("q", h), two(qn[:, h, :]), phalf(("q", h)))
                for h in range(HEADS):
                    copy(("kn", h), two(kn[:, h, :]), phalf(("kn", h)))
                for i in range(2):
                    copy(("v", i), v[:, 2 * i:2 * i + 2, :], pst(("v", i))[:, :, :])
                copy(("v", 2), v[0:LT[-1][1], NT - 1, :], pst(("v", 2))[0:LT[-1][1], 0, :])
                act.wait_ge(qr_ready, layer + 1)
                for i, (t0, m) in enumerate(LT):
                    copy(("pq", i), pq[0:m, i, :, :], pst(("pq", i))[0:m, :, 0:256])

                def exponentials(h):
                    for i, (t0, m) in enumerate(LT):
                        n = h * NT + i
                        act.wait_ge(max_ready, layer * NEXP + n + 1)
                        act.activation(two(probs[0:m, h % 2, i, :]), phalf(("s", h, i), 0, m), ACT.Exp, bias=nmax[0:m, n:n + 1],
                                       accum_out=rsum[0:m, n:n + 1]).then_inc(act_out, 1)

                def turned(h):
                    for j, (k0, kj) in enumerate(LT):
                        copy(("t", h, j), pT[0:kj, j, :], pflat(("t", h, j))[0:kj, 0:L])

                def mix_rounded(c, g):
                    wait_vec(g)
                    act.activation(x_hi[:, c, :], mix[:, c, :], ACT.Copy).then_inc(mixhi_ready, 1)

                exponentials(0)
                exponentials(1)
                for c in range(2):
                    mix_rounded(c, ("yf", c))
                turned(0)
                exponentials(2)
                for c in range(2):
                    mix_rounded(2 + c, ("yp", c))
                turned(1)
                exponentials(3)
                mix_rounded(4, ("a", 0))
                rounded(NWIN)
                rounded(NWIN + 1)
                turned(2)
                turned(3)
                mix_rounded(5, ("a", 1))
                mix_rounded(6, ("a", 2))
                mix_rounded(7, ("a", 3))
                for m in range(KD - 2):
                    rounded(NWIN + m + 2)

            act.wait_ge(T.mem_loaded, 16)
            act.wait_ge(mm_done, LAYERS * NG1 + GI1["a", HEADS - 1] + 1)
            for k in range(KD):
                act.activation(T.mem_sq[:, k, :], T.mem_in[:, k, :], ACT.Square).then_inc(sq_ready, 1)
            for k in range(KD):
                act.wait_ge(vec_out, LAYERS * NV1 + VI1["o", k])
                act.activation(sq[:, k, :], hT[:, k, :], ACT.Square).then_inc(sq_ready, 1)
            for n, (src, out) in enumerate(((ps[0][:, 0, 0:MEM], rstd[:, 1, 0:MEM]), (ps[1][:, :, 0:LH], two(rstd[:, 0, :])))):
                act.wait_ge(mm_done, (LAYERS + 1) * NG1 + n + 1)
                act.activation(out, src, ACT.Ln, bias=eps[:, :], scale=1.0 / D).then_inc(act_out, 1)
                act.wait_ge(act_out, (LAYERS + 1) * NA1 + n + 1)
                act.activation(out, out, ACT.Exp, scale=-0.5).then_inc(rstd_ready, 1)


def load_expert(queue, dram, T, pair, e, j):
    name, k = (("eg", KD), ("eu", KD), ("ed", 512 // P))[j]
    src = dram[name][bass.ds(pair * 2 + e, 1), :, :].rearrange("a (k p) n -> p (a k) n", p=P)
    queue.dma_start(T.weights[e][j].rearrange("p (k n) -> p k n", k=k), src).then_inc(T.w_loaded[e][j], 16)


ROUTE_GROUP, ROUTE_CHOSEN, ROUTE_PAIR = 6, 20, 21


class Routing:

    def __init__(self, T, sem):
        place = T.qn[:, :, :].rearrange("p h n -> p (h n)")
        at = [0]

        def take(*shape):
            n = math.prod(shape)
            view = place[:, at[0]:at[0] + n]
            at[0] += n
            return view if len(shape) == 1 else view.rearrange("p (i n) -> p i n", i=shape[0])

        self.gmax, self.gsum, self.m1, self.m2, self.low, self.w1, self.w2, self.e2, self.den = (take(TT) for _ in range(9))
        self.iota_g, self.ge, self.gone = (take(TT, NGRP) for _ in range(3))
        self.iota_e, self.le, self.one1, self.one2, self.tmp, self.tmp2, self.chosen = (take(TT, NE) for _ in range(7))
        self.wcomb, self.rank = take(TT, NE + 2), take(TT, NE + 2)
        self.slot = take(TT, CAP)
        self.before = take(P)
        self.cmax = take(1)
        self.steps8 = take(ROUNDS_MAX - 1)
        assert at[0] <= HEADS * L
        self.const_made = sem("const_made")
        self.CONSTS = 8
        self.route_step = sem("route_step")
        self.group_exp = sem("group_exp")
        self.pair_exp = sem("pair_exp")
        self.rounds_ready = sem("rounds_ready")


def route(dve, T, R, mm_done, vec_out, ranks):
    lg = T.logits[:, :].rearrange("p (i n) -> p i n", i=TT)
    G4, G32 = [P, TT, NGRP], [P, TT, NE]
    steps = [0]

    def step(ins):
        steps[0] += 1
        ins.then_inc(R.route_step, 1)
        dve.wait_ge(R.route_step, steps[0])

    def over(a, shape):
        return a.unsqueeze(2).broadcast_to(shape)

    def first_highest(values, m, one, iota, tmp, shape):
        step(dve.tensor_reduce(m, values, AX.X, ALU.max))
        step(tt(tmp, values, over(m, shape), ALU.is_equal))
        step(stt(tmp, tmp, -100.0, iota, ALU.mult, ALU.add))
        step(dve.tensor_reduce(R.low, tmp, AX.X, ALU.min))
        step(tt(one, tmp, over(R.low, shape), ALU.is_equal))

    tt, stt, ts = dve.tensor_tensor, dve.scalar_tensor_tensor, dve.tensor_scalar
    dve.wait_ge(R.const_made, R.CONSTS)
    first_highest(lg[:, :, 0:NGRP], R.gmax, R.gone, R.iota_g, R.ge, G4)
    tt(R.ge, lg[:, :, 0:NGRP], over(R.gmax, G4), ALU.subtract).then_inc(R.route_step, 1)
    steps[0] += 1
    assert steps[0] == ROUTE_GROUP
    step(ts(R.gone, R.gone, 1e30, -1e30, ALU.mult, ALU.add))
    step(tt(R.le.rearrange("p i (q n) -> p i q n", q=NGRP), lg[:, :, NGRP:].rearrange("p i (q n) -> p i q n", q=NGRP),
            R.gone.unsqueeze(3).broadcast_to([P, TT, NGRP, EPG]), ALU.add))
    first_highest(R.le, R.m1, R.one1, R.iota_e, R.tmp, G32)
    step(stt(R.le, R.one1, -3e30, R.le, ALU.mult, ALU.add))
    first_highest(R.le, R.m2, R.one2, R.iota_e, R.tmp, G32)
    step(tt(R.chosen, R.one1, R.one2, ALU.add))
    assert steps[0] == ROUTE_CHOSEN
    step(tt(R.m2, R.m2, R.m1, ALU.subtract))
    assert steps[0] == ROUTE_PAIR
    dve.wait_ge(mm_done, GI2["rank",] + 1)
    step(stt(R.tmp, ranks[:, 0, 0:TT * NE].rearrange("p (i n) -> p i n", i=TT), 1.0, R.chosen, ALU.add, ALU.mult))
    step(ts(R.rank[:, :, 0:NE], R.tmp, CAP - 1.0, None, ALU.add))
    dve.tensor_reduce(R.cmax, ranks[:, 1, 0:NE], AX.X, ALU.max).then_inc(vec_out, 1)
    dve.wait_ge(vec_out, VI2["rank",])
    step(ts(R.steps8, R.steps8, R.cmax[:, 0:1], None, ALU.is_lt))
    step(dve.tensor_reduce(R.cmax, R.steps8, AX.X, ALU.add))
    dve.tensor_scalar(T.rounds[:, :], R.cmax, 1.0, None, ALU.add).then_inc(R.rounds_ready, 1)
    dve.wait_ge(R.group_exp, 1)
    step(dve.tensor_reduce(R.gsum, R.ge, AX.X, ALU.add))
    dve.wait_ge(R.pair_exp, 1)
    step(ts(R.den, R.e2, 1.0, None, ALU.add))
    step(tt(R.den, R.den, R.gsum, ALU.mult))
    step(dve.reciprocal(R.w1, R.den))
    step(tt(R.w2, R.w1, R.e2, ALU.mult))
    step(tt(R.tmp, R.one1, over(R.w1, G32), ALU.mult))
    step(tt(R.tmp2, R.one2, over(R.w2, G32), ALU.mult))
    step(tt(R.wcomb[:, :, 0:NE], R.tmp, R.tmp2, ALU.add))


def second_block(nc, dram, T, R, sem):
    ctx = ExitStack()
    with ctx:
        def sb(name, shape):
            return ctx.enter_context(nc.sbuf_tensor(name, shape, F32))

        def placed_before(name, shape):
            with nc.sbuf_tensor(name, shape, F32R) as t:
                return t

        hT, ring, ones, ident, eps, lw, ps = T.hT, T.ring, T.ones, T.ident, T.eps, T.lw, T.ps
        x = hT[:, :, META:L]
        x_lo = placed_before("x2_lo", [P, KD, SEQ])
        sq = sb("sq", [P, KD, SEQ])
        xn = sb("xn", [P, KD, SEQ])
        ox = xn
        rstd = T.rstd[:, 1:3, 0:SEQ]
        memn = T.memn
        kx = T.area_u1[:, 0:KD * MEM].rearrange("p (k n) -> p k n", k=KD)
        vx = T.area_u1[:, KD * MEM:KD * MEM + 2 * D].rearrange("p (j n) -> p j n", j=2)
        wide = T.area_u0
        xr = wide[:, 0:KH * (SEQ + 3)].rearrange("p (c n) -> p c n", c=KH)
        xg = wide[:, KH * (SEQ + 3):KH * (2 * SEQ + 3)].rearrange("p (c n) -> p c n", c=KH)
        qx = wide[:, 0:KD * SEQ].rearrange("p (c n) -> p c n", c=KD)
        qa, kaE, kaO, va = (T.area_g[:, n * KH * SEQ:(n + 1) * KH * SEQ].rearrange("p (c n) -> p c n", c=KH) for n in range(4))
        x_hi = placed_before("x2_hi", [P, KD, SEQ])
        bias = sb("bias", [P, AH, SEQ])
        sbuf = sb("sbuf", [P, 2, SBW])
        xc = sb("xc", [P, KH, SEQ])
        r = T.gates_place.rearrange("p (c b) n -> p c (b n)", c=KH)
        pT = r
        gi = vx[:, :, :].rearrange("p c (b n) -> p (c b) n", b=2)
        aa, th = sq[:, 0:KH, :], sq[:, KH:, :]
        yr = xn[:, 0:KH, :]
        vec = lw[:, LW_VEC:LW_VEC + NV2]
        wr = lw[:, LW_WR:LW_WR + KD * NL].rearrange("p (k n) -> p k n", k=KD)
        rb = lw[:, LW_RB:LW_RB + TT * NL]
        wab = sbuf[:, 1, 0:2 * KH * P].rearrange("p (c n) -> p c n", c=2 * KH)
        nsp = sb("nsp", [P, 6, KH])
        mx = sb("mx", [P, 4 * AH])
        nmx = sb("nmx", [P, 4 * (AH + XH)])
        rsum = sb("rsum2", [P, 4 * (AH + XH)])
        rinv = sb("rinv2", [P, 4 * (AH + XH)])

        mm_done = sem("mm2_done")
        vec_out = sem("vec2_out")
        act_out = sem("act2_out")
        w_ready = T.w_ready
        loaded = sem("loaded2")
        key_pad = sem("key_pad")
        sum_step = sem("sum2_step")
        whi_ready = sem("whi2_ready")
        wlo_ready = sem("wlo2_ready")
        half_done = sem("half_done")
        xhi_ready = sem("xhi2_ready")
        xlo_ready = sem("xlo2_ready")
        sq_ready = sem("sq2_ready")
        rstd_ready = sem("rstd2_ready")
        norm_ready = sem("norm_ready")
        pad_ready = sem("pad_ready")
        mask_ready = sem("mask_ready")
        conv_step = sem("conv_step")
        sp_step = sem("sp_step")
        sp_exp = sem("sp_exp")
        decay_ready = sem("decay_ready")
        m2_ready = sem("m2_ready")
        logs_ready = sem("logs_ready")
        root_ready = sem("root_ready")
        gelu_ready = sem("gelu_ready")
        rnn_step = sem("rnn_step")
        scanned = sem("scanned")
        nmax_ready = sem("nmax_ready")
        exp_done = sem("exp2_done")
        inv_ready = sem("inv2_ready")
        probs_ready = sem("probs2_ready")

        def col(name, c):
            o = V2[name][0] + c
            return vec[:, o:o + 1]

        def pst(g):
            return ps[GI2[g] % NPS]

        def pflat(g):
            return pst(g)[:, :, :].rearrange("p a n -> p (a n)")

        def norm_at(name):
            return KD * NORMS.index(name)

        def split(n, part):
            return T.w2_split[:, n % 2, part, :].rearrange("p (k n) -> p k n", k=KD)

        def raw(n):
            return panel_view(ring, WI2[PANEL2[SPLIT2[n]]])[:, :, n % 2 * P:n % 2 * P + P]

        def panel_count(n):
            return 16 * (LAYERS * NW1 // RING + (1 if n < 2 else n // 2))

        def squares(name):
            return sq if name in ("ln1", "mixed") else xn

        def adds_at(name):
            n = NORMS.index(name)
            return n * (KD - 1) - (1 if n >= NORMS.index("mixed") else 0)

        block = ctx.enter_context(nc.Block())

        @block.sync
        def _(sp):
            for n, (name, i) in enumerate(W2):
                if n >= RING:
                    if W2[n - 2] in CHUNK2:
                        sp.wait_ge(wlo_ready, CHUNK2[W2[n - 2]] + 2)
                    else:
                        sp.wait_ge(mm_done, GI2[W2_USER[W2[n - 2]]] + 1)
                    sp.dma_start(panel_view(ring, n), panel_source(dram, name, i)).then_inc(w_ready[slot2(n)], 16)
                if (name, i) in (("xq", 0), ("xq", 2)):
                    sp.wait_ge(mm_done, GI2["at", AH - 1] + 1)
                    load_expert(sp, dram, T, 0, i // 2, 0)
            sp.wait_ge(mm_done, GI2["sx", XH - 1] + 1)
            load_expert(sp, dram, T, 0, 0, 1)
            sp.wait_ge(mm_done, GI2["ax", XH - 1] + 1)
            load_expert(sp, dram, T, 0, 1, 1)

        @block.gpsimd
        def _(pool):
            pool.dma_start(wab, dram["wab"]).then_inc(loaded, 16)
            pool.memset(xr[:, :, 0:3], 0.0).then_inc(pad_ready, 1)
            pool.wait_ge(pad_ready, 1)
            pool.memset(kaE[64:128, :, :], 0.0).then_inc(key_pad, 1)
            pool.wait_ge(key_pad, 1)
            pool.memset(kaO[0:64, :, :], 0.0).then_inc(key_pad, 1)
            pool.wait_ge(key_pad, 2)
            pool.wait_ge(mm_done, GI2["ka", 1] + 1)
            pool.dma_start(bias[:, :, :], dram["bias"].rearrange("h p n -> p h n")).then_inc(loaded, 16)
            pool.wait_ge(loaded, 16 * 2)
            pool.memset(bias[0:64, :, SEQ - 64:SEQ], -1e30).then_inc(mask_ready, 1)
            pool.wait_ge(act_out, AI2["gt", KH - 1])
            pool.tensor_tensor(gi, gi, xc[:, :, :], ALU.mult).then_inc(rnn_step, 1)
            pool.wait_ge(logs_ready, 2)
            pool.tensor_tensor(yr, yr, th, ALU.subtract).then_inc(rnn_step, 1)
            pool.wait_ge(root_ready, 1)
            pool.wait_ge(rnn_step, 2)
            pool.tensor_tensor(gi, gi, yr, ALU.mult).then_inc(rnn_step, 1)
            pool.wait_ge(scanned, KH)
            pool.wait_ge(gelu_ready, 1)
            pool.tensor_tensor(yr, yr, xg, ALU.mult).then_inc(rnn_step, 1)
            pool.wait_ge(mm_done, GI2["vx", 3] + 1)
            made = R.const_made
            pool.iota(R.iota_g, pattern=[[0, TT], [1, NGRP]], base=0, channel_multiplier=0,
                      allow_small_or_imprecise_dtypes=True).then_inc(made, 1)
            pool.iota(R.iota_e, pattern=[[0, TT], [1, NE]], base=0, channel_multiplier=0,
                      allow_small_or_imprecise_dtypes=True).then_inc(made, 1)
            pool.iota(R.slot, pattern=[[0, TT], [1, CAP]], base=0, channel_multiplier=0,
                      allow_small_or_imprecise_dtypes=True).then_inc(made, 1)
            pool.iota(R.steps8, pattern=[[CAP, ROUNDS_MAX - 1]], base=CAP, channel_multiplier=0,
                      allow_small_or_imprecise_dtypes=True).then_inc(made, 1)
            pool.memset(R.wcomb[:, :, NE:], 0.0).then_inc(made, 1)
            pool.memset(R.rank[:, :, NE:], CAP - 1.0).then_inc(made, 1)
            pool.memset(R.before, 1.0).then_inc(made, 1)
            pool.wait_ge(made, 7)
            pool.affine_select(out=R.before, in_=R.before, compare_op=ALU.is_gt, fill=0.0, base=0,
                               pattern=[[1, P]], channel_multiplier=-1).then_inc(made, 1)

        @block.tensor
        def _(pe):
            def begin(g):
                n = GI2[g]
                if n >= NPS:
                    prev = G2[n - NPS]
                    if prev in AI2:
                        pe.wait_ge(act_out, AI2[prev])
                    else:
                        pe.wait_ge(vec_out, VI2[prev])

            def panel(name, i):
                n = WI2[name, i]
                pe.wait_ge(w_ready[slot2(n)], panel_count(n))
                return panel_view(ring, n)

            def sums(g, name, banks=1, n=SEQ):
                begin(g)
                pe.wait_ge(sum_step, adds_at(name))
                for b in range(banks):
                    mm = pe.matmul(pst(g)[:, b, 0:n], ones[:, :], squares(name)[:, b * KD // banks, 0:n], start=True, stop=True)
                mm.then_inc(mm_done, 1)

            def two(g, ready=None):
                first = SPLIT2.index(g)
                begin(g)
                for b in range(2):
                    pe.wait_ge(wlo_ready, first + b + 1)
                    for k in range(KD):
                        if b == 0 and ready is not None:
                            pe.wait_ge(xlo_ready, ready + k + 1)
                        for t, (part, src) in enumerate(((0, x_hi), (0, x_lo), (1, x_hi))):
                            mm = pe.matmul(pst(g)[:, b, :], split(first + b, part)[:, k, :], src[:, k, :],
                                           start=k == 0 and t == 0, stop=k == KD - 1 and t == 2)
                    mm.then_inc(mm_done if b else half_done, 1)

            def memory_keys(q):
                g = ("kx", q)
                w = panel("xk", q)
                begin(g)
                for m in range(2):
                    for k in range(KD):
                        mm = pe.matmul(pst(g)[:, 0, m * MEM:m * MEM + MEM], w[:, k, m * P:m * P + P], memn[:, k, :],
                                       start=k == 0, stop=k == KD - 1)
                mm.then_inc(mm_done, 1)

            def memory_values(q):
                g = ("vx", q)
                w = panel("xv", q)
                begin(g)
                for j in range(2):
                    for k in range(KD):
                        mm = pe.matmul(pst(g)[:, j, 0:256], memn[:, k, j * P:j * P + P], w[:, k, :], start=k == 0, stop=k == KD - 1)
                mm.then_inc(mm_done, 1)

            pe.wait_ge(T.lw_ready, 16 * (LAYERS + 1))
            pe.wait_ge(T.memn_ready, KD)
            memory_keys(0)
            memory_keys(1)
            sums(("n", 1), "ln1")
            memory_keys(2)
            for name in ("xr", "xg", "qa", "ka"):
                for c in range(2):
                    two((name, c), 0 if (name, c) == ("xr", 0) else None)
            begin(("va", 0))
            begin(("va", 1))
            for half in range(2):
                w = panel("win2", 8 + half)
                for i in range(TT):
                    for k in range(KD):
                        mm = pe.matmul(pst(("va", i // 2))[:, i % 2, half * 256:half * 256 + 256], xn[:, k, i * P:i * P + P], w[:, k, :],
                                       start=k == 0, stop=k == KD - 1)
                    if half and i % 2:
                        mm.then_inc(mm_done, 1)

            pe.wait_ge(loaded, 16 * 2)
            pe.wait_ge(conv_step, CONV)
            for c in range(KH):
                g = ("gt", c)
                begin(g)
                for b in range(2):
                    mm = pe.matmul(pst(g)[:, b, :], wab[:, b * KH + c, :], xc[:, c, :], start=True, stop=True)
                mm.then_inc(mm_done, 1)

            def scores(h):
                keys = kaO if h % 2 else kaE
                for g, tiles in ((("sA", h), (3, 2)), (("sB", h), (1, 0))):
                    begin(g)
                    for b, i in enumerate(tiles):
                        mm = pe.matmul(pst(g)[:, b, 0:(i + 1) * P], qa[:, h // 2, i * P:i * P + P], keys[:, h // 2, 0:(i + 1) * P],
                                       start=True, stop=True)
                    mm.then_inc(mm_done, 1)

            def turn(h):
                pe.wait_ge(probs_ready, 4 * h + 4)
                for g, js in ((("tA", h), (0, 1)), (("tB", h), (2, 3))):
                    begin(g)
                    for b, j in enumerate(js):
                        for i in range(j, TT):
                            o = SOFF[i] + j * P
                            mm = pe.transpose(pst(g)[:, b, i * P:i * P + P], sbuf[:, h % 2, o:o + P], ident[:, :])
                    mm.then_inc(mm_done, 1)

            def attend(h):
                g = ("at", h)
                begin(g)
                pe.wait_ge(act_out, AI2["tB", h])
                for j in range(TT):
                    mm = pe.matmul(pst(g)[0:64, 0, j * P:SEQ], va[:, j, h * 64:h * 64 + 64], pT[:, j, j * P:SEQ],
                                   start=j == 0, stop=j == TT - 1)
                mm.then_inc(mm_done, 1)

            pe.wait_ge(act_out, AI2["ka", 1])
            pe.wait_ge(vec_out, VI2["va", 1])
            pe.wait_ge(key_pad, 2)
            scores(0)
            scores(1)
            memory_keys(3)
            for h in range(AH):
                turn(h)
                if h + 2 < AH:
                    scores(h + 2)
                attend(h)

            pe.wait_ge(scanned, KH)
            memory_values(0)
            sums(("n", 2), "mixed", banks=2)
            memory_values(1)
            for m in range(4):
                two(("o", m), KD if m == 0 else None)
            memory_values(2)
            sums(("n", 3), "ln2")
            memory_values(3)
            for m in range(4):
                two(("qx", m), 2 * KD if m == 0 else None)

            def cross_scores(h):
                g = ("sx", h)
                begin(g)
                for i in range(TT):
                    for c in range(2):
                        mm = pe.matmul(pflat(g)[:, i * MEM:i * MEM + MEM], qx[:, 2 * h + c, i * P:i * P + P], kx[:, 2 * h + c, :],
                                       start=c == 0, stop=c == 1)
                mm.then_inc(mm_done, 1)

            def cross_turn(h):
                g = ("tx", h)
                pe.wait_ge(probs_ready, 4 * AH + 4 * h + 4)
                begin(g)
                for j in range(2):
                    for i in range(TT):
                        mm = pe.transpose(pst(g)[:, j, i * P:i * P + P], sbuf[:, h % 2, i * MEM + j * P:i * MEM + j * P + P], ident[:, :])
                mm.then_inc(mm_done, 1)

            def cross_attend(h):
                g = ("ax", h)
                begin(g)
                pe.wait_ge(act_out, AI2["tx", h])
                for b in range(2):
                    for j in range(2):
                        mm = pe.matmul(pst(g)[:, b, :], vx[:, j, h * 256 + b * P:h * 256 + b * P + P], pT[:, j, :],
                                       start=j == 0, stop=j == 1)
                mm.then_inc(mm_done, 1)

            pe.wait_ge(act_out, AI2["qx", 3])
            pe.wait_ge(vec_out, VI2["vx", 3])
            cross_scores(0)
            cross_scores(1)
            for h in range(XH):
                cross_turn(h)
                if h + 2 < XH:
                    cross_scores(h + 2)
                cross_attend(h)
            for m in range(4):
                two(("xo", m), 3 * KD if m == 0 else None)

            def to_tokens(name, src, tiles=range(TT)):
                for i in tiles:
                    g = (name, i)
                    begin(g)
                    for k in range(KD):
                        mm = pe.transpose(pflat(g)[:, k * P:k * P + P], src[:, k, i * P:i * P + P], ident[:, :])
                    mm.then_inc(mm_done, 1)

            pe.wait_ge(vec_out, VI2["xo", 3])
            to_tokens("xt", x, (0,))
            sums(("n", 4), "ln3")
            to_tokens("xt", x, range(1, TT))
            g = ("lg",)
            begin(g)
            for i in range(TT):
                for k in range(KD):
                    if i == 0:
                        pe.wait_ge(norm_ready, norm_at("ln3") + k + 1)
                    mm = pe.matmul(pst(g)[:, 0, i * NL:i * NL + NL], xn[:, k, i * P:i * P + P], wr[:, k, :], start=k == 0, stop=k == KD - 1)
            mm.then_inc(mm_done, 1)
            to_tokens("ht", xn)
            g = ("rank",)
            begin(g)
            pe.wait_ge(R.const_made, R.CONSTS)
            pe.wait_ge(R.route_step, ROUTE_CHOSEN)
            for i in range(TT):
                for j in range(i + 1):
                    pe.matmul(pst(g)[:, 0, i * NE:i * NE + NE], ones[:, :] if j < i else R.before, R.chosen[:, j, :],
                              start=j == 0, stop=j == i)
            for j in range(TT):
                mm = pe.matmul(pst(g)[:, 1, 0:NE], ones[:, :], R.chosen[:, j, :], start=j == 0, stop=j == TT - 1)
            mm.then_inc(mm_done, 1)

        @block.vector
        def _(dve):
            def wait_mm(g):
                dve.wait_ge(mm_done, GI2[g] + 1)

            def norm(name, out, src, w, r=lambda k: 0, stage=None, chunk=None):
                dve.wait_ge(rstd_ready, NORMS.index(name))
                for k in range(KD):
                    dve.scalar_tensor_tensor(out[:, k, :], src[:, k, :], w(k), rstd[:, r(k), :], ALU.mult, ALU.mult).then_inc(norm_ready, 1)
                    if stage is not None and k:
                        if k == 1 and chunk is not None:
                            rest(chunk)
                        x_rest(stage, k - 1, out)
                if stage is not None:
                    x_rest(stage, KD - 1, out)

            def x_rest(stage, k, src):
                dve.wait_ge(xhi_ready, stage * KD + k + 1)
                dve.tensor_tensor(x_lo[:, k, :], src[:, k, :], x_hi[:, k, :].bitcast(F32), ALU.subtract).then_inc(xlo_ready, 1)

            def rest(*chunks):
                for n in chunks:
                    dve.wait_ge(whi_ready, n + 1)
                    dve.tensor_tensor(split(n, 1), raw(n), split(n, 0).bitcast(F32), ALU.subtract).then_inc(wlo_ready, 1)

            def copy(g, out, src):
                wait_mm(g)
                dve.tensor_copy(out, src).then_inc(vec_out, 1)

            dve.wait_ge(T.lw_ready, 16 * (LAYERS + 1))
            for k in range(KD):
                dve.scalar_tensor_tensor(x[:, k, :], x[:, k, :], lw[:, k:k + 1], T.rstd[:, 0, META:L], ALU.mult, ALU.mult
                                         ).then_inc(norm_ready, 1)
            dve.wait_ge(norm_ready, norm_at("first") + KD)

            def memory_values(q):
                copy(("vx", q), vx[:, :, 256 * q:256 * q + 256], pst(("vx", q))[:, :, 0:256])

            adds = [0]

            def add_squares(name, banks=1, chunks=range(KD)):
                per = KD // banks
                buf = squares(name)
                for c in chunks:
                    if c % per:
                        dve.wait_ge(sq_ready, norm_at(name) - KD + c + 1)
                        if c % per > 1:
                            dve.wait_ge(sum_step, adds[0])
                        first = c // per * per
                        dve.tensor_tensor(buf[:, first, :], buf[:, first, :], buf[:, c, :], ALU.add).then_inc(sum_step, 1)
                        adds[0] += 1

            add_squares("ln1")

            lam = vec[:, V2["lam"][0]:V2["lam"][0] + KH]
            absl, e, z, z2, acc, res = (nsp[:, i, :] for i in range(6))
            steps = [0]

            def step(ins):
                steps[0] += 1
                ins.then_inc(sp_step, 1)
                dve.wait_ge(sp_step, steps[0])

            step(dve.scalar_tensor_tensor(absl, lam, -1.0, lam, ALU.mult, ALU.max))
            dve.wait_ge(sp_exp, 1)
            step(dve.tensor_scalar(z2, e, 2.0, None, ALU.add))
            step(dve.reciprocal(z2, z2))
            step(dve.tensor_tensor(z, e, z2, ALU.mult))
            step(dve.tensor_tensor(z2, z, z, ALU.mult))
            step(dve.tensor_scalar(acc, z2, 1.0 / 17, None, ALU.mult))
            for odd in (15, 13, 11, 9, 7, 5, 3):
                step(dve.scalar_tensor_tensor(acc, acc, 1.0 / odd, z2, ALU.add, ALU.mult))
            step(dve.scalar_tensor_tensor(acc, acc, 1.0, z, ALU.add, ALU.mult))
            step(dve.tensor_scalar(res, lam, -1.0, 0.0, ALU.mult, ALU.max))
            step(dve.scalar_tensor_tensor(res, acc, 2.0, res, ALU.mult, ALU.add))
            step(dve.tensor_scalar(res, res, -8.0, None, ALU.mult))
            T.sp_steps = steps[0]

            rest(0, 1)
            norm("ln1", xn, x, lambda k: col("ln1", k), stage=0)
            for c in range(2):
                rest(2 * c + 2, 2 * c + 3)
                copy(("xr", c), xr[:, 2 * c:2 * c + 2, 3:3 + SEQ], pst(("xr", c))[:, :, :])
            for c in range(2):
                rest(2 * c + 6, 2 * c + 7)
                copy(("xg", c), xg[:, 2 * c:2 * c + 2, :], pst(("xg", c))[:, :, :])
            dve.wait_ge(pad_ready, 1)
            dve.wait_ge(vec_out, VI2["xr", 1])
            for c in range(KH):
                last = dve.tensor_scalar(xc[:, c, :], xr[:, c, 3:3 + SEQ], col("cw", 3 * KH + c), col("cb", c), ALU.mult, ALU.add)
            last.then_inc(conv_step, 1)
            for j in range(CONV - 1):
                rest(10 + 2 * j, 11 + 2 * j)
                dve.wait_ge(conv_step, j + 1)
                for c in range(KH):
                    last = dve.scalar_tensor_tensor(xc[:, c, :], xr[:, c, j:j + SEQ], col("cw", j * KH + c), xc[:, c, :],
                                                    ALU.mult, ALU.add)
                last.then_inc(conv_step, 1)
            for c in range(2):
                copy(("va", c), va[:, 2 * c:2 * c + 2, :], pst(("va", c))[:, :, :])

            def biased(h):
                for g, tiles in ((("sA", h), (3, 2)), (("sB", h), (1, 0))):
                    wait_mm(g)
                    for b, i in enumerate(tiles):
                        n = (i + 1) * P
                        last = dve.tensor_tensor_reduce(sbuf[:, h % 2, SOFF[i]:SOFF[i] + n], pst(g)[:, b, 0:n], bias[:, h, SEQ - n:SEQ],
                                                        1.0, -3e38, ALU.add, ALU.max, mx[:, 4 * h + i:4 * h + i + 1])
                    last.then_inc(vec_out, 1)
                dve.wait_ge(vec_out, VI2["sB", h])
                dve.tensor_scalar(nmx[:, 4 * h:4 * h + 4], mx[:, 4 * h:4 * h + 4], -1.0, None, ALU.mult).then_inc(nmax_ready, 1)

            def normalise(h, n, places):
                if h < AH:
                    dve.wait_ge(exp_done, 4 * h + 4)
                else:
                    dve.wait_ge(act_out, AI2["sx", h - AH])
                dve.reciprocal(rinv[:, 4 * h:4 * h + 4], rsum[:, 4 * h:4 * h + 4]).then_inc(inv_ready, 1)
                dve.wait_ge(inv_ready, h + 1)
                for i in range(TT):
                    p = sbuf[:, n, places[i][0]:places[i][0] + places[i][1]]
                    dve.tensor_scalar(p, p, rinv[:, 4 * h + i:4 * h + i + 1], None, ALU.mult).then_inc(probs_ready, 1)

            places = [(SOFF[i], (i + 1) * P) for i in range(TT)]

            def attended(h):
                rows = slice(64 * (h % 2), 64 * (h % 2) + 64)
                copy(("at", h), xn[rows, KH + h // 2, :], pst(("at", h))[0:64, 0, :])

            def decay():
                dve.wait_ge(decay_ready, KH)
                dve.wait_ge(mm_done, GI2["va", 1] + 1)
                dve.tensor_scalar(yr, th, -2.0, TINY, ALU.mult, ALU.max).then_inc(m2_ready, 1)

            def scan():
                dve.wait_ge(rnn_step, 3)
                for c in range(KH):
                    dve.tensor_tensor_scan(yr[:, c, :], aa[:, c, :], gi[:, c, :], 0.0, ALU.mult, ALU.add).then_inc(scanned, 1)

            dve.wait_ge(mask_ready, 1)
            biased(0)
            decay()
            biased(1)
            normalise(0, 0, places)
            for h in range(AH):
                if h + 1 < AH:
                    normalise(h + 1, (h + 1) % 2, places)
                if h + 2 < AH:
                    biased(h + 2)
                attended(h)
                if h == 3:
                    scan()
            add_squares("mixed", 2)
            memory_values(0)
            norm("mixed", xn, xn, lambda k: col("gnr", k) if k < KH else col("gna", k - KH), lambda k: k // KH, stage=1, chunk=16)
            rest(17)
            memory_values(1)

            def add(g, m):
                wait_mm(g)
                dve.tensor_tensor(x[:, 2 * m:2 * m + 2, :], pst(g)[:, :, :], x[:, 2 * m:2 * m + 2, :], ALU.add).then_inc(vec_out, 1)

            for m in range(4):
                if m < 3:
                    rest(18 + 2 * m, 19 + 2 * m)
                add(("o", m), m)
                if m:
                    add_squares("ln2", chunks=(2 * m - 2, 2 * m - 1))
            add_squares("ln2", chunks=(KD - 2, KD - 1))
            memory_values(2)
            norm("ln2", xn, x, lambda k: col("ln2", k), stage=2, chunk=24)
            rest(25)
            memory_values(3)
            for m in range(3):
                rest(26 + 2 * m, 27 + 2 * m)

            def cross_max(h):
                wait_mm(("sx", h))
                n = 4 * (AH + h)
                dve.tensor_reduce(nmx[:, n:n + 4], pflat(("sx", h)).rearrange("p (i n) -> p i n", i=TT), AX.X, ALU.max,
                                  negate=True).then_inc(nmax_ready, 1)

            xplaces = [(i * MEM, MEM) for i in range(TT)]
            cross_max(0)
            cross_max(1)
            normalise(AH, 0, xplaces)
            rest(32, 33)
            for h in range(XH):
                if h + 1 < XH:
                    normalise(AH + h + 1, (h + 1) % 2, xplaces)
                if h + 2 < XH:
                    cross_max(h + 2)
                copy(("ax", h), ox[:, 2 * h:2 * h + 2, :], pst(("ax", h))[:, :, :])
                if h:
                    x_rest(3, 2 * h - 2, ox)
                    x_rest(3, 2 * h - 1, ox)
            x_rest(3, KD - 2, ox)
            x_rest(3, KD - 1, ox)
            for m in range(4):
                if m < 3:
                    rest(34 + 2 * m, 35 + 2 * m)
                add(("xo", m), m)
                if m:
                    add_squares("ln3", chunks=(2 * m - 2, 2 * m - 1))
            add_squares("ln3", chunks=(KD - 2, KD - 1))
            norm("ln3", xn, x, lambda k: col("ln3", k))
            wait_mm(("lg",))
            dve.tensor_tensor(T.logits[:, :], pst(("lg",))[:, 0, 0:TT * NL], rb[:, :], ALU.add).then_inc(vec_out, 1)
            dve.wait_ge(vec_out, VI2["lg",])
            route(dve, T, R, mm_done, vec_out, pst(("rank",)))

        @block.scalar
        def _(act):
            def wait_mm(g):
                act.wait_ge(mm_done, GI2[g] + 1)

            def square(name, k, src, n=SEQ):
                act.activation(squares(name)[:, k, 0:n], src[:, k, 0:n], ACT.Square).then_inc(sq_ready, 1)

            def rms(g, size, banks=1, n=SEQ):
                wait_mm(g)
                out = rstd[:, 0:banks, 0:n]
                act.activation(out, pst(g)[:, 0:banks, 0:n], ACT.Ln, bias=eps[:, :], scale=1.0 / size).then_inc(act_out, 1)
                act.wait_ge(act_out, AI2[g])
                act.activation(out, out, ACT.Exp, scale=-0.5).then_inc(rstd_ready, 1)

            def copy(g, out, src, scale=1.0):
                wait_mm(g)
                act.activation(out, src, ACT.Copy, scale=scale).then_inc(act_out, 1)

            def rounded(*chunks):
                for n in chunks:
                    at = WI2[PANEL2[SPLIT2[n]]]
                    act.wait_ge(w_ready[slot2(at)], panel_count(at))
                    if n < 2:
                        act.wait_ge(mm_done, GI2["kx", 1] + 1)
                    elif n % 2:
                        act.wait_ge(mm_done, GI2[SPLIT2[n - 2]] + 1)
                    else:
                        act.wait_ge(half_done, n // 2)
                    act.activation(split(n, 0), raw(n), ACT.Copy).then_inc(whi_ready, 1)

            def squares_of(name, g, m):
                act.wait_ge(vec_out, VI2[g, m])
                for k in (2 * m, 2 * m + 1):
                    square(name, k, x)

            def x_rounded(stage, src, name=None, chunks=range(KD)):
                for k in chunks:
                    if name is not None:
                        act.wait_ge(norm_ready, norm_at(name) + k + 1)
                    act.activation(x_hi[:, k, :], src[:, k, :], ACT.Copy).then_inc(xhi_ready, 1)

            def memory_keys(q):
                copy(("kx", q), kx[:, 2 * q:2 * q + 2, :].rearrange("p m n -> p (m n)"), pst(("kx", q))[:, 0, :])

            act.wait_ge(T.lw_ready, 16 * (LAYERS + 1))
            for k in range(KD):
                act.wait_ge(norm_ready, norm_at("first") + k + 1)
                square("ln1", k, x)
            memory_keys(0)
            memory_keys(1)
            act.wait_ge(sp_step, 1)
            act.activation(nsp[:, 1, :], nsp[:, 0, :], ACT.Exp, scale=-1.0).then_inc(sp_exp, 1)
            rounded(0, 1)
            rms(("n", 1), D)
            x_rounded(0, xn, "ln1")
            memory_keys(2)
            rounded(*range(2, 10))
            for c in range(2):
                rounded(10 + 2 * c, 11 + 2 * c)
                copy(("qa", c), qa[:, 2 * c:2 * c + 2, :], pst(("qa", c))[:, :, :], scale=64 ** -0.5)
            for c in range(2):
                g = ("ka", c)
                if c == 0:
                    rounded(14, 15)
                wait_mm(g)
                act.activation(kaE[0:64, 2 * c:2 * c + 2, :], pst(g)[0:64, :, :], ACT.Copy)
                act.activation(kaO[64:128, 2 * c:2 * c + 2, :], pst(g)[64:128, :, :], ACT.Copy).then_inc(act_out, 1)
            for c in range(KH):
                g = ("gt", c)
                wait_mm(g)
                act.activation(r[:, c, :], pst(g)[:, 0, :], ACT.Sigmoid, bias=col("ba", c))
                act.activation(gi[:, c, :], pst(g)[:, 1, :], ACT.Sigmoid, bias=col("bx", c)).then_inc(act_out, 1)
            act.wait_ge(act_out, AI2["gt", KH - 1])
            act.wait_ge(sp_step, T.sp_steps)
            for c in range(KH):
                act.activation(th[:, c, :], r[:, c, :], ACT.Tanh, scale=nsp[:, 5, c:c + 1]).then_inc(decay_ready, 1)
            for c in range(KH):
                act.activation(aa[:, c, :], r[:, c, :], ACT.Exp, scale=nsp[:, 5, c:c + 1]).then_inc(decay_ready, 1)

            def exponentials(h):
                act.wait_ge(nmax_ready, h + 1)
                for i in range(TT):
                    p = sbuf[:, h % 2, SOFF[i]:SOFF[i] + (i + 1) * P]
                    act.activation(p, p, ACT.Exp, bias=nmx[:, 4 * h + i:4 * h + i + 1],
                                   accum_out=rsum[:, 4 * h + i:4 * h + i + 1]).then_inc(exp_done, 1)

            def turned(h):
                for g, js in ((("tA", h), (0, 1)), (("tB", h), (2, 3))):
                    wait_mm(g)
                    for b, j in enumerate(js):
                        last = act.activation(pT[:, j, j * P:SEQ], pst(g)[:, b, j * P:SEQ], ACT.Copy)
                    last.then_inc(act_out, 1)

            def root():
                act.wait_ge(m2_ready, 1)
                act.activation(yr, yr, ACT.Ln).then_inc(logs_ready, 1)
                act.activation(th, th, ACT.Ln, scale=-1.0, bias=ones[:, 0:1]).then_inc(logs_ready, 1)

            def root_exp():
                act.wait_ge(rnn_step, 2)
                act.activation(yr, yr, ACT.Exp, scale=0.5).then_inc(root_ready, 1)

            def gelu():
                act.wait_ge(vec_out, VI2["xg", 1])
                act.activation(xg, xg, ACT.Gelu_apprx_tanh).then_inc(gelu_ready, 1)

            exponentials(0)
            exponentials(1)
            memory_keys(3)
            act.wait_ge(decay_ready, 2 * KH)
            for h in range(AH):
                turned(h)
                if h < 3:
                    (root, root_exp, gelu)[h]()
                if h + 2 < AH:
                    exponentials(h + 2)
            act.wait_ge(rnn_step, 4)
            for k in range(KH):
                square("mixed", k, xn)
            for k in range(KH, KD):
                act.wait_ge(vec_out, VI2["at", 2 * (k - KH) + 1])
                square("mixed", k, xn)
            rms(("n", 2), DH, banks=2)
            rounded(16)
            x_rounded(1, xn, "mixed")
            rounded(17)
            for m in range(4):
                if m < 3:
                    rounded(18 + 2 * m, 19 + 2 * m)
                squares_of("ln2", "o", m)
            rms(("n", 3), D)
            rounded(24)
            x_rounded(2, xn, "ln2")
            rounded(25)
            for m in range(4):
                if m < 3:
                    rounded(26 + 2 * m, 27 + 2 * m)
                copy(("qx", m), qx[:, 2 * m:2 * m + 2, :], pst(("qx", m))[:, :, :], scale=256 ** -0.5)

            def cross_exponentials(h):
                n = 4 * (AH + h)
                act.wait_ge(nmax_ready, AH + h + 1)
                for i in range(TT):
                    last = act.activation(sbuf[:, h % 2, i * MEM:i * MEM + MEM], pflat(("sx", h))[:, i * MEM:i * MEM + MEM], ACT.Exp,
                                          bias=nmx[:, n + i:n + i + 1], accum_out=rsum[:, n + i:n + i + 1])
                last.then_inc(act_out, 1)

            cross_exponentials(0)
            cross_exponentials(1)
            rounded(32, 33)

            def ox_rounded(h):
                act.wait_ge(vec_out, VI2["ax", h])
                x_rounded(3, ox, chunks=(2 * h, 2 * h + 1))

            for h in range(XH):
                copy(("tx", h), pT[:, 0:2, :], pst(("tx", h))[:, :, :])
                if h + 2 < XH:
                    cross_exponentials(h + 2)
                if h:
                    ox_rounded(h - 1)
            ox_rounded(XH - 1)
            for m in range(4):
                if m < 3:
                    rounded(34 + 2 * m, 35 + 2 * m)
                squares_of("ln3", "xo", m)
            copy(("xt", 0), T.xtok[:, 0, :], pflat(("xt", 0)))
            rms(("n", 4), D)
            for i in range(1, TT):
                copy(("xt", i), T.xtok[:, i, :], pflat(("xt", i)))
            for i in range(TT):
                copy(("ht", i), T.htok[:, i, :], pflat(("ht", i)))
            act.wait_ge(R.route_step, ROUTE_GROUP)
            act.activation(R.ge, R.ge, ACT.Exp).then_inc(R.group_exp, 1)
            act.wait_ge(R.route_step, ROUTE_PAIR)
            act.activation(R.e2, R.m2, ACT.Exp).then_inc(R.pair_exp, 1)


G3 = ([("x", 0), ("x", 1)] + [("o", n) for n in range(4)] + [("gt",), ("up",)] + [("o", n) for n in range(4, 8)]
      + [("ht",), ("st",), ("y", 0), ("y", 1)])
BANK = {g: n % 8 for n, g in enumerate(G3)}
ACT_OWNS3 = [("x", 0), ("gt",), ("ht",), ("y", 0), ("y", 1)]
GI3 = {g: n for n, g in enumerate(G3)}
AI3 = {g: n + 1 for n, g in enumerate(ACT_OWNS3)}
VI3 = {g: n + 1 for n, g in enumerate(g for g in G3 if g not in ACT_OWNS3)}
NG3, NA3, NV3 = len(G3), len(AI3), len(VI3)


def experts(nc, dram, T, R, sem, out):
    ctx = ExitStack()
    with ctx:
        def sb(name, shape, dt=F32):
            return ctx.enter_context(nc.sbuf_tensor(name, shape, dt))

        htok, acc, ident, eps = T.htok, T.xtok, T.ident, T.eps
        weights, w_loaded = T.weights, T.w_loaded
        for e in range(2):
            weights[e].append(sb(f"w_down{e}", [P, KF * D])[:, :])
        slot, wcomb, rank, rounds, rounds_ready = R.slot, R.wcomb, R.rank, T.rounds, R.rounds_ready
        sel = sb("sel", [P, TT, 2 * CAP])
        selw = sb("selw", [P, TT, 2 * CAP])
        selT = sb("selT", [P, SEQ], F32R)
        wslot = sb("wslot", [P, 1])
        xe = sb("xe", [P, KD, 2 * CAP])
        sg = sb("sg", [P, FE])
        he = sb("he", [P, FE])
        hT = sb("heT", [P, KF, 2 * CAP])
        old = T.hT[:, :, :].rearrange("p k n -> p (k n)")
        fw, sqo, ysw = (old[:, n * D:(n + 1) * D] for n in range(3))
        ys_hi = sb("ys_hi", [P, D], F32R)
        ys_lo = sb("ys_lo", [P, D], F32R)
        ssum = sb("ssum", [P, TT])

        mm_done = sem("mm3_done")
        vec_out = sem("vec3_out")
        act_out = sem("act3_out")
        zeros_made = sem("zeros_made")
        fw_loaded = sem("fw_loaded")
        sel_made = sem("sel_made")
        sel_ready = sem("sel_ready")
        rank_moved = sem("rank_moved")
        wslot_ready = sem("wslot_ready")
        hi_ready = sem("hi_ready")
        lo_ready = sem("lo_ready")
        ss_done = sem("ss_done")
        rstd_done = sem("rstd3_done")
        out_ready = sem("out_ready")
        stored = sem("stored")

        def scatter_product(to, i, half):
            for n, part in enumerate((ys_hi, ys_lo)):
                mm = nc.tensor.matmul(to, selT[:, i * P:i * P + P], part[:, half * 512:half * 512 + 512], start=n == 0, stop=n == 1)
            mm.then_inc(mm_done, 1)

        def bank(g):
            return T.ps[BANK[g] // 2][:, BANK[g] % 2, :]

        block = ctx.enter_context(nc.Block())

        @block.sync
        def _(sp):
            def load(pair, it):
                for j, last in enumerate((("gt",), ("up",), ("y", 1))):
                    sp.wait_ge(mm_done, it * NG3 + GI3[last] + 1)
                    for e in range(2):
                        load_expert(sp, dram, T, pair, e, j)

            for e in range(2):
                load_expert(sp, dram, T, 0, e, 2)
            with sp.Fori(1, PAIRS) as pair:
                load(pair, pair)
            sp.wait_ge(rounds_ready, 1)
            n_rounds = sp.value_load(rounds[0:1, 0:1], min_val=1, max_val=ROUNDS_MAX)
            with sp.If(n_rounds > 1):
                with sp.Fori(1, n_rounds) as rnd:
                    with sp.Fori(0, PAIRS) as pair:
                        load(pair, rnd * PAIRS + pair)
            for i in range(TT):
                sp.wait_ge(out_ready, i + 1)
                sp.dma_start(out[0, i * P:i * P + P, :], acc[:, i, :]).then_inc(stored, 16)
            sp.wait_ge(stored, 16 * TT)

        @block.gpsimd
        def _(pool):
            pool.dma_start(fw[:, :], dram["fw"].partition_broadcast(P)).then_inc(fw_loaded, 16)
            for zeros in (ys_hi, ys_lo, selT):
                pool.memset(zeros[:, :].bitcast(F32), 0.0).then_inc(zeros_made, 1)

        @block.vector
        def _(dve):
            dve.sem_inc(vec_out, NV3)
            dve.wait_ge(rounds_ready, 1)
            n_rounds = dve.value_load(rounds[0:1, 0:1], min_val=1, max_val=ROUNDS_MAX)

            def select(first, count):
                for e in range(2):
                    r = rank[:, :, bass.ds(first + e, 1)].broadcast_to([P, TT, CAP])
                    last = dve.tensor_tensor(sel[:, :, e * CAP:e * CAP + CAP], slot[:, :, :], r, ALU.is_equal)
                last.then_inc(sel_made, 1)
                dve.wait_ge(sel_made, count)
                for e in range(2):
                    w = wcomb[:, :, bass.ds(first + e, 1)].broadcast_to([P, TT, CAP])
                    last = dve.tensor_tensor(selw[:, :, e * CAP:e * CAP + CAP], sel[:, :, e * CAP:e * CAP + CAP], w, ALU.mult)
                last.then_inc(sel_ready, 1)

            with dve.Fori(0, n_rounds) as rnd:
                per = PAIRS + 1
                dve.wait_ge(vec_out, rnd * (PAIRS * NV3) + NV3)
                dve.tensor_scalar(rank[:, :, :], rank[:, :, :], -float(CAP), None, ALU.add).then_inc(rank_moved, 1)
                dve.wait_ge(rank_moved, rnd + 1)
                select(0, rnd * per + 1)
                with dve.Fori(0, PAIRS) as pair:
                    it = rnd * PAIRS + pair

                    def wait_mm(g):
                        dve.wait_ge(mm_done, (it + 1) * NG3 + GI3[g] + 1)

                    def add(n):
                        half, i = n // TT, n % TT
                        wait_mm(("o", n))
                        a = acc[:, i, half * 512:half * 512 + 512]
                        dve.tensor_tensor(a, bank(("o", n)), a, ALU.add).then_inc(vec_out, 1)

                    wait_mm(("x", 1))
                    dve.tensor_copy(xe[:, 4:8, :], bank(("x", 1)).rearrange("p (k n) -> p k n", k=4)).then_inc(vec_out, 1)
                    for n in range(4):
                        add(n)
                    wait_mm(("up",))
                    dve.wait_ge(act_out, (it + 1) * NA3 + AI3["gt",])
                    dve.tensor_tensor(he[:, :], sg[:, :], bank(("up",)), ALU.mult).then_inc(vec_out, 1)
                    for n in range(4, 8):
                        add(n)
                    wait_mm(("st",))
                    dve.tensor_reduce(wslot[:, :], bank(("st",)), AX.X, ALU.add).then_inc(wslot_ready, 1)
                    dve.tensor_scalar(selT[:, :], bank(("st",)), 0.0, None, ALU.not_equal).then_inc(vec_out, 1)
                    select(pair * 2 + 2, rnd * per + pair + 2)
                    for half in range(2):
                        h = slice(half * 512, half * 512 + 512)
                        dve.wait_ge(hi_ready, 2 * it + half + 1)
                        dve.tensor_tensor(ys_lo[:, h], ysw[:, h], ys_hi[:, h].bitcast(F32), ALU.subtract).then_inc(lo_ready, 1)

            done = n_rounds * PAIRS + 1
            dve.wait_ge(fw_loaded, 16)
            for n in range(8):
                i, half = n // 2, n % 2
                a = acc[:, i, half * 512:half * 512 + 512]
                dve.wait_ge(mm_done, done * NG3 + n + 1)
                dve.tensor_tensor(a, T.ps[n // 2][:, n % 2, :], a, ALU.add).then_inc(vec_out, 1)
            for i in range(TT):
                dve.wait_ge(rstd_done, i + 1)
                dve.scalar_tensor_tensor(acc[:, i, :], acc[:, i, :], ssum[:, i:i + 1], fw[:, :], ALU.mult, ALU.mult).then_inc(out_ready, 1)

        @block.tensor
        def _(pe):
            pe.sem_inc(mm_done, NG3)
            pe.sem_inc(lo_ready, 2)
            pe.wait_ge(zeros_made, 3)
            pe.wait_ge(rounds_ready, 1)
            n_rounds = pe.value_load(rounds[0:1, 0:1], min_val=1, max_val=ROUNDS_MAX)
            with pe.Fori(0, n_rounds) as rnd, pe.Fori(0, PAIRS) as pair:
                it = rnd * PAIRS + pair

                def begin(g):
                    same = [q for q in G3 if BANK[q] == BANK[g]]
                    prev = same[same.index(g) - 1]
                    back = 1 if GI3[prev] < GI3[g] else 0
                    if prev in AI3:
                        pe.wait_ge(act_out, (it + back) * NA3 + AI3[prev])
                    else:
                        pe.wait_ge(vec_out, (it + back) * NV3 + VI3[prev])

                def weight(e, j, k):
                    pe.wait_ge(w_loaded[e][j], (it + 1) * 16)
                    return weights[e][j].rearrange("p (k n) -> p k n", k=k)

                pe.wait_ge(sel_ready, rnd * (PAIRS + 1) + pair + 1)
                for half in range(2):
                    g = ("x", half)
                    begin(g)
                    for c in range(4):
                        k = half * 4 + c
                        for i in range(TT):
                            mm = pe.matmul(bank(g)[:, c * P:c * P + P], htok[:, i, k * P:k * P + P], sel[:, i, :],
                                           start=i == 0, stop=i == TT - 1)
                    mm.then_inc(mm_done, 1)

                def scatter(n):
                    half, i = n // TT, n % TT
                    begin(("o", n))
                    scatter_product(bank(("o", n)), i, half)

                def both(g, j, lhs, k, col):
                    begin(g)
                    for c in range(k):
                        for e in range(2):
                            s = slice(e * CAP, e * CAP + CAP)
                            mm = pe.matmul(bank(g)[s, :], lhs[:, c, s], weight(e, j, k)[:, c, col:col + 512],
                                           start=c == 0, stop=c == k - 1)
                    mm.then_inc(mm_done, 1)

                pe.wait_ge(lo_ready, 2 * it + 2)
                pe.wait_ge(vec_out, it * NV3 + VI3["st",])
                for n in range(4):
                    scatter(n)
                pe.wait_ge(act_out, (it + 1) * NA3 + AI3["x", 0])
                pe.wait_ge(vec_out, (it + 1) * NV3 + VI3["x", 1])
                both(("gt",), 0, xe, KD, 0)
                both(("up",), 1, xe, KD, 0)
                for n in range(4, 8):
                    scatter(n)
                begin(("ht",))
                pe.wait_ge(vec_out, (it + 1) * NV3 + VI3["up",])
                for f in range(KF):
                    mm = pe.transpose(bank(("ht",))[:, f * P:f * P + P], he[:, f * P:f * P + P], ident[:, :])
                mm.then_inc(mm_done, 1)
                begin(("st",))
                for i in range(TT):
                    mm = pe.transpose(bank(("st",))[:, i * P:i * P + P], selw[:, i, :], ident[:, :])
                mm.then_inc(mm_done, 1)
                pe.wait_ge(act_out, (it + 1) * NA3 + AI3["ht",])
                for half in range(2):
                    both(("y", half), 2, hT, KF, half * 512)
            done = n_rounds * PAIRS + 1
            pe.wait_ge(lo_ready, 2 * done)
            pe.wait_ge(act_out, done * NA3)
            pe.wait_ge(vec_out, done * NV3)
            for n in range(8):
                scatter_product(T.ps[n // 2][:, n % 2, :], n // 2, n % 2)

        @block.scalar
        def _(act):
            act.sem_inc(act_out, NA3)
            act.wait_ge(rounds_ready, 1)
            n_rounds = act.value_load(rounds[0:1, 0:1], min_val=1, max_val=ROUNDS_MAX)
            with act.Fori(0, n_rounds) as rnd, act.Fori(0, PAIRS) as pair:
                it = rnd * PAIRS + pair

                def wait_mm(g):
                    act.wait_ge(mm_done, (it + 1) * NG3 + GI3[g] + 1)

                wait_mm(("x", 0))
                act.activation(xe[:, 0:4, :], bank(("x", 0)).rearrange("p (k n) -> p k n", k=4), ACT.Copy).then_inc(act_out, 1)
                wait_mm(("gt",))
                act.activation(sg[:, :], bank(("gt",)), ACT.Silu).then_inc(act_out, 1)
                wait_mm(("ht",))
                act.activation(hT[:, :, :], bank(("ht",)).rearrange("p (f n) -> p f n", f=KF), ACT.Copy).then_inc(act_out, 1)
                act.wait_ge(wslot_ready, it + 1)
                for half in range(2):
                    h = slice(half * 512, half * 512 + 512)
                    wait_mm(("y", half))
                    act.activation(ysw[:, h], bank(("y", half)), ACT.Copy, scale=wslot[:, 0:1]).then_inc(act_out, 1)
                    act.wait_ge(act_out, (it + 1) * NA3 + AI3["y", half])
                    act.activation(ys_hi[:, h], ysw[:, h], ACT.Copy).then_inc(hi_ready, 1)
            done = n_rounds * PAIRS + 1
            for i in range(TT):
                s = ssum[:, i:i + 1]
                act.wait_ge(vec_out, done * NV3 + 2 * i + 2)
                if i:
                    act.wait_ge(rstd_done, i)
                act.activation(sqo[:, :], acc[:, i, :], ACT.Square, accum_out=s).then_inc(ss_done, 1)
                act.wait_ge(ss_done, 2 * i + 1)
                act.activation(s, s, ACT.Ln, bias=eps[:, :], scale=1.0 / D).then_inc(ss_done, 1)
                act.wait_ge(ss_done, 2 * i + 2)
                act.activation(s, s, ACT.Exp, scale=-0.5).then_inc(rstd_done, 1)


def build(nc, dram, out):
    T = Tiles()
    with ExitStack() as ctx:
        def sb(name, shape, dt=F32):
            return ctx.enter_context(nc.sbuf_tensor(name, shape, dt))

        def sem(name):
            return ctx.enter_context(nc.semaphore(name))

        T.hT = sb("hT", [P, KD, L])
        T.rstd = sb("rstd", [P, 3, L])
        with nc.sbuf_tensor("x_lo", [P, KD, L], F32R) as T.x_lo:
            pass
        T.qn = sb("qn", [P, HEADS, L])
        T.kn = sb("kn", [P, HEADS, L])
        T.area_g = sb("area_g", [P, 2 * NT * L + 6 * DH])[:, :]
        T.area_u0 = sb("area_u0", [P, 8 * L])[:, :]
        T.area_u1 = sb("area_u1", [P, 512 + NT * 512 + 2 * (L + 32)])[:, :]
        T.weights = [[T.area_g[:, e * KD * 512:(e + 1) * KD * 512], (T.area_u0, T.area_u1)[e][:, 0:KD * 512]] for e in range(2)]
        T.w_loaded = [[sem(f"w_loaded{e}{j}") for j in range(3)] for e in range(2)]
        T.mem_in = T.area_g[:, 0:KD * MEM].rearrange("p (k n) -> p k n", k=KD)
        T.gates_place, T.memn = (t[:, :, :].rearrange("p h n -> p (h n)")[:, 0:KD * MEM].rearrange("p (k n) -> p k n", k=KD)
                          for t in (T.kn, T.qn))
        with nc.sbuf_tensor("ring_front", [P, 2, PANEL], F32), nc.sbuf_tensor("w2_split", [P, 2, 2, KD * P], F32R) as T.w2_split:
            pass
        T.ring = sb("ring", [P, RING, PANEL])
        T.ones = sb("ones", [P, P])
        T.ident = sb("ident", [P, P])
        T.eps = sb("eps", [P, 1])
        T.lw = sb("lw", [P, LW])
        T.ps = [ctx.enter_context(nc.psum_tensor(f"ps{i}", [P, 2, 512], F32)) for i in range(NPS)]
        T.logits = sb("logits", [P, TT * NL])
        T.rounds = sb("rounds", [P, 1], mybir.dt.int32)
        T.htok = T.ring[:, 0:2, :].rearrange("p a (b n) -> p (a b) n", b=2)
        T.xtok = T.ring[:, 2:4, :].rearrange("p a (b n) -> p (a b) n", b=2)
        T.setup = sem("setup")
        T.N_SETUP = 4
        T.lw_ready = sem("lw_ready")
        T.w_ready = [sem(f"w_ready{i}") for i in range(RING)]
        T.mem_loaded = sem("mem_loaded")
        T.memn_ready = sem("memn_ready")
        with nc.Block() as block:
            @block.gpsimd
            def _(pool):
                pool.memset(T.ones[:, :], 1.0).then_inc(T.setup, 1)
                pool.memset(T.eps[:, :], EPS).then_inc(T.setup, 1)
                pool.memset(T.ident[:, :], 0.0).then_inc(T.setup, 1)
                pool.wait_ge(T.setup, 3)
                pool.affine_select(out=T.ident[:, :], in_=T.ident[:, :], compare_op=ALU.not_equal, fill=1.0,
                                   base=0, pattern=[[-1, P]], channel_multiplier=1).then_inc(T.setup, 1)
        first_block(nc, dram, T, sem)
        R = Routing(T, sem)
        second_block(nc, dram, T, R, sem)
        experts(nc, dram, T, R, sem, out)


def kernel(**inputs):
    import numpy as np
    import concourse.bacc as bacc
    from concourse.bass_utils import run_bass_kernel_spmd

    a = {k: np.asarray(x) for k, x in inputs.items()}

    def rows(x):
        return x.reshape(-1, P).T

    def cols(*parts):
        return np.concatenate(parts, axis=-1)

    def diag(x):
        n = x.shape[0]
        y = np.zeros((n // 2, P, P), x.dtype)
        y[:, :64, :64], y[:, 64:, 64:] = x[0::2], x[1::2]
        return cols(*y)

    arrays = {}
    arrays["hT"] = np.concatenate([a["meta_tokens"], a["x"][0]], axis=0).T
    w = a["w_in"]
    arrays["win"] = cols(w[..., 1024:1664], w[..., 1664:1728], w[..., 0:256], w[..., 512:768],
                         w[..., 256:512], w[..., 768:1024], w[..., 1728:2240])
    w = a["w_uq"].reshape(LAYERS, QR, HEADS, P + ROPE)
    arrays["wuq"] = cols(w[..., :P].reshape(LAYERS, QR, -1), w[..., P:P + 32].reshape(LAYERS, QR, -1),
                         w[..., P + 32:].reshape(LAYERS, QR, -1))
    w = a["w_ukv"].reshape(LAYERS, KVR, HEADS, 2 * P)
    arrays["wukv"] = cols(w[..., :P].reshape(LAYERS, KVR, -1), w[..., P:].reshape(LAYERS, KVR, -1))
    arrays["wout"] = a["w_out"]
    small = [cols(rows(a["norm_w"][l]), rows(a["pool_scale"][l]), rows(a["q_norm_w"][l]), rows(a["kv_norm_w"][l]),
                  diag(a["fourier_w"][l]), diag(a["pool_w"][l])) for l in range(LAYERS)]
    last = np.zeros_like(small[0])
    last[:, 0:KD] = rows(a["final_norm_w"])
    last[:, LW_VEC:LW_WR] = cols(rows(a["ln1_w_2"]), *(rows(a["conv_w_2"][0, j]) for j in range(CONV)), rows(a["conv_b_2"]), rows(a["rnn_ba_2"]),
                         rows(a["rnn_bx_2"]), rows(a["rnn_lambda_2"]), rows(a["gn_rnn_w_2"]), rows(a["gn_att_w_2"]), rows(a["ln2_w_2"]),
                         rows(a["mem_norm_w_2"]), rows(a["ln3_w_2"]))
    last[:, LW_WR:LW_RB] = cols(a["router_group_w_2"][0], *a["router_expert_w_2"][0]).reshape(KD, P, NL).transpose(1, 0, 2).reshape(P, -1)
    last[:, LW_RB:LW_RB + TT * NL] = np.tile(cols(a["router_group_b_2"][0], *a["router_expert_b_2"][0]), TT)
    arrays["lw"] = np.stack(small + [last])

    arrays["memT"] = a["mem_2"][0].T
    for name, source in (("xk", "xk_w_2"), ("xv", "xv_w_2"), ("xq", "xq_w_2"), ("xo", "xo_w_2"), ("win2", "w_in_2"), ("wout2", "w_out_2")):
        arrays[name] = a[source][0]
    arrays["wab"] = cols(diag(a["rnn_wa_2"][0]), diag(a["rnn_wx_2"][0])).reshape(P, 2 * KH, P)
    distance = np.arange(P)[:, None] + (SEQ - P) - np.arange(SEQ)[None, :]
    arrays["bias"] = a["rel_bias_2"][0][:, np.clip(distance, -P, P) + P]

    arrays["eg"], arrays["eu"], arrays["ed"] = a["expert_gate_w_2"][0], a["expert_up_w_2"][0], a["expert_down_w_2"][0]
    arrays["fw"] = a["final_norm_w_2"]

    n = np.arange(L)
    angle = 2 * np.pi * ((n[:, None] * n[None, :]) % L) / L
    tables = np.zeros((4, NT * P, LH))
    for half in range(2):
        tables[2 * half, :L] = np.cos(angle)[:, half * LH:half * LH + LH]
        tables[2 * half + 1, :L] = np.sin(angle)[:, half * LH:half * LH + LH]
    arrays["dft"] = tables.astype(np.float32)
    c = np.arange(64)
    angle = 2 * np.pi * ((c[:, None] * c[None, :]) % 64) / 64
    both = np.zeros((P, 2, P))
    for b in range(2):
        s = slice(64 * b, 64 * b + 64)
        both[s, 0, s] = np.cos(angle) / math.sqrt(L * 64)
        both[s, 1, s] = -np.sin(angle) / math.sqrt(L * 64)
    arrays["cdsd"] = both.astype(np.float32)
    inv = (1.0 / (np.float32(10000.0) ** (np.arange(0, ROPE, 2, dtype=np.float32) / np.float32(ROPE)))).astype(np.float32)
    angle = n.astype(np.float32)[:, None] * inv[None, :]
    arrays["rope"] = np.stack([np.tile(np.cos(angle).T, (4, 1)), np.tile(np.sin(angle).T, (4, 1))], axis=1).astype(np.float32)
    count = np.zeros((P, 2, L))
    for g, win in enumerate((2, 4, 8, 16)):
        have = np.clip(n + win // 2, 0, L) - np.clip(n - win // 2, 0, L)
        count[64 * (g % 2):64 * (g % 2) + 64, g // 2] = 1.0 / have
    arrays["cnt"] = count.astype(np.float32)

    nc = bacc.Bacc("TRN2", target_bir_lowering=False, num_devices=1)
    dram, fed = {}, {}
    for name, x in arrays.items():
        fed[f"in_{name}"] = np.ascontiguousarray(x)
        dram[name] = nc.dram_tensor(f"in_{name}", x.shape, mybir.dt.from_np(x.dtype), kind="ExternalInput").ap()
    out = nc.dram_tensor("out_0", (1, SEQ, D), F32, kind="ExternalOutput").ap()
    build(nc, dram, out)
    r = run_bass_kernel_spmd(nc, [fed], core_ids=[0])
    return r.results[0]["out_0"]
```
